# Optimizing a Trainium2 kernel written in Bass

```python
import math
import jax, jax.numpy as jnp
from jax import lax
import numpy as np

D_MODEL = 1024
BATCH = 1
SEQ = 512
DEPTH = 1

D_MIX = D_MODEL
GLA_HEADS = 4
GLA_DV = D_MIX // 2 // GLA_HEADS
GLA_DK = GLA_DV // 2
GLA_LOWRANK = 16
GLA_TAU = 16.0
GLA_CHUNK = 64
SWA_HEADS = 8
SWA_KV_HEADS = 2
SWA_HD = (D_MIX - GLA_HEADS * GLA_DV) // SWA_HEADS
SWA_WINDOW = 128
D_FF = 2816
CONV_K = 3
EPS = 1e-6

GLA_Q = GLA_HEADS * GLA_DK
GLA_K = GLA_HEADS * GLA_DK
GLA_V = GLA_HEADS * GLA_DV
GLA_R = GLA_HEADS * GLA_DV
SWA_Q = SWA_HEADS * SWA_HD
SWA_K = SWA_KV_HEADS * SWA_HD
SWA_V = SWA_KV_HEADS * SWA_HD
SPLITS = (GLA_Q, GLA_K, GLA_V, GLA_R, GLA_LOWRANK, SWA_Q, SWA_K, SWA_V)
P_IN = sum(SPLITS)


def alibi_slopes(n_heads):
    return np.array([2.0 ** (-8.0 * (h + 1) / n_heads) for h in range(n_heads)], dtype=np.float32)

def rms_norm(x, g):
    xf = x.astype(jnp.float32)
    y = xf * lax.rsqrt(jnp.mean(xf * xf, axis=-1, keepdims=True) + EPS)
    return (y * g.astype(jnp.float32)).astype(x.dtype)

def split_cols(z, sizes):
    idx = np.cumsum(sizes)[:-1].tolist()
    return jnp.split(z, idx, axis=-1)

def gla_chunked(q, k, v, log_a):
    B, L, H, dk = q.shape
    dv = v.shape[-1]
    C = GLA_CHUNK
    n = L // C

    def chunk(t):
        return t.astype(jnp.float32).reshape(B, n, C, H, t.shape[-1]).transpose(0, 3, 1, 2, 4)

    q, k, v, log_a = chunk(q), chunk(k), chunk(v), chunk(log_a)
    b = jnp.cumsum(log_a, axis=-2)
    b_last = b[..., -1:, :]
    qe = q * jnp.exp(b)
    ke = k * jnp.exp(-b)
    causal = jnp.tril(jnp.ones((C, C), dtype=bool))
    A = jnp.einsum('bhncd,bhnsd->bhncs', qe, ke)
    A = jnp.where(causal, A, 0.0)
    o_intra = jnp.einsum('bhncs,bhnsv->bhncv', A, v)
    kd = k * jnp.exp(b_last - b)
    chunk_state = jnp.einsum('bhncd,bhncv->bhndv', kd, v)
    decay = jnp.exp(b_last[..., 0, :])

    def step(S, inp):
        dec, cs = inp
        return S * dec[..., None] + cs, S

    S0 = jnp.zeros((B, H, dk, dv), jnp.float32)
    _, S_prev = lax.scan(step, S0, (jnp.moveaxis(decay, 2, 0), jnp.moveaxis(chunk_state, 2, 0)))
    S_prev = jnp.moveaxis(S_prev, 0, 2)
    o_inter = jnp.einsum('bhncd,bhndv->bhncv', qe, S_prev)
    o = o_intra + o_inter
    return o.transpose(0, 2, 3, 1, 4).reshape(B, L, H, dv)

def swa_sink_attention(q, k, v, sinks):
    B, L, Hq, hd = q.shape
    Hkv = k.shape[2]
    G = Hq // Hkv
    W = SWA_WINDOW
    nb = L // W
    qb = q.reshape(B, nb, W, Hkv, G, hd)
    kb = k.reshape(B, nb, W, Hkv, hd)
    vb = v.reshape(B, nb, W, Hkv, hd)
    pad = ((0, 0), (1, 0), (0, 0), (0, 0), (0, 0))
    kk = jnp.concatenate([jnp.pad(kb, pad)[:, :-1], kb], axis=2)
    vv = jnp.concatenate([jnp.pad(vb, pad)[:, :-1], vb], axis=2)
    s = jnp.einsum('bnqkgd,bnskd->bnkgqs', qb, kk,
                   preferred_element_type=jnp.float32) * (1.0 / math.sqrt(hd))
    i = jnp.arange(W)[:, None]
    j = jnp.arange(2 * W)[None, :]
    dist = (W + i - j).astype(jnp.float32)
    key_abs = (jnp.arange(nb)[:, None, None] - 1) * W + j[None]
    mask = (dist >= 0) & (dist < W) & (key_abs >= 0)
    slopes = jnp.asarray(alibi_slopes(Hq)).reshape(Hkv, G)
    s = s - slopes[:, :, None, None] * dist
    s = jnp.where(mask[None, :, None, None], s, -jnp.inf)
    sink = sinks.astype(jnp.float32).reshape(Hkv, G)[None, None, :, :, None, None]
    m = jnp.maximum(jnp.max(s, axis=-1, keepdims=True), sink)
    p = jnp.exp(s - m)
    denom = jnp.sum(p, axis=-1, keepdims=True) + jnp.exp(sink - m)
    p = p / denom
    o = jnp.einsum('bnkgqs,bnskd->bnqkgd', p, vv.astype(jnp.float32))
    return o.reshape(B, L, Hq * hd)

def causal_dwconv(u, w, b):
    K = w.shape[0]
    L = u.shape[1]
    up = jnp.pad(u, ((0, 0), (K - 1, 0), (0, 0)))
    out = up[:, 0:L] * w[0]
    for j in range(1, K):
        out = out + up[:, j:j + L] * w[j]
    return out + b

def hybrid_layer(x, mix_norm, w_in, w_alpha2, b_alpha, gla_norm, q_norm, k_norm, sinks,
                 w_out, ffn_norm, w_up, conv_w, conv_b, w_down):
    B, L, _ = x.shape
    dt = x.dtype
    h = rms_norm(x, mix_norm)
    z = h @ w_in
    gq, gk, gv, gr, glr, sq, sk, sv = split_cols(z, SPLITS)

    log_a = jax.nn.log_sigmoid((glr @ w_alpha2 + b_alpha).astype(jnp.float32)) / GLA_TAU
    gq = gq.reshape(B, L, GLA_HEADS, GLA_DK) * (GLA_DK ** -0.5)
    gk = gk.reshape(B, L, GLA_HEADS, GLA_DK)
    gv = gv.reshape(B, L, GLA_HEADS, GLA_DV)
    o_gla = gla_chunked(gq, gk, gv, log_a.reshape(B, L, GLA_HEADS, GLA_DK))
    o_gla = rms_norm(o_gla, gla_norm).reshape(B, L, GLA_V)
    o_gla = (o_gla * jax.nn.silu(gr.astype(jnp.float32))).astype(dt)

    sq = rms_norm(sq.reshape(B, L, SWA_HEADS, SWA_HD), q_norm)
    sk = rms_norm(sk.reshape(B, L, SWA_KV_HEADS, SWA_HD), k_norm)
    sv = sv.reshape(B, L, SWA_KV_HEADS, SWA_HD)
    o_swa = swa_sink_attention(sq, sk, sv, sinks).astype(dt)

    x = x + jnp.concatenate([o_gla, o_swa], axis=-1) @ w_out

    h2 = rms_norm(x, ffn_norm)
    u = causal_dwconv(h2 @ w_up, conv_w, conv_b)
    a, bval = jnp.split(u, 2, axis=-1)
    return x + (jax.nn.silu(a) * bval) @ w_down

def first_inputs(seed: int = 0) -> dict:
    key = jax.random.key(seed)
    ks = jax.random.split(key, 16)
    f = jnp.float32

    def nrm(k, shape, scale):
        return jax.random.normal(k, shape, f) * scale

    return {
        "x": nrm(ks[0], (BATCH, SEQ, D_MODEL), 1.0),
        "mix_norm": 1.0 + nrm(ks[1], (DEPTH, D_MODEL), 0.02),
        "w_in": nrm(ks[2], (DEPTH, D_MODEL, P_IN), D_MODEL ** -0.5),
        "w_alpha2": nrm(ks[3], (DEPTH, GLA_LOWRANK, GLA_Q), GLA_LOWRANK ** -0.5),
        "b_alpha": nrm(ks[4], (DEPTH, GLA_Q), 0.1),
        "gla_norm": 1.0 + nrm(ks[5], (DEPTH, GLA_DV), 0.02),
        "q_norm": 1.0 + nrm(ks[6], (DEPTH, SWA_HD), 0.02),
        "k_norm": 1.0 + nrm(ks[7], (DEPTH, SWA_HD), 0.02),
        "sinks": nrm(ks[8], (DEPTH, SWA_HEADS), 0.5),
        "w_out": nrm(ks[9], (DEPTH, D_MIX, D_MODEL), (2.0 * D_MIX) ** -0.5),
        "ffn_norm": 1.0 + nrm(ks[10], (DEPTH, D_MODEL), 0.02),
        "w_up": nrm(ks[11], (DEPTH, D_MODEL, 2 * D_FF), D_MODEL ** -0.5),
        "conv_w": nrm(ks[12], (DEPTH, CONV_K, 2 * D_FF), CONV_K ** -0.5),
        "conv_b": nrm(ks[13], (DEPTH, 2 * D_FF), 0.02),
        "w_down": nrm(ks[14], (DEPTH, D_FF, D_MODEL), (2.0 * D_FF) ** -0.5),
    }

def first_block(x, mix_norm, w_in, w_alpha2, b_alpha, gla_norm, q_norm, k_norm, sinks,
              w_out, ffn_norm, w_up, conv_w, conv_b, w_down):
    for l in range(DEPTH):
        x = hybrid_layer(x, mix_norm[l], w_in[l], w_alpha2[l], b_alpha[l], gla_norm[l],
                         q_norm[l], k_norm[l], sinks[l], w_out[l], ffn_norm[l], w_up[l],
                         conv_w[l], conv_b[l], w_down[l])
    return x


DEPTH_2 = 2

HEAD_DIM = 64
FOX_HEADS = 8
NSA_HEADS = 8
NSA_KV_GROUPS = 2
NSA_GROUP_SIZE = NSA_HEADS // NSA_KV_GROUPS
CMP_BLOCK = 32
CMP_STRIDE = 16
SLC_BLOCK = 64
N_SELECT = 16
WINDOW = 512
Q_BLOCK = 128
POOL_WINDOWS = (2, 4, 8, 16)
POOL_GROUP = D_MODEL // len(POOL_WINDOWS)
FFN_HIDDEN = -(-8 * D_MODEL // (3 * 256)) * 256
RMS_EPS = 1e-6
NEG_INF = -1e30
BIG = 1e30
N_EVEN = (DEPTH_2 + 1) // 2
N_ODD = DEPTH_2 // 2
MIX_WIDTH = (FOX_HEADS + NSA_HEADS) * HEAD_DIM
KV_DIM = NSA_KV_GROUPS * HEAD_DIM
IN_SIZES = (FOX_HEADS * HEAD_DIM, FOX_HEADS * HEAD_DIM, FOX_HEADS * HEAD_DIM, FOX_HEADS,
            NSA_HEADS * HEAD_DIM, KV_DIM, KV_DIM, KV_DIM, KV_DIM, KV_DIM, KV_DIM, 3 * NSA_HEADS)
IN_COLS = sum(IN_SIZES)


def rmsnorm(x, g):
    xf = x.astype(jnp.float32)
    y = xf * lax.rsqrt(jnp.mean(xf * xf, axis=-1, keepdims=True) + RMS_EPS)
    return (y * g.astype(jnp.float32)).astype(x.dtype)

def masked_softmax(s, mask):
    s = jnp.where(mask, s, NEG_INF)
    m = jnp.max(s, axis=-1, keepdims=True)
    e = jnp.where(mask, jnp.exp(s - m), 0.0)
    return e / jnp.maximum(jnp.sum(e, axis=-1, keepdims=True), 1e-30)

def alibi_slopes_2(n):
    return jnp.asarray(2.0 ** (-8.0 * (np.arange(n, dtype=np.float32) + 1.0) / n), dtype=jnp.float32)

def fox_attention(q, k, v, log_f):
    B, S, H, dh = q.shape
    c = jnp.transpose(jnp.cumsum(log_f, axis=1), (0, 2, 1))
    kpos = jnp.arange(S)
    scale = dh ** -0.5

    def block(qb):
        start = qb * Q_BLOCK
        t = start + jnp.arange(Q_BLOCK)
        qi = lax.dynamic_slice_in_dim(q, start, Q_BLOCK, axis=1)
        ci = lax.dynamic_slice_in_dim(c, start, Q_BLOCK, axis=2)
        s = jnp.einsum('bqhd,bkhd->bhqk', qi, k).astype(jnp.float32) * scale
        s = s + ci[..., None] - c[:, :, None, :]
        mask = kpos[None, :] <= t[:, None]
        p = masked_softmax(s, mask)
        return jnp.einsum('bhqk,bkhd->bqhd', p.astype(v.dtype), v)

    out = lax.map(block, jnp.arange(S // Q_BLOCK))
    return jnp.transpose(out, (1, 0, 2, 3, 4)).reshape(B, S, H * dh)

def nsa_compress(tok, pe, w1, w2):
    B, S, G, dh = tok.shape
    r = CMP_BLOCK // CMP_STRIDE
    n_chunks = S // CMP_STRIDE
    n_c = n_chunks - r + 1
    chunks = tok.reshape(B, n_chunks, CMP_STRIDE, G, dh)
    blocks = jnp.concatenate([chunks[:, j:j + n_c] for j in range(r)], axis=2)
    blocks = blocks + pe[None, None, :, None, :]
    flat = jnp.transpose(blocks, (0, 1, 3, 2, 4)).reshape(B, n_c, G, CMP_BLOCK * dh)
    return jax.nn.gelu(flat @ w1) @ w2

def nsa_attention(q, k_c, v_c, k_s, v_s, k_w, v_w, gates, pe, w1, w2):
    B, S, H, dh = q.shape
    G = k_c.shape[2]
    R = H // G
    scale = dh ** -0.5
    slopes = alibi_slopes_2(H).reshape(G, R)
    dt = q.dtype
    r = CMP_BLOCK // CMP_STRIDE
    ratio = SLC_BLOCK // CMP_STRIDE
    n_s = S // SLC_BLOCK
    n_sel = min(N_SELECT, n_s)

    kc = nsa_compress(k_c, pe[0], w1[0], w2[0])
    vc = nsa_compress(v_c, pe[1], w1[1], w2[1])
    n_c = kc.shape[1]
    cmp_end = jnp.arange(n_c) * CMP_STRIDE + CMP_BLOCK - 1

    q_g = q.reshape(B, S, G, R, dh)
    k_blocks = jnp.transpose(k_s.reshape(B, n_s, SLC_BLOCK, G, dh), (0, 3, 1, 2, 4)).reshape(B, G, n_s, SLC_BLOCK * dh)
    v_blocks = jnp.transpose(v_s.reshape(B, n_s, SLC_BLOCK, G, dh), (0, 3, 1, 2, 4)).reshape(B, G, n_s, SLC_BLOCK * dh)
    k_w_pad = jnp.pad(k_w, ((0, 0), (WINDOW, 0), (0, 0), (0, 0)))
    v_w_pad = jnp.pad(v_w, ((0, 0), (WINDOW, 0), (0, 0), (0, 0)))
    blk = jnp.arange(n_s)

    def block(qb):
        start = qb * Q_BLOCK
        t = start + jnp.arange(Q_BLOCK)
        tf = t.astype(jnp.float32)
        qi = lax.dynamic_slice_in_dim(q_g, start, Q_BLOCK, axis=1)
        gi = lax.dynamic_slice_in_dim(gates, start, Q_BLOCK, axis=1)

        d_c = tf[:, None] - cmp_end[None, :].astype(jnp.float32)
        s_c = jnp.einsum('bqgrd,bngd->bgrqn', qi, kc).astype(jnp.float32) * scale
        s_c = s_c - slopes[None, :, :, None, None] * d_c
        p_c = masked_softmax(s_c, d_c >= 0)
        o_c = jnp.einsum('bgrqn,bngd->bqgrd', p_c.astype(dt), vc)

        imp = jnp.sum(p_c, axis=2)
        imp = jnp.pad(imp, ((0, 0), (0, 0), (0, 0), (r - 1, ratio * n_s + r - 1 - n_c - (r - 1))))
        p_slc = imp[..., 0:ratio * n_s:ratio]
        for o in range(1, ratio + r - 1):
            p_slc = p_slc + imp[..., o:o + ratio * n_s:ratio]
        cur = t // SLC_BLOCK
        forced = (blk[None, :] == 0) | (blk[None, :] == cur[:, None]) | (blk[None, :] == cur[:, None] - 1)
        future = blk[None, :] > cur[:, None]
        p_slc = jnp.where(forced, BIG, jnp.where(future, NEG_INF, p_slc))
        _, idx = lax.top_k(p_slc, n_sel)

        flat_idx = idx.reshape(B, G, Q_BLOCK * n_sel)[..., None]
        kg = jnp.take_along_axis(k_blocks, flat_idx, axis=2).reshape(B, G, Q_BLOCK, n_sel * SLC_BLOCK, dh)
        vg = jnp.take_along_axis(v_blocks, flat_idx, axis=2).reshape(B, G, Q_BLOCK, n_sel * SLC_BLOCK, dh)
        kpos = (idx[..., None] * SLC_BLOCK + jnp.arange(SLC_BLOCK)).reshape(B, G, Q_BLOCK, n_sel * SLC_BLOCK)
        d_s = (t[None, None, :, None] - kpos).astype(jnp.float32)
        s_s = jnp.einsum('bqgrd,bgqkd->bgrqk', qi, kg).astype(jnp.float32) * scale
        s_s = s_s - slopes[None, :, :, None, None] * d_s[:, :, None]
        p_s = masked_softmax(s_s, (d_s >= 0)[:, :, None])
        o_s = jnp.einsum('bgrqk,bgqkd->bqgrd', p_s.astype(dt), vg)

        kw = lax.dynamic_slice_in_dim(k_w_pad, start, WINDOW + Q_BLOCK, axis=1)
        vw = lax.dynamic_slice_in_dim(v_w_pad, start, WINDOW + Q_BLOCK, axis=1)
        wpos = start - WINDOW + jnp.arange(WINDOW + Q_BLOCK)
        d_w = t[:, None] - wpos[None, :]
        m_w = (d_w >= 0) & (d_w < WINDOW) & (wpos[None, :] >= 0)
        s_w = jnp.einsum('bqgrd,bkgd->bgrqk', qi, kw).astype(jnp.float32) * scale
        s_w = s_w - slopes[None, :, :, None, None] * d_w.astype(jnp.float32)
        p_w = masked_softmax(s_w, m_w)
        o_w = jnp.einsum('bgrqk,bkgd->bqgrd', p_w.astype(dt), vw)

        return gi[..., 0:1] * o_c + gi[..., 1:2] * o_s + gi[..., 2:3] * o_w

    out = lax.map(block, jnp.arange(S // Q_BLOCK))
    return jnp.transpose(out, (1, 0, 2, 3, 4, 5)).reshape(B, S, H * dh)

def mixer_fox_nsa(h, w_in, b_f, cmp_pe, cmp_w1, cmp_w2, w_out):
    B, S, _ = h.shape
    proj = h @ w_in
    offs = [0]
    for n in IN_SIZES:
        offs.append(offs[-1] + n)
    fq, fk, fv, ff, nq, kc, vc, ks, vs, kw, vw, ng = [proj[..., offs[i]:offs[i + 1]] for i in range(len(IN_SIZES))]
    hd = (B, S, FOX_HEADS, HEAD_DIM)
    log_f = jax.nn.log_sigmoid((ff + b_f).astype(jnp.float32))
    o_fox = fox_attention(fq.reshape(hd), fk.reshape(hd), fv.reshape(hd), log_f)
    kvd = (B, S, NSA_KV_GROUPS, HEAD_DIM)
    gates = jax.nn.sigmoid(ng.astype(jnp.float32)).astype(h.dtype).reshape(B, S, NSA_KV_GROUPS, NSA_GROUP_SIZE, 3)
    o_nsa = nsa_attention(nq.reshape(B, S, NSA_HEADS, HEAD_DIM), kc.reshape(kvd), vc.reshape(kvd),
                          ks.reshape(kvd), vs.reshape(kvd), kw.reshape(kvd), vw.reshape(kvd),
                          gates, cmp_pe, cmp_w1, cmp_w2)
    return jnp.concatenate([o_fox, o_nsa], axis=-1) @ w_out

def mixer_pool(h, w_groups, scale):
    B, S, D = h.shape
    hf = h.astype(jnp.float32)
    c = jnp.cumsum(hf, axis=1)
    count = jnp.arange(1, S + 1, dtype=jnp.float32)
    outs = []
    for gi, w in enumerate(POOL_WINDOWS):
        sl = slice(gi * POOL_GROUP, (gi + 1) * POOL_GROUP)
        cg = c[..., sl]
        lag = jnp.pad(cg, ((0, 0), (w, 0), (0, 0)))[:, :S]
        mean = (cg - lag) / jnp.minimum(count, float(w))[None, :, None]
        outs.append(mean - hf[..., sl])
    pooled = jnp.stack(outs, axis=2).astype(h.dtype)
    y = jnp.einsum('bsgc,gcd->bsgd', pooled, w_groups).reshape(B, S, D)
    return y * scale

def swiglu(h, w_gate, w_up, w_down):
    return (jax.nn.silu(h @ w_gate) * (h @ w_up)) @ w_down

def second_inputs(seed: int = 0) -> dict:
    key = jax.random.key(seed)
    ks = jax.random.split(key, 13)
    f32 = jnp.float32
    dh = HEAD_DIM
    x = jax.random.normal(ks[0], (BATCH, SEQ, D_MODEL), f32)
    norm_g = 1.0 + 0.05 * jax.random.normal(ks[1], (DEPTH_2, 4, D_MODEL), f32)
    attn_w_in = jax.random.normal(ks[2], (N_EVEN, D_MODEL, IN_COLS), f32) * D_MODEL ** -0.5
    fox_b_f = jax.random.uniform(ks[3], (N_EVEN, FOX_HEADS), f32, 1.0, 4.0)
    nsa_cmp_pe = 0.1 * jax.random.normal(ks[4], (N_EVEN, 2, CMP_BLOCK, dh), f32)
    nsa_cmp_w1 = jax.random.normal(ks[5], (N_EVEN, 2, CMP_BLOCK * dh, dh), f32) * (CMP_BLOCK * dh) ** -0.5
    nsa_cmp_w2 = jax.random.normal(ks[6], (N_EVEN, 2, dh, dh), f32) * dh ** -0.5
    attn_w_out = jax.random.normal(ks[7], (N_EVEN, MIX_WIDTH, D_MODEL), f32) * MIX_WIDTH ** -0.5
    pool_w = jax.random.normal(ks[8], (N_ODD, len(POOL_WINDOWS), POOL_GROUP, POOL_GROUP), f32) * POOL_GROUP ** -0.5
    pool_scale = 1.0 + 0.1 * jax.random.normal(ks[9], (N_ODD, D_MODEL), f32)
    ffn_w_gate = jax.random.normal(ks[10], (DEPTH_2, D_MODEL, FFN_HIDDEN), f32) * D_MODEL ** -0.5
    ffn_w_up = jax.random.normal(ks[11], (DEPTH_2, D_MODEL, FFN_HIDDEN), f32) * D_MODEL ** -0.5
    ffn_w_down = jax.random.normal(ks[12], (DEPTH_2, FFN_HIDDEN, D_MODEL), f32) * FFN_HIDDEN ** -0.5
    return {"x": x, "norm_g": norm_g, "attn_w_in": attn_w_in, "fox_b_f": fox_b_f,
            "nsa_cmp_pe": nsa_cmp_pe, "nsa_cmp_w1": nsa_cmp_w1, "nsa_cmp_w2": nsa_cmp_w2,
            "attn_w_out": attn_w_out, "pool_w": pool_w, "pool_scale": pool_scale,
            "ffn_w_gate": ffn_w_gate, "ffn_w_up": ffn_w_up, "ffn_w_down": ffn_w_down}

def second_block(x, norm_g, attn_w_in, fox_b_f, nsa_cmp_pe, nsa_cmp_w1, nsa_cmp_w2, attn_w_out,
              pool_w, pool_scale, ffn_w_gate, ffn_w_up, ffn_w_down):
    h = x
    for layer in range(DEPTH_2):
        g = norm_g[layer]
        i = layer // 2
        u = rmsnorm(h, g[0])
        if layer % 2 == 0:
            m = mixer_fox_nsa(u, attn_w_in[i], fox_b_f[i], nsa_cmp_pe[i], nsa_cmp_w1[i], nsa_cmp_w2[i], attn_w_out[i])
        else:
            m = mixer_pool(u, pool_w[i], pool_scale[i])
        h = h + rmsnorm(m, g[1])
        u = rmsnorm(h, g[2])
        h = h + rmsnorm(swiglu(u, ffn_w_gate[layer], ffn_w_up[layer], ffn_w_down[layer]), g[3])
    return h


def setup_inputs(seed=0):
    out = dict(first_inputs(seed))
    for name, value in second_inputs(seed + 1).items():
        if name != "x":
            out[name + "_2"] = value
    return out


def reference(
    x, mix_norm, w_in, w_alpha2, b_alpha, gla_norm, q_norm, k_norm, sinks, w_out, ffn_norm,
    w_up, conv_w, conv_b, w_down, norm_g_2, attn_w_in_2, fox_b_f_2, nsa_cmp_pe_2, nsa_cmp_w1_2,
    nsa_cmp_w2_2, attn_w_out_2, pool_w_2, pool_scale_2, ffn_w_gate_2, ffn_w_up_2, ffn_w_down_2,
):
    x = first_block(
        x, mix_norm, w_in, w_alpha2, b_alpha, gla_norm, q_norm, k_norm, sinks, w_out, ffn_norm,
        w_up, conv_w, conv_b, w_down,
    )
    return second_block(
        x, norm_g_2, attn_w_in_2, fox_b_f_2, nsa_cmp_pe_2, nsa_cmp_w1_2, nsa_cmp_w2_2,
        attn_w_out_2, pool_w_2, pool_scale_2, ffn_w_gate_2, ffn_w_up_2, ffn_w_down_2,
    )


_drawn_inputs = setup_inputs


def setup_inputs(seed=0):
    import zlib

    import numpy as np

    out = dict(_drawn_inputs(seed))
    spreads = {}
    factors = {'b_alpha': 2.935,
     'gla_norm': 5.276,
     'q_norm': 8.0,
     'k_norm': 8.0,
     'sinks': 33.816,
     'ffn_norm': 3.578,
     'conv_b': 3.412,
     'nsa_cmp_pe_2': 6.157,
     'pool_scale_2': 3.695}
    for name, (base, spread) in spreads.items():
        noise = np.random.default_rng([zlib.crc32(name.encode()), seed]).standard_normal(out[name].shape)
        drawn = base * np.exp(spread * noise) if base else spread * noise
        out[name] = __import__('jax').numpy.asarray(drawn.astype(out[name].dtype))
    for name, factor in factors.items():
        out[name] = (out[name] * factor).astype(out[name].dtype)
    return out
```

```python
import numpy as np
import concourse.bass as bass
from concourse import mybir
from contextlib import ExitStack


P = 128
S = 512
D = 1024
KD = D // P
FF = 2816
KF = FF // P
KH = KF // 2
EPS = 1e-6
HD = 64
CHUNK = 64
NCH = S // CHUNK
NB = S // P
NCMP = 31
BIG = 1e33
NHEADS = 8
SLOPE = [2.0 ** -(h + 1) for h in range(NHEADS)]
RAW, SPL = 4, 2

PHASES = [("in_a", 19, 8), ("out_a", 8, 8), ("up_a", 44, 8), ("down_a", 16, 11),
          ("in_b", 23, 8), ("out_b", 8, 8), ("up_b0", 44, 8), ("down_b0", 16, 11),
          ("pool", 2, 8), ("up_b1", 44, 8), ("down_b1", 16, 11)]
FIRST, COUNT, BLOCKS, ORDER = {}, {}, {}, [p[0] for p in PHASES]
_n = 0
for _name, _c, _b in PHASES:
    FIRST[_name], COUNT[_name], BLOCKS[_name] = _n, _c, _b
    _n += _c

FLOW = [("norm", 0), ("gemm", "in_a"), ("mix_a", 0), ("gemm", "out_a"), ("norm", 1), ("gemm", "up_a"),
        ("gemm", "down_a"), ("norm", 2), ("gemm", "in_b"), ("mix_b", 0), ("gemm", "out_b"), ("post", 3),
        ("norm", 4), ("gemm", "up_b0"), ("gemm", "down_b0"), ("post", 5), ("norm", 6), ("pooling", 0),
        ("gemm", "pool"), ("post", 7), ("norm", 8), ("gemm", "up_b1"), ("gemm", "down_b1"), ("post", 9)]
GAIN = {0: "mix_norm", 1: "ffn_norm", 2: "g00", 3: "g01", 4: "g02", 5: "g03", 6: "g10", 7: "g11",
        8: "g12", 9: "g13"}
STREAMED = {1: "out_a", 2: "down_a", 3: "out_b", 5: "down_b0", 7: "pool", 9: "down_b1"}
BOUNDARY = [0, 4, 6, 8]
APPLIED = [0, 1, 2, 4, 8]
POSTS = [3, 5, 7, 9]
XMODE = ("out_a", "down_a")

FLOW = [("norm", 0), ("gemm", "in_a"), ("mix_a", 0), ("gemm", "out_a"), ("norm", 1), ("gemm", "up_a"),
        ("gemm", "down_a"), ("norm", 2), ("gemm", "in_b"), ("mix_b", 0), ("gemm", "out_b"), ("post", 3),
        ("norm", 4), ("gemm", "up_b0"), ("gemm", "down_b0"), ("post", 5), ("norm", 6), ("pooling", 0),
        ("gemm", "pool"), ("post", 7), ("norm", 8), ("gemm", "up_b1"), ("gemm", "down_b1"), ("post", 9)]
GAIN = {0: "mix_norm", 1: "ffn_norm", 2: "g00", 3: "g01", 4: "g02", 5: "g03", 6: "g10", 7: "g11",
        8: "g12", 9: "g13"}
STREAMED = {1: "out_a", 2: "down_a", 3: "out_b", 5: "down_b0", 7: "pool", 9: "down_b1"}
BOUNDARY = [0, 4, 6, 8]
APPLIED = [0, 1, 2, 4, 8]
POSTS = [3, 5, 7, 9]
XMODE = ("out_a", "down_a")

FLOW = [("norm", 0), ("gemm", "in_a"), ("mix_a", 0), ("gemm", "out_a"), ("norm", 1), ("gemm", "up_a"),
        ("gemm", "down_a"), ("norm", 2), ("gemm", "in_b"), ("mix_b", 0), ("gemm", "out_b"), ("post", 3),
        ("norm", 4), ("gemm", "up_b0"), ("gemm", "down_b0"), ("post", 5), ("norm", 6), ("pooling", 0),
        ("gemm", "pool"), ("post", 7), ("norm", 8), ("gemm", "up_b1"), ("gemm", "down_b1"), ("post", 9)]
GAIN = {0: "mix_norm", 1: "ffn_norm", 2: "g00", 3: "g01", 4: "g02", 5: "g03", 6: "g10", 7: "g11",
        8: "g12", 9: "g13"}
STREAMED = {1: "out_a", 2: "down_a", 3: "out_b", 5: "down_b0", 7: "pool", 9: "down_b1"}
BOUNDARY = [0, 4, 6, 8]
APPLIED = [0, 1, 2, 4, 8]
POSTS = [3, 5, 7, 9]
XMODE = ("out_a", "down_a")

FLOW = [("norm", 0), ("gemm", "in_a"), ("mix_a", 0), ("gemm", "out_a"), ("norm", 1), ("gemm", "up_a"),
        ("gemm", "down_a"), ("norm", 2), ("gemm", "in_b"), ("mix_b", 0), ("gemm", "out_b"), ("post", 3),
        ("norm", 4), ("gemm", "up_b0"), ("gemm", "down_b0"), ("post", 5), ("norm", 6), ("pooling", 0),
        ("gemm", "pool"), ("post", 7), ("norm", 8), ("gemm", "up_b1"), ("gemm", "down_b1"), ("post", 9)]
GAIN = {0: "mix_norm", 1: "ffn_norm", 2: "g00", 3: "g01", 4: "g02", 5: "g03", 6: "g10", 7: "g11",
        8: "g12", 9: "g13"}
STREAMED = {1: "out_a", 2: "down_a", 3: "out_b", 5: "down_b0", 7: "pool", 9: "down_b1"}
BOUNDARY = [0, 4, 6, 8]
APPLIED = [0, 1, 2, 4, 8]
POSTS = [3, 5, 7, 9]
XMODE = ("out_a", "down_a")

FLOW = [("norm", 0), ("gemm", "in_a"), ("mix_a", 0), ("gemm", "out_a"), ("norm", 1), ("gemm", "up_a"),
        ("gemm", "down_a"), ("norm", 2), ("gemm", "in_b"), ("mix_b", 0), ("gemm", "out_b"), ("post", 3),
        ("norm", 4), ("gemm", "up_b0"), ("gemm", "down_b0"), ("post", 5), ("norm", 6), ("pooling", 0),
        ("gemm", "pool"), ("post", 7), ("norm", 8), ("gemm", "up_b1"), ("gemm", "down_b1"), ("post", 9)]
GAIN = {0: "mix_norm", 1: "ffn_norm", 2: "g00", 3: "g01", 4: "g02", 5: "g03", 6: "g10", 7: "g11",
        8: "g12", 9: "g13"}
STREAMED = {1: "out_a", 2: "down_a", 3: "out_b", 5: "down_b0", 7: "pool", 9: "down_b1"}
BOUNDARY = [0, 4, 6, 8]
APPLIED = [0, 1, 2, 4, 8]
POSTS = [3, 5, 7, 9]
XMODE = ("out_a", "down_a")

VEC = {}
_c = 0
for _name, _w in [("mix_norm", 8), ("ffn_norm", 8), ("g00", 8), ("g01", 8), ("g02", 8), ("g03", 8),
                  ("g10", 8), ("g11", 8), ("g12", 8), ("g13", 8), ("pool_scale", 8), ("b_alpha", 2),
                  ("gla_norm", 1), ("q_norm", 1), ("k_norm", 1), ("b_f", 1)]:
    VEC[_name] = _c
    _c += _w
NVEC = _c


def build(nc, xT, vecs, conv, sinks, w_alpha2, pe, cmp_w1, cmp_w2, weights, yT, flow=FLOW):
    f32, f32r, bf16, i32 = mybir.dt.float32, mybir.dt.float32r, mybir.dt.bfloat16, mybir.dt.int32
    ALU, ACT, AX = mybir.AluOpType, mybir.ActivationFunctionType, mybir.AxisListType
    names = [w for k, w in flow if k == "gemm"]
    n_units = FIRST[names[-1]] + COUNT[names[-1]]
    has_b = "in_b" in names
    ctx = ExitStack()
    with ctx:
        def sb(name, shape, dt=f32, where=ctx):
            return where.enter_context(nc.sbuf_tensor(name, shape, dt))

        def sem(name):
            return ctx.enter_context(nc.semaphore(name))

        raw = [sb(f"raw{i}", [P, KH * P]) for i in range(RAW)]
        whi = [sb(f"whi{i}", [P, KH * P], f32r) for i in range(SPL)]
        wlo = [sb(f"wlo{i}", [P, KH * P], f32r) for i in range(SPL)]
        x = sb("x", [P, KD * S])
        hhi = sb("hhi", [P, KD * S], f32r)
        hlo = sb("hlo", [P, KD * S], f32r)
        rstd = sb("rstd", [P, S])
        sumsq = sb("sumsq", [P, S])
        sq = sb("sq", [P, 2, S])
        hf = sq
        ident = sb("ident", [P, P])
        ones = sb("ones", [P, P])
        vec = sb("vec", [P, NVEC])
        convw = sb("convw", [P, 4 * 2 * KF])
        epsc = sb("epsc", [P, 1])
        identb = sb("identb", [P, P], bf16)
        triang = sb("triang", [P, P], bf16)
        ffn = ExitStack()
        ahi = sb("ahi", [P, KF * S], f32r, ffn)
        alo = sb("alo", [P, KF * S], f32r, ffn)
        tmp = ExitStack()
        cvt = sb("cvt", [P, 2, S], f32, tmp)
        sil = sb("sil", [P, S], f32, tmp)
        gated = sb("gated", [P, S], f32, tmp)
        tmp.close()
        mt = sb("mt", [P, KD * S], f32, ffn)
        ffn.close()
        ma = ExitStack()
        za = sb("za", [P, 19 * S], f32, ma)
        la = sb("la", [P, 2 * S], f32, ma)
        cum = sb("cum", [P, 2 * S], f32, ma)
        eb = sb("eb", [P, 2 * S], f32, ma)
        kd = sb("kd", [P, 2 * S], f32, ma)
        segm = sb("segm", [P, S], f32, ma)
        kdT = sb("kdT", [P, 2 * S], f32, ma)
        gvT = sb("gvT", [P, 4 * S], f32, ma)
        aT = sb("aT", [P, 4 * S], f32, ma)
        svT = sb("svT", [P, S], f32, ma)
        state = sb("state", [P, 2, NCH, P], f32, ma)
        blk64 = sb("blk64", [P, P], f32, ma)
        cmask = sb("cmask", [P, P], f32, ma)
        biasA = sb("biasA", [P, NHEADS, 2 * P], f32, ma)
        distA = sb("distA", [P, 2 * P], f32, ma)
        sink = sb("sink", [P, NHEADS], f32, ma)
        nsink = sb("nsink", [P, NHEADS], f32, ma)
        wal = sb("wal", [16, 2 * P], f32, ma)
        pA = sb("pA", [P, 3, 2 * P], f32, ma)
        pTA = sb("pTA", [P, 2, 2 * P], f32, ma)
        statA = sb("statA", [P, 4 * 32], f32, ma)
        ma.close()
        mb = ExitStack()
        zb = sb("zb", [P, 23 * S], f32, mb)
        vT = sb("vT", [P, 6 * S], f32, mb)
        biasB = sb("biasB", [P, NHEADS, S], f32, mb)
        w1m = ExitStack()
        cw1 = sb("cw1", [P, 2, 32 * HD], f32, w1m)
        w1m.close()
        pTc = sb("pTc", [32, NHEADS * S], f32, mb)
        pB = sb("pB", [P, 3, S], f32, mb)
        pTB = sb("pTB", [P, 2, S], f32, mb)
        pc = pB[:, 0:2, :].rearrange("p a s -> p (a s)")
        statB = sb("statB", [P, 3 * 96], f32, mb)
        kcmp = sb("kcmp", [P, 32], f32, mb)
        vcmp = sb("vcmp", [32, P], f32, mb)
        cw2 = sb("cw2", [P, 2 * HD], f32, mb)
        cpe = sb("cpe", [P, 2 * 32], f32, mb)
        glu = sb("glu", [P, 2 * 32], f32, mb)
        cst = sb("cst", [P, 2 * 32], f32, mb)
        gates = sb("gates", [P, NB * HD], f32, mb)
        distC = sb("distC", [P, P], f32, mb)
        maskC = sb("maskC", [P, P], f32, mb)
        mb.close()
        mp = ExitStack()
        pu = sb("pu", [P, KD * S], f32, mp)
        win = sb("win", [P, 2, 16 + S], f32, mp)
        invc = sb("invc", [P, 4, S], f32, mp)
        mp.close()

        ps = ctx.enter_context(nc.psum_tensor("ps", [P, 8, S], f32))

        raw_ready = [sem(f"raw_ready{i}") for i in range(RAW)]
        hi_done, lo_done, unit_done = sem("hi_done"), sem("lo_done"), sem("unit_done")
        evac = {p: sem(f"evac_{p}") for p in names}
        sq_ready, sq_used = sem("sq_ready"), sem("sq_used")
        sq_base = {p: 8 * k for k, p in enumerate(STREAMED.values())}
        zeroed = sem("zeroed")
        hid = {k: sem("hidden_" + k) for k in ("tap2", "tap1", "tap0", "silu", "prod", "ahi", "alo")}
        pair_base = {"up_a": 0, "up_b0": KF, "up_b1": 2 * KF}
        ms_ready, rstd_ln, rstd_ready = sem("ms_ready"), sem("rstd_ln"), sem("rstd_ready")
        bsq_ready, bsq_used = sem("bsq_ready"), sem("bsq_used")
        hf_ready, h_hi, h_lo = sem("hf_ready"), sem("h_hi"), sem("h_lo")
        post_done, x_done = sem("post_done"), sem("x_done")
        ld_x, ld_vec, ld_cmp = sem("ld_x"), sem("ld_vec"), sem("ld_cmp")
        filled, const_0, const_a, const_b = sem("filled"), sem("const_0"), sem("const_a"), sem("const_b")
        stored = sem("stored")
        A = {k: sem("a_" + k) for k in (
                "logit", "logit_b", "abs", "exp", "log1p", "logsig", "decay", "rest", "eb", "enb", "ed",
                "qke", "kd", "kdT", "kdT_c", "gvT", "gvT_c", "svT", "svT_c", "score", "masked", "cs",
                "st", "o", "osq", "oms", "oln", "orstd", "sig", "on", "og", "ohi", "olo", "nsq", "nms",
                "nln", "nrstd", "nq", "sinkn", "bias", "s", "m", "es", "p", "den", "r", "pn", "t", "tc",
                "pv")}
        B = {}
        if has_b:
            B = {k: sem("b_" + k) for k in (
                "vt", "vt_c", "gt", "gx", "g1", "gate", "fz", "fabs", "fexp", "fln", "fls", "fc", "nc",
                "nc_c", "bias", "pe", "hid", "gelu", "kc", "kc_c", "cs", "cb", "cm", "cd", "ce", "ck",
                "csum", "cf", "cp", "ct", "ct_c", "s", "m", "p", "den", "r", "pn", "t", "tc", "pv",
                "ohi", "olo", "pool_u", "pool_w", "pool_m", "pool_hi", "pool_lo")}

        BANK_MS = 4
        if flow[-1][0] == "post":
            final_sem, final_count = x_done, 8 * (POSTS.index(flow[-1][1]) + 1)
        else:
            final_sem, final_count = evac[names[-1]], 8
        mix_unit = FIRST["in_b"]

        def split_cols(n):
            return next(BLOCKS[p] * P for p in ORDER if FIRST[p] <= n < FIRST[p] + COUNT[p])

        def units(eng, first, last, peel, step):
            for u in range(first, min(peel, last)):
                step(u, 0)
            first = max(first, peel)
            loops = (last - first) // 4
            if loops >= 2:
                with eng.Fori(0, loops) as i:
                    for u in range(first, first + 4):
                        step(u, i)
                first += 4 * loops
            for u in range(first, last):
                step(u, 0)

        def tile(buf, t):
            return buf[:, bass.ds(t * S, S)]

        def col(name, t=0):
            return vec[:, VEC[name] + t:VEC[name] + t + 1]

        def peel_of(p):
            return 8 if p[:4] == "down" else 4

        ITEMS_A = [(t, half, b) for t in range(4) for half in range(2) for b in range(NB)]
        ITEMS_B = [(br, t, half, b) for t in range(4) for half in range(2) for b in range(NB)
                   for br in ("slc", "win")]
        ITEMS_B += [("fox", t, half, b) for t in range(4) for half in range(2) for b in range(NB)]
        ZQ, ZKC, ZVC, ZKS, ZVS, ZKW, ZVW, ZFQ, ZFK, ZFV = 1, 5, 6, 7, 8, 9, 10, 11, 15, 19
        ZV = [ZVS, ZVW, ZFV, ZFV + 1, ZFV + 2, ZFV + 3]
        ZNC = [ZKC, ZVC, ZVS, ZVW, ZFV, ZFV + 1, ZFV + 2, ZFV + 3]
        GROUPS_B = [(4 + t, 16 * (t + 1)) for t in range(4)] + [(t, 64 + 8 * (t + 1)) for t in range(4)]

        block = ctx.enter_context(nc.Block())

        @block.sync
        def _(sp):
            sp.dma_start(x[:, :], xT).then_inc(ld_x, 16)
            for p in names:
                n0, cols = FIRST[p], BLOCKS[p] * P

                def load(u, i, p=p, n0=n0, cols=cols):
                    n = n0 + u
                    if n >= RAW:
                        sp.wait_ge(lo_done, n - RAW + 1 + 4 * i)
                    sp.dma_start(raw[n % RAW][:, 0:cols],
                                 weights[p][bass.ds(u + 4 * i, 1), :, :].rearrange("a p c -> (a p) c")
                                 ).then_inc(raw_ready[n % RAW], 16)

                units(sp, 0, COUNT[p], 4, load)
            sp.wait_ge(final_sem, final_count)
            sp.dma_start(yT, x[:, :]).then_inc(stored, 16)
            sp.wait_ge(stored, 16)

        @block.gpsimd
        def _(pool):
            pool.dma_start(vec[:, :], vecs).then_inc(ld_vec, 16)
            pool.dma_start(convw[:, :], conv).then_inc(ld_vec, 16)
            pool.dma_start(wal[:, :], w_alpha2).then_inc(ld_vec, 16)
            pool.dma_start(sink[:, :], sinks).then_inc(ld_vec, 16)
            n_filled = [0]

            def fill(ins):
                n_filled[0] += 1
                ins.then_inc(filled, 1)
                pool.wait_ge(filled, n_filled[0])

            def select(out, pattern, base, chan, op, value):
                return pool.affine_select(out=out, in_=out, compare_op=op, fill=value, base=base,
                                          pattern=pattern, channel_multiplier=chan)

            fill(pool.memset(ones[:, :], 1.0 / D))
            fill(pool.memset(epsc[:, :], EPS))
            fill(pool.memset(ident[:, :], 0.0))
            select(ident[:, :], [[-1, P]], 0, 1, ALU.not_equal, 1.0).then_inc(const_0, 1)
            fill(pool.memset(identb[:, :], 0.0))
            fill(select(identb[:, :], [[-1, P]], 0, 1, ALU.not_equal, 1.0))
            fill(pool.memset(triang[:, :], 0.0))
            fill(select(triang[:, :], [[-1, P]], 0, 1, ALU.is_ge, -1e32))
            fill(pool.memset(segm[:, :], 1.0))
            fill(pool.memset(segm[:, :].rearrange("p (n c) -> p n c", c=CHUNK)[:, :, 0:1], 0.0))
            fill(pool.memset(cmask[:, :], 1.0))
            fill(select(cmask[:, :], [[1, P]], 0, -1, ALU.is_ge, 0.0))
            fill(select(cmask[:, CHUNK:P], [[0, P - CHUNK]], -CHUNK, 1, ALU.is_ge, 0.0))
            fill(pool.memset(blk64[:, :], 1.0 / HD))
            fill(select(blk64[:, 0:HD], [[0, HD]], HD - 1, -1, ALU.is_ge, 0.0))
            fill(select(blk64[:, HD:P], [[0, HD]], -HD, 1, ALU.is_ge, 0.0))
            fill(pool.iota(distA[:, :], [[-1, 2 * P]], P, 1, allow_small_or_imprecise_dtypes=True))
            fill(select(distA[:, :], [[-1, 2 * P]], P, 1, ALU.is_ge, BIG))
            select(distA[:, :], [[1, 2 * P]], -1, -1, ALU.is_ge, BIG).then_inc(const_a, 1)
            if has_b:
                pool.wait_ge(unit_done, mix_unit + 1)
                for half in range(2):
                    rows = slice(HD * half, HD * half + HD)
                    for kv in range(2):
                        pool.dma_start(cw1[rows, kv, :], cmp_w1[kv]).then_inc(ld_cmp, 16)
                        pool.dma_start(cw2[rows, kv * HD:kv * HD + HD], cmp_w2[kv]).then_inc(ld_cmp, 16)
                        pool.dma_start(cpe[rows, kv * 32:kv * 32 + 32], pe[kv]).then_inc(ld_cmp, 16)
                fill(pool.iota(biasB[:, 0, :], [[-1, S]], S - P, 1, allow_small_or_imprecise_dtypes=True))
                fill(select(biasB[:, 0, :], [[-1, S]], S - P, 1, ALU.is_ge, BIG))
                dc = distC[:, :].rearrange("p (b n) -> p b n", n=32)
                mc = maskC[:, :].rearrange("p (b n) -> p b n", n=32)
                pat = [[P, NB], [-16, 32]]
                fill(pool.iota(dc, pat, -31, 1, allow_small_or_imprecise_dtypes=True))
                fill(select(dc, pat, -31, 1, ALU.is_ge, BIG))
                fill(pool.memset(dc[:, :, NCMP:32], BIG))
                fill(pool.memset(maskC[:, :], 1.0))
                fill(select(mc, pat, -31, 1, ALU.is_ge, 0.0))
                fill(pool.memset(mc[:, :, NCMP:32], 0.0))
                fill(pool.memset(kcmp[:, :], 0.0))
                pool.memset(vcmp[:, :], 0.0).then_inc(const_b, 1)
            for kind, what in flow:
                if kind == "post":
                    e = POSTS.index(what)
                    for m in range(KD):
                        pool.wait_ge(post_done, 8 * e + m + 1)
                        pool.tensor_tensor(tile(x, m), tile(x, m), tile(mt, m), ALU.add).then_inc(x_done, 1)

        @block.scalar
        def _(act):
            def split_hi(n, i, cols):
                act.wait_ge(raw_ready[n % RAW], 16 * (n // RAW + 1 + i))
                if n >= SPL:
                    act.wait_ge(unit_done, n - SPL + 1 + 4 * i)
                act.activation(whi[n % SPL][:, 0:cols], raw[n % RAW][:, 0:cols], ACT.Copy).then_inc(hi_done, 1)

            def evacuate(p, u, i):
                n = FIRST[p] + u
                if p[:2] == "in":
                    z = za if p == "in_a" else zb
                    act.wait_ge(unit_done, n + 1 + 4 * i)
                    act.activation(tile(z, u + 4 * i), ps[:, u % 4, :], ACT.Copy).then_inc(evac[p], 1)
                elif p[:2] == "up":
                    if u % 2:
                        hidden(p, u, i)
                elif p == "pool":
                    act.wait_ge(B["pool_lo"], KD)
                    for j in range(4):
                        act.wait_ge(unit_done, n + 1)
                        normalized(p, 4 * u + j, 0, j, col("pool_scale", 4 * u + j))
                elif p[:4] == "down":
                    if u % 2:
                        act.wait_ge(unit_done, n + 1 + 4 * i)
                        normalized(p, u // 2, 2 * i, (u // 2) % 2, None)
                else:
                    act.wait_ge(unit_done, n + 1)
                    normalized(p, u, 0, u % 4, None)

            def normalized(p, m, i, bank, scale):
                src = x
                if p not in XMODE:
                    act.activation(tile(mt, m + i), ps[:, bank, :], ACT.Copy,
                                   scale=1.0 if scale is None else scale).then_inc(evac[p], 1)
                    src = mt
                act.wait_ge(evac[p], m + 1 + i)
                if m >= 2:
                    act.wait_ge(sq_used, sq_base[p] + m - 1 + i)
                act.activation(sq[:, m % 2, :], tile(src, m + i), ACT.Square).then_inc(sq_ready, 1)

            def hidden(p, u, i):
                k, f, fi = hid, u // 2, 2 * i
                done = pair_base[p] + f + fi
                act.wait_ge(unit_done, FIRST[p] + u + 1 + 4 * i)
                if p == "up_a":
                    if f >= 1:
                        act.wait_ge(k["prod"], done)
                    for s in range(2):
                        c = f + s * KF
                        act.activation(cvt[:, s, :], ps[:, (u - 1 + s) % 4, :], ACT.Identity,
                                       bias=convw[:, bass.ds(3 * 2 * KF + c + fi, 1)],
                                       scale=convw[:, bass.ds(2 * 2 * KF + c + fi, 1)]).then_inc(k["tap2"], 1)
                    act.wait_ge(k["tap0"], 2 * f + 1 + 2 * fi)
                    act.activation(sil[:, :], cvt[:, 0, :], ACT.Silu).then_inc(k["silu"], 1)
                else:
                    if f >= 1:
                        act.wait_ge(k["prod"], done)
                    act.activation(sil[:, :], ps[:, (u - 1) % 4, :], ACT.Silu).then_inc(k["silu"], 1)
                act.wait_ge(k["prod"], done + 1)
                act.activation(tile(ahi, f + fi), gated[:, :], ACT.Copy).then_inc(k["ahi"], 1)

            def gemm(p):
                n0, count = FIRST[p], COUNT[p]

                def step(u, i):
                    split_hi(n0 + u, i, BLOCKS[p] * P)
                    evacuate(p, u - 2, i)

                units(act, 2, count, count if p[:4] == "down" else peel_of(p), step)
                for k in range(2):
                    n = n0 + count + k
                    if n < n_units:
                        split_hi(n, 0, split_cols(n))
                    evacuate(p, count - 2 + k, 0)

            def statistics(e):
                act.wait_ge(ms_ready, e + 1)
                act.activation(rstd[:, :], ps[:, BANK_MS, :], ACT.Ln, bias=epsc[:, :]).then_inc(rstd_ln, 1)
                act.wait_ge(rstd_ln, e + 1)
                act.activation(rstd[:, :], rstd[:, :], ACT.Exp, scale=-0.5).then_inc(rstd_ready, 1)

            def norm(e):
                if e in BOUNDARY:
                    base = 8 * BOUNDARY.index(e)
                    for m in range(KD):
                        if e == 0:
                            if m == 0:
                                act.wait_ge(ld_x, 16)
                        else:
                            act.wait_ge(x_done, 8 * POSTS.index(e - 1) + m + 1)
                        if m >= 2:
                            act.wait_ge(bsq_used, 7 * BOUNDARY.index(e) + m - 1)
                        act.activation(sq[:, m % 2, :], tile(x, m), ACT.Square).then_inc(bsq_ready, 1)
                statistics(e)
                if e in APPLIED:
                    base = 8 * APPLIED.index(e)
                    for m in range(KD):
                        act.wait_ge(hf_ready, base + m + 1)
                        act.activation(tile(hhi, m), hf[:, m % 2, :], ACT.Copy).then_inc(h_hi, 1)

            def mix_a():
                act.wait_ge(A["logit_b"], 2)
                act.activation(eb[:, :], la[:, :], ACT.Abs).then_inc(A["abs"], 1)
                act.wait_ge(A["abs"], 1)
                act.activation(eb[:, :], eb[:, :], ACT.Exp, scale=-1.0).then_inc(A["exp"], 1)
                act.wait_ge(A["exp"], 1)
                act.activation(eb[:, :], eb[:, :], ACT.Ln, bias=1.0).then_inc(A["log1p"], 1)
                for h in range(4):
                    act.wait_ge(A["gvT"], h + 1)
                    act.activation(tile(gvT, h), ps[:, 4 + h, :], ACT.Copy).then_inc(A["gvT_c"], 1)
                act.wait_ge(A["svT"], 1)
                act.activation(svT[:, :], ps[:, 2, :], ACT.Copy).then_inc(A["svT_c"], 1)
                act.wait_ge(A["decay"], 2)
                act.activation(eb[:, :], cum[:, :], ACT.Exp, scale=1 / 16).then_inc(A["eb"], 1)
                act.activation(la[:, :], cum[:, :], ACT.Exp, scale=-1 / 16).then_inc(A["enb"], 1)
                act.wait_ge(A["rest"], 2)
                act.activation(kd[:, :], kd[:, :], ACT.Exp, scale=1 / 16).then_inc(A["ed"], 1)
                for j in range(5):
                    if j >= 2:
                        act.wait_ge(A["nms"], j - 1)
                    act.activation(sq[:, j % 2, :], tile(za, 13 + j), ACT.Square).then_inc(A["nsq"], 1)
                    act.wait_ge(A["nms"], j + 1)
                    if j >= 1:
                        act.wait_ge(A["nq"], j)
                    act.activation(rstd[:, :], ps[:, 4 + j % 2, :], ACT.Ln, bias=epsc[:, :]).then_inc(A["nln"], 1)
                    act.wait_ge(A["nln"], j + 1)
                    act.activation(rstd[:, :], rstd[:, :], ACT.Exp, scale=-0.5).then_inc(A["nrstd"], 1)
                for t in range(2):
                    act.wait_ge(A["kdT"], t + 1)
                    act.activation(tile(kdT, t), ps[:, t, :], ACT.Copy).then_inc(A["kdT_c"], 1)
                act.wait_ge(const_a, 1)
                for h in range(NHEADS):
                    act.activation(biasA[:, h, :], distA[:, :], ACT.Copy, scale=-8 * SLOPE[h]).then_inc(A["bias"], 1)
                act.activation(za[:, 9 * S:13 * S], za[:, 9 * S:13 * S], ACT.Silu).then_inc(A["sig"], 1)
                for h in range(4):
                    act.wait_ge(A["o"], h + 1)
                    if h >= 2:
                        act.wait_ge(A["oms"], h - 1)
                    act.activation(sq[:, h % 2, :], ps[:, h, :], ACT.Square).then_inc(A["osq"], 1)
                    act.wait_ge(A["oms"], h + 1)
                    if h >= 1:
                        act.wait_ge(A["on"], h)
                    act.activation(rstd[:, :], ps[:, 4 + h % 2, :], ACT.Ln, bias=epsc[:, :],
                                   scale=float(D // P)).then_inc(A["oln"], 1)
                    act.wait_ge(A["oln"], h + 1)
                    act.activation(rstd[:, :], rstd[:, :], ACT.Exp, scale=-0.5).then_inc(A["orstd"], 1)
                    act.wait_ge(A["og"], h + 1)
                    act.activation(tile(hhi, h), tile(aT, h), ACT.Copy).then_inc(A["ohi"], 1)
                for s in range(len(ITEMS_A) + 4):
                    if s < len(ITEMS_A):
                        t, half, b = ITEMS_A[s]
                        w = P * min(b + 1, 2)
                        act.wait_ge(A["m"], s + 1)
                        act.activation(statA[:, 4 * s + 3:4 * s + 4], sink[:, t + 4 * half:t + 4 * half + 1], ACT.Exp,
                                       bias=statA[:, 4 * s:4 * s + 1]).then_inc(A["es"], 1)
                        act.activation(pA[:, s % 3, 0:w], pA[:, s % 3, 0:w], ACT.Exp, scale=-1.0,
                                       bias=statA[:, 4 * s:4 * s + 1],
                                       accum_out=statA[:, 4 * s + 1:4 * s + 2]).then_inc(A["p"], 1)
                    if 0 <= s - 2 < len(ITEMS_A):
                        g = s - 2
                        w = P * min(ITEMS_A[g][2] + 1, 2)
                        act.wait_ge(A["t"], g + 1)
                        if g >= 2:
                            act.wait_ge(A["pv"], g - 1)
                        act.activation(pTA[:, g % 2, 0:w], ps[:, 2 + g % 2, 0:w], ACT.Copy).then_inc(A["tc"], 1)
                    if s % 8 == 3 and s > 8:
                        t = s // 8 - 1
                        act.wait_ge(A["pv"], 8 * (t + 1))
                        act.activation(tile(hhi, 4 + t), ps[:, 4 + t % 2, :], ACT.Copy).then_inc(A["ohi"], 1)

            def mix_b():
                for j in range(6):
                    act.wait_ge(B["vt"], j + 1)
                    act.activation(tile(vT, j), ps[:, j % 4, :], ACT.Copy).then_inc(B["vt_c"], 1)
                act.wait_ge(B["gt"], 1)
                act.activation(gates[:, :], ps[:, 4, 0:NB * HD], ACT.Exp, scale=-1.0).then_inc(B["gx"], 1)
                act.wait_ge(B["fz"], 1)
                act.activation(sq[0:8, 1, :], sq[0:8, 0, :], ACT.Abs).then_inc(B["fabs"], 1)
                act.wait_ge(B["fabs"], 1)
                act.activation(sq[0:8, 1, :], sq[0:8, 1, :], ACT.Exp, scale=-1.0).then_inc(B["fexp"], 1)
                act.wait_ge(B["fexp"], 1)
                act.activation(sq[0:8, 1, :], sq[0:8, 1, :], ACT.Ln, bias=1.0).then_inc(B["fln"], 1)
                act.wait_ge(B["hid"], 2)
                for kv in range(2):
                    act.activation(glu[:, 32 * kv:32 * kv + NCMP], ps[:, 5, 32 * kv:32 * kv + NCMP],
                                   ACT.Gelu_apprx_tanh).then_inc(B["gelu"], 1)
                act.wait_ge(const_b, 1)
                act.wait_ge(B["kc"], 2)
                act.activation(kcmp[:, 0:NCMP], ps[:, 6, 0:NCMP], ACT.Copy).then_inc(B["kc_c"], 1)
                for g in range(2):
                    act.activation(vcmp[0:NCMP, HD * g:HD * g + HD], ps[0:NCMP, 2 + g, 0:HD], ACT.Copy
                                   ).then_inc(B["kc_c"], 1)
                for h in [1, 2, 3, 4, 5, 6, 7, 0]:
                    if h == 0:
                        act.wait_ge(B["bias"], 7)
                    act.activation(biasB[:, h, :], biasB[:, 0, :], ACT.Copy, scale=-8 * SLOPE[h]).then_inc(B["bias"], 1)
                for h in range(NHEADS):
                    act.wait_ge(B["nc"], h + 1)
                    act.activation(tile(zb, ZNC[h]), ps[:, h % 4, :], ACT.Copy, scale=-8.0).then_inc(B["nc_c"], 1)
                act.wait_ge(B["cd"], 2)
                act.activation(pc[:, :], pc[:, :], ACT.Exp, scale=0.125).then_inc(B["ce"], 1)
                for h in range(NHEADS):
                    act.wait_ge(B["ct"], h + 1)
                    act.activation(pTc[:, h * S:h * S + S], ps[0:32, 6 + h % 2, :], ACT.Copy).then_inc(B["ct_c"], 1)
                n = len(ITEMS_B)
                for s in range(n + 4):
                    if s < n:
                        w = P * (ITEMS_B[s][3] + 1)
                        act.wait_ge(B["m"], s + 1)
                        act.activation(pB[:, s % 3, 0:w], pB[:, s % 3, 0:w], ACT.Exp, scale=-1.0,
                                       bias=statB[:, 3 * s:3 * s + 1],
                                       accum_out=statB[:, 3 * s + 1:3 * s + 2]).then_inc(B["p"], 1)
                    if 0 <= s - 2 < n:
                        g = s - 2
                        w = P * (ITEMS_B[g][3] + 1)
                        act.wait_ge(B["t"], g + 1)
                        if g >= 2:
                            act.wait_ge(B["pv"], g - 1)
                        act.activation(pTB[:, g % 2, 0:w], ps[:, 2 + g % 2, 0:w], ACT.Copy).then_inc(B["tc"], 1)
                    for j, (row, end) in enumerate(GROUPS_B):
                        if s == end + 3:
                            act.wait_ge(B["pv"], end)
                            act.activation(tile(hhi, row), ps[:, 4 + j % 2, :], ACT.Copy).then_inc(B["ohi"], 1)

            def pooling():
                for m in range(KD):
                    act.wait_ge(B["pool_m"], m + 1)
                    act.activation(tile(hhi, m), hf[:, m % 2, :], ACT.Copy).then_inc(B["pool_hi"], 1)

            act.wait_ge(const_0, 1)
            for n in range(2):
                split_hi(n, 0, split_cols(n))
            for kind, what in flow:
                if kind == "norm":
                    norm(what)
                elif kind == "gemm":
                    gemm(what)
                elif kind == "post":
                    statistics(what)
                elif kind == "mix_a":
                    mix_a()
                elif kind == "mix_b":
                    mix_b()
                elif kind == "pooling":
                    pooling()

        @block.vector
        def _(dve):
            def split_lo(n, i, cols):
                dve.wait_ge(hi_done, n + 1 + 4 * i)
                dve.tensor_tensor(wlo[n % SPL][:, 0:cols], raw[n % RAW][:, 0:cols],
                                  whi[n % SPL][:, 0:cols].bitcast(f32), ALU.subtract).then_inc(lo_done, 1)

            def summed(p, m, i):
                dve.wait_ge(sq_ready, sq_base[p] + m + 1 + i)
                if m >= 1:
                    dve.wait_ge(sq_used, sq_base[p] + m + i)
                dve.tensor_tensor(sumsq[:, :], sumsq[:, :], sq[:, m % 2, :], ALU.add).then_inc(sq_used, 1)

            def residual(p, m, i, bank):
                if p in XMODE:
                    dve.tensor_tensor(tile(x, m + i), ps[:, bank, :], tile(x, m + i), ALU.add).then_inc(evac[p], 1)
                summed(p, m, i)

            def evacuate(p, u, i):
                n = FIRST[p] + u
                if p[:2] == "up":
                    if u % 2:
                        hidden(p, u, i)
                elif p == "pool":
                    for j in range(4):
                        residual(p, 4 * u + j, 0, j)
                elif p[:4] == "down":
                    if u % 2:
                        dve.wait_ge(unit_done, n + 1 + 4 * i)
                        residual(p, u // 2, 2 * i, (u // 2) % 2)
                elif p[:3] == "out":
                    dve.wait_ge(unit_done, n + 1)
                    residual(p, u, 0, u % 4)

            def hidden(p, u, i):
                k, f, fi = hid, u // 2, 2 * i
                done = pair_base[p] + f + fi
                dve.wait_ge(unit_done, FIRST[p] + u + 1 + 4 * i)
                if p == "up_a":
                    for s in range(2):
                        c = f + s * KF
                        bank = (u - 1 + s) % 4
                        dve.wait_ge(k["tap2"], 2 * f + s + 1 + 2 * fi)
                        dve.scalar_tensor_tensor(out=cvt[:, s, 1:S], in0=ps[:, bank, 0:S - 1],
                                                 scalar=convw[:, bass.ds(2 * KF + c + fi, 1)],
                                                 in1=cvt[:, s, 1:S], op0=ALU.mult, op1=ALU.add
                                                 ).then_inc(k["tap1"], 1)
                        dve.wait_ge(k["tap1"], 2 * f + s + 1 + 2 * fi)
                        dve.scalar_tensor_tensor(out=cvt[:, s, 2:S], in0=ps[:, bank, 0:S - 2],
                                                 scalar=convw[:, bass.ds(c + fi, 1)],
                                                 in1=cvt[:, s, 2:S], op0=ALU.mult, op1=ALU.add
                                                 ).then_inc(k["tap0"], 1)
                    dve.wait_ge(k["tap0"], 2 * f + 2 + 2 * fi)
                    other = cvt[:, 1, :]
                else:
                    other = ps[:, u % 4, :]
                dve.wait_ge(k["silu"], done + 1)
                if f >= 1:
                    dve.wait_ge(k["alo"], done)
                dve.tensor_tensor(gated[:, :], other, sil[:, :], ALU.mult).then_inc(k["prod"], 1)
                dve.wait_ge(k["ahi"], done + 1)
                dve.tensor_tensor(tile(alo, f + fi), gated[:, :], tile(ahi, f + fi).bitcast(f32),
                                  ALU.subtract).then_inc(k["alo"], 1)

            def gemm(p):
                n0, count = FIRST[p], COUNT[p]
                if p in sq_base:
                    e = next(e for e, q in STREAMED.items() if q == p)
                    dve.memset(sumsq[:, :], 0.0).then_inc(zeroed, 1)
                    dve.wait_ge(zeroed, sorted(STREAMED).index(e) + 1)

                def step(u, i):
                    split_lo(n0 + u, i, BLOCKS[p] * P)
                    evacuate(p, u - 2, i)

                units(dve, 2, count, peel_of(p), step)
                for k in range(2):
                    n = n0 + count + k
                    if n < n_units:
                        split_lo(n, 0, split_cols(n))
                    evacuate(p, count - 2 + k, 0)

            def norm(e):
                dve.wait_ge(rstd_ready, e + 1)
                if e == 0:
                    dve.wait_ge(ld_vec, 64)
                if e == 6:
                    for m in range(KD):
                        dve.scalar_tensor_tensor(out=tile(pu, m), in0=tile(x, m), scalar=col(GAIN[e], m),
                                                 in1=rstd[:, :], op0=ALU.mult, op1=ALU.mult
                                                 ).then_inc(B["pool_u"], 1)
                    return
                base = 8 * APPLIED.index(e)
                for m in range(KD + 1):
                    if m < KD:
                        if m >= 2:
                            dve.wait_ge(h_hi, base + m - 1)
                            dve.wait_ge(h_lo, base + m - 1)
                        dve.scalar_tensor_tensor(out=hf[:, m % 2, :], in0=tile(x, m), scalar=col(GAIN[e], m),
                                                 in1=rstd[:, :], op0=ALU.mult, op1=ALU.mult).then_inc(hf_ready, 1)
                    if m >= 1:
                        dve.wait_ge(h_hi, base + m)
                        dve.tensor_tensor(tile(hlo, m - 1), hf[:, (m - 1) % 2, :],
                                          tile(hhi, m - 1).bitcast(f32), ALU.subtract).then_inc(h_lo, 1)

            def post(e):
                dve.wait_ge(rstd_ready, e + 1)
                for m in range(KD):
                    dve.scalar_tensor_tensor(out=tile(mt, m), in0=tile(mt, m), scalar=col(GAIN[e], m),
                                             in1=rstd[:, :], op0=ALU.mult, op1=ALU.mult).then_inc(post_done, 1)

            def mix_a():
                for t in range(2):
                    dve.wait_ge(A["logit"], t + 1)
                    dve.tensor_scalar(tile(la, t), ps[:, t, :], col("b_alpha", t), None, ALU.add
                                      ).then_inc(A["logit_b"], 1)
                dve.wait_ge(A["log1p"], 1)
                dve.wait_ge(A["logit_b"], 2)
                dve.scalar_tensor_tensor(out=la[:, :], in0=la[:, :], scalar=0.0, in1=eb[:, :], op0=ALU.min,
                                         op1=ALU.subtract).then_inc(A["logsig"], 1)
                dve.wait_ge(A["logsig"], 1)
                dve.wait_ge(const_a, 1)
                for t in range(2):
                    dve.tensor_tensor_scan(tile(cum, t), segm[:, :], tile(la, t), 0.0, ALU.mult, ALU.add
                                           ).then_inc(A["decay"], 1)
                dve.wait_ge(A["decay"], 2)
                for t in range(2):
                    cv = tile(cum, t).rearrange("p (n c) -> p n c", c=CHUNK)
                    ev = tile(kd, t).rearrange("p (n c) -> p n c", c=CHUNK)
                    dve.tensor_tensor(ev, cv[:, :, CHUNK - 1:CHUNK].broadcast_to([P, NCH, CHUNK]), cv,
                                      ALU.subtract).then_inc(A["rest"], 1)
                dve.wait_ge(A["eb"], 1)
                dve.scalar_tensor_tensor(out=za[:, 3 * S:5 * S], in0=za[:, 3 * S:5 * S], scalar=HD ** -0.5,
                                         in1=eb[:, :], op0=ALU.mult, op1=ALU.mult).then_inc(A["qke"], 1)
                dve.wait_ge(A["ed"], 1)
                dve.wait_ge(A["enb"], 1)
                dve.tensor_tensor(kd[:, :], za[:, S:3 * S], kd[:, :], ALU.mult).then_inc(A["kd"], 1)
                dve.tensor_tensor(za[:, S:3 * S], za[:, S:3 * S], la[:, :], ALU.mult).then_inc(A["qke"], 1)
                for j in range(5):
                    dve.wait_ge(A["nrstd"], j + 1)
                    dve.scalar_tensor_tensor(out=tile(za, 13 + j), in0=tile(za, 13 + j),
                                             scalar=col("q_norm" if j < 4 else "k_norm"), in1=rstd[:, :],
                                             op0=ALU.mult, op1=ALU.mult).then_inc(A["nq"], 1)
                dve.tensor_scalar(nsink[:, :], sink[:, :], -1.0, None, ALU.mult).then_inc(A["sinkn"], 1)
                for h in range(4):
                    dve.wait_ge(A["score"], h + 1)
                    dve.tensor_tensor(tile(aT, h).rearrange("p (b c) -> p b c", c=P),
                                      ps[:, 2 + h % 2, :].rearrange("p (b c) -> p b c", c=P),
                                      cmask[:, :].rearrange("p (b c) -> p b c", b=1).broadcast_to([P, NB, P]),
                                      ALU.mult).then_inc(A["masked"], 1)
                dve.memset(state[:, :, 0, :], 0.0).then_inc(A["st"], 1)
                for n in range(NCH - 1):
                    for t in range(2):
                        if n == 0:
                            dve.wait_ge(A["cs"], t + 1)
                        dve.wait_ge(A["st"], 1 + (0 if n == 0 else 2 * n - 1 + t))
                        c = t * S + n * CHUNK + CHUNK - 1
                        dve.scalar_tensor_tensor(out=state[:, t, n + 1, :], in0=state[:, t, n, :],
                                                 scalar=eb[:, c:c + 1],
                                                 in1=ps[:, 4 + 2 * t + n % 2, (n // 2) * P:(n // 2) * P + P],
                                                 op0=ALU.mult, op1=ALU.add).then_inc(A["st"], 1)
                dve.wait_ge(A["sig"], 1)
                for h in range(4):
                    dve.wait_ge(A["orstd"], h + 1)
                    dve.scalar_tensor_tensor(out=tile(aT, h), in0=ps[:, h, :], scalar=col("gla_norm"),
                                             in1=rstd[:, :], op0=ALU.mult, op1=ALU.mult).then_inc(A["on"], 1)
                    dve.wait_ge(A["on"], h + 1)
                    dve.tensor_tensor(tile(aT, h), tile(aT, h), tile(za, 9 + h), ALU.mult).then_inc(A["og"], 1)
                    dve.wait_ge(A["ohi"], h + 1)
                    dve.tensor_tensor(tile(hlo, h), tile(aT, h), tile(hhi, h).bitcast(f32), ALU.subtract
                                      ).then_inc(A["olo"], 1)
                dve.wait_ge(A["bias"], NHEADS)
                dve.wait_ge(A["sinkn"], 1)
                for s in range(len(ITEMS_A) + 4):
                    if s < len(ITEMS_A):
                        t, half, b = ITEMS_A[s]
                        h, w = t + 4 * half, P * min(b + 1, 2)
                        dve.wait_ge(A["s"], s + 1)
                        if s >= 3:
                            dve.wait_ge(A["t"], s - 2)
                        dve.tensor_tensor_reduce(out=pA[:, s % 3, 0:w], in0=ps[:, s % 2, 0:w],
                                                 in1=biasA[:, h, 2 * P - w:2 * P], scale=-0.125,
                                                 scalar=nsink[:, h:h + 1], op0=ALU.add, op1=ALU.min,
                                                 accum_out=statA[:, 4 * s:4 * s + 1]).then_inc(A["m"], 1)
                    if 0 <= s - 1 < len(ITEMS_A):
                        g = s - 1
                        w = P * min(ITEMS_A[g][2] + 1, 2)
                        dve.wait_ge(A["p"], g + 1)
                        dve.wait_ge(A["es"], g + 1)
                        c = 4 * g
                        dve.tensor_tensor(statA[:, c + 2:c + 3], statA[:, c + 1:c + 2], statA[:, c + 3:c + 4], ALU.add
                                          ).then_inc(A["den"], 1)
                        dve.wait_ge(A["den"], g + 1)
                        dve.reciprocal(statA[:, c + 2:c + 3], statA[:, c + 2:c + 3]).then_inc(A["r"], 1)
                        dve.wait_ge(A["r"], g + 1)
                        dve.tensor_scalar(pA[:, g % 3, 0:w], pA[:, g % 3, 0:w], statA[:, c + 2:c + 3], None, ALU.mult
                                          ).then_inc(A["pn"], 1)
                    if s % 8 == 3 and s > 8:
                        t = s // 8 - 1
                        dve.wait_ge(A["ohi"], 4 + t + 1)
                        dve.tensor_tensor(tile(hlo, 4 + t), ps[:, 4 + t % 2, :], tile(hhi, 4 + t).bitcast(f32),
                                          ALU.subtract).then_inc(A["olo"], 1)

            def mix_b():
                dve.wait_ge(evac["in_b"], COUNT["in_b"])
                dve.tensor_scalar(sq[0:8, 0, :], zb[0:8, 0:S], vec[0:8, VEC["b_f"]:VEC["b_f"] + 1], None, ALU.add
                                  ).then_inc(B["fz"], 1)
                dve.wait_ge(ld_cmp, 16 * 12)
                for kv in range(2):
                    zt = tile(zb, ZKC + kv)
                    for part in (1, 0):
                        out = zt if part == 0 else pTB[:, kv, :]
                        add = cpe[:, 32 * kv + 16 * part:32 * kv + 16 * part + 16]
                        dve.tensor_tensor(out.rearrange("p (n l) -> p n l", l=16),
                                          zt.rearrange("p (n l) -> p n l", l=16),
                                          add.rearrange("p (n l) -> p n l", n=1).broadcast_to([P, 32, 16]),
                                          ALU.add).then_inc(B["pe"], 1)
                dve.wait_ge(B["gx"], 1)
                dve.tensor_scalar(gates[:, :], gates[:, :], 1.0, None, ALU.add).then_inc(B["g1"], 1)
                dve.wait_ge(B["g1"], 1)
                dve.reciprocal(gates[:, :], gates[:, :]).then_inc(B["gate"], 1)
                dve.wait_ge(B["fln"], 1)
                dve.scalar_tensor_tensor(out=sq[0:8, 0, :], in0=sq[0:8, 0, :], scalar=0.0, in1=sq[0:8, 1, :],
                                         op0=ALU.min, op1=ALU.subtract).then_inc(B["fls"], 1)
                dve.memset(sumsq[0:8, :], 1.0).then_inc(B["fls"], 1)
                dve.wait_ge(B["fls"], 2)
                dve.tensor_tensor_scan(rstd[0:8, :], sumsq[0:8, :], sq[0:8, 0, :], 0.0, ALU.mult, ALU.add
                                       ).then_inc(B["fc"], 1)
                dve.wait_ge(const_b, 1)
                pc4 = pc.rearrange("p (h c) -> p h c", c=P)
                pg = pc.rearrange("p (g n) -> p g n", n=32)
                for h in range(NHEADS):
                    if h % 4 == 0:
                        dve.wait_ge(B["cs"], h // 4 + 1)
                    dve.scalar_tensor_tensor(out=pc4[:, h, :], in0=distC[:, :], scalar=-8 * SLOPE[h],
                                             in1=ps[:, 4 + h // 4, (h % 4) * P:(h % 4) * P + P],
                                             op0=ALU.mult, op1=ALU.add).then_inc(B["cb"], 1)
                dve.wait_ge(B["cb"], NHEADS)
                dve.tensor_reduce(cst[:, 0:32], pg, AX.X, ALU.max).then_inc(B["cm"], 1)
                dve.wait_ge(B["cm"], 1)
                for k in range(2):
                    dve.tensor_tensor(pg[:, 16 * k:16 * k + 16, :], pg[:, 16 * k:16 * k + 16, :],
                                      cst[:, 16 * k:16 * k + 16].rearrange("p (g n) -> p g n", n=1)
                                      .broadcast_to([P, 16, 32]), ALU.subtract).then_inc(B["cd"], 1)
                dve.wait_ge(B["ce"], 1)
                dve.tensor_tensor(pc4, pc4, maskC[:, :].rearrange("p (h c) -> p h c", h=1)
                                  .broadcast_to([P, NHEADS, P]), ALU.mult).then_inc(B["ck"], 1)
                dve.wait_ge(B["ck"], 1)
                dve.tensor_reduce(cst[:, 32:64], pg, AX.X, ALU.add).then_inc(B["csum"], 1)
                dve.wait_ge(B["csum"], 1)
                dve.tensor_scalar(cst[:, 32:64], cst[:, 32:64], 1e-30, None, ALU.max).then_inc(B["cf"], 1)
                dve.wait_ge(B["cf"], 1)
                dve.reciprocal(cst[:, 32:64], cst[:, 32:64]).then_inc(B["cf"], 1)
                dve.wait_ge(B["cf"], 2)
                dve.wait_ge(B["gate"], 1)
                gv = gates[:, :].rearrange("p (b c) -> p b c", c=HD)
                for h in range(NHEADS):
                    dve.tensor_tensor(cst[:, 32 + 4 * h:36 + 4 * h], cst[:, 32 + 4 * h:36 + 4 * h],
                                      gv[:, :, 32 + 3 * h:33 + 3 * h].rearrange("p b c -> p (b c)"), ALU.mult
                                      ).then_inc(B["cf"], 1)
                dve.wait_ge(B["cf"], 2 + NHEADS)
                dve.tensor_tensor(pg, pg, cst[:, 32:64].rearrange("p (g n) -> p g n", n=1)
                                  .broadcast_to([P, 32, 32]), ALU.mult).then_inc(B["cp"], 1)
                n = len(ITEMS_B)
                dve.wait_ge(B["bias"], NHEADS)
                dve.wait_ge(B["ct"], NHEADS)
                for s in range(n + 4):
                    if s < n:
                        kind, t, half, b = ITEMS_B[s]
                        w = P * (b + 1)
                        if kind == "fox":
                            h = 2 * t + half
                            dve.wait_ge(B["nc_c"], h + 1)
                            bias = zb[:, ZNC[h] * S:ZNC[h] * S + w]
                        else:
                            bias = biasB[:, t + 4 * half, S - w:S]
                        dve.wait_ge(B["s"], s + 1)
                        if s >= 3:
                            dve.wait_ge(B["t"], s - 2)
                        dve.tensor_tensor_reduce(out=pB[:, s % 3, 0:w], in0=ps[:, s % 2, 0:w], in1=bias,
                                                 scale=-0.125, scalar=3e38, op0=ALU.add, op1=ALU.min,
                                                 accum_out=statB[:, 3 * s:3 * s + 1]).then_inc(B["m"], 1)
                    if 0 <= s - 1 < n:
                        g = s - 1
                        kind, t, half, b = ITEMS_B[g]
                        w, c = P * (b + 1), 3 * g
                        dve.wait_ge(B["p"], g + 1)
                        dve.tensor_scalar(statB[:, c + 2:c + 3], statB[:, c + 1:c + 2], 1e-30, None, ALU.max
                                          ).then_inc(B["den"], 1)
                        dve.wait_ge(B["den"], g + 1)
                        dve.reciprocal(statB[:, c + 2:c + 3], statB[:, c + 2:c + 3]).then_inc(B["r"], 1)
                        dve.wait_ge(B["r"], g + 1)
                        if kind == "fox":
                            dve.tensor_scalar(pB[:, g % 3, 0:w], pB[:, g % 3, 0:w], statB[:, c + 2:c + 3], None,
                                              ALU.mult).then_inc(B["pn"], 1)
                        else:
                            gc = HD * b + 32 + 3 * (t + 4 * half) + (1 if kind == "slc" else 2)
                            dve.tensor_scalar(pB[:, g % 3, 0:w], pB[:, g % 3, 0:w], statB[:, c + 2:c + 3],
                                              gates[:, gc:gc + 1], ALU.mult, ALU.mult).then_inc(B["pn"], 1)
                    for j, (row, end) in enumerate(GROUPS_B):
                        if s == end + 3:
                            dve.wait_ge(B["ohi"], j + 1)
                            dve.tensor_tensor(tile(hlo, row), ps[:, 4 + j % 2, :], tile(hhi, row).bitcast(f32),
                                              ALU.subtract).then_inc(B["olo"], 1)

            def pooling():
                count = [0]

                def link(ins):
                    count[0] += 1
                    ins.then_inc(B["pool_w"], 1)
                    dve.wait_ge(B["pool_w"], count[0])

                for g in range(4):
                    w = 2 << g
                    link(dve.memset(invc[:, g, :], 1.0 / w))
                    for c in range(w - 1):
                        link(dve.memset(invc[:, g, c:c + 1], 1.0 / (c + 1)))
                link(dve.memset(win[:, :, 0:16], 0.0))
                for m in range(KD):
                    g = m // 2
                    dve.wait_ge(B["pool_u"], m + 1)
                    link(dve.tensor_copy(win[:, 0, 16:16 + S], tile(pu, m)))
                    for k in range(g + 1):
                        a, c, sh = k % 2, (k + 1) % 2, 1 << k
                        link(dve.tensor_tensor(win[:, c, 16:16 + S], win[:, a, 16:16 + S],
                                               win[:, a, 16 - sh:16 - sh + S], ALU.add))
                    c = (g + 1) % 2
                    link(dve.tensor_tensor(win[:, c, 16:16 + S], win[:, c, 16:16 + S], invc[:, g, :], ALU.mult))
                    if m >= 2:
                        dve.wait_ge(B["pool_hi"], m - 1)
                        dve.wait_ge(B["pool_lo"], m - 1)
                    dve.tensor_tensor(hf[:, m % 2, :], win[:, c, 16:16 + S], tile(pu, m), ALU.subtract
                                      ).then_inc(B["pool_m"], 1)
                    dve.wait_ge(B["pool_hi"], m + 1)
                    dve.tensor_tensor(tile(hlo, m), hf[:, m % 2, :], tile(hhi, m).bitcast(f32), ALU.subtract
                                      ).then_inc(B["pool_lo"], 1)

            for n in range(2):
                split_lo(n, 0, split_cols(n))
            for kind, what in flow:
                if kind == "norm":
                    norm(what)
                elif kind == "gemm":
                    gemm(what)
                elif kind == "post":
                    post(what)
                elif kind == "mix_a":
                    mix_a()
                elif kind == "mix_b":
                    mix_b()
                elif kind == "pooling":
                    pooling()

        @block.tensor
        def _(pe_):
            def three(out, slot, j, hi, lo, start, stop):
                wh, wl = whi[slot][:, j * P:j * P + P], wlo[slot][:, j * P:j * P + P]
                pe_.matmul(out, wh, hi, start=start, stop=False)
                pe_.matmul(out, wh, lo, start=False, stop=False)
                return pe_.matmul(out, wl, hi, start=False, stop=stop)

            def operand_ready(p, u, k):
                if p in ("in_a", "up_a", "in_b", "up_b0", "up_b1"):
                    pe_.wait_ge(h_lo, 8 * ["in_a", "up_a", "in_b", "up_b0", "up_b1"].index(p) + k + 1)
                elif p == "out_a":
                    pe_.wait_ge(A["olo"], k + 1)
                elif p == "out_b":
                    pe_.wait_ge(B["olo"], 8)

            def gemm(p):
                n0 = FIRST[p]
                up = {"down_a": "up_a", "down_b0": "up_b0", "down_b1": "up_b1"}.get(p)

                def step(u, i):
                    n = n0 + u
                    slot = n % SPL
                    pe_.wait_ge(lo_done, n + 1 + 4 * i)
                    if p == "pool":
                        for j in range(4):
                            m = 4 * u + j
                            pe_.wait_ge(B["pool_lo"], 2 * (m // 2) + 2)
                            if u:
                                pe_.wait_ge(evac[p], j + 1)
                            for k in range(2):
                                r = 2 * (m // 2) + k
                                last = three(ps[:, j, :], slot, 2 * j + k, tile(hhi, r), tile(hlo, r), k == 0, k == 1)
                        last.then_inc(unit_done, 1)
                        return
                    if up:
                        m, half = u // 2, u % 2
                        bank = m % 2
                        if u == 0:
                            pe_.wait_ge(hid["alo"], pair_base[up] + KF - 1)
                        if u == 1:
                            pe_.wait_ge(hid["alo"], pair_base[up] + KF)
                        if half == 0 and m >= 2:
                            pe_.wait_ge(evac[p], m - 1 + 2 * i)
                        for j in range(KH):
                            r = half * KH + j
                            last = three(ps[:, bank, :], slot, j, tile(ahi, r), tile(alo, r),
                                         half == 0 and j == 0, half == 1 and j == KH - 1)
                        last.then_inc(unit_done, 1)
                        return
                    if u >= 4:
                        if p == "up_a":
                            pe_.wait_ge(hid["tap0"], u - 3 + 4 * i)
                        elif p[:2] == "up":
                            pe_.wait_ge(hid["prod"], pair_base[p] + (u - 4) // 2 + 1 + 2 * i)
                        else:
                            pe_.wait_ge(evac[p], u - 3 + 4 * i)
                    for j in range(KD):
                        if u == 0:
                            operand_ready(p, u, j)
                        last = three(ps[:, u % 4, :], slot, j, tile(hhi, j), tile(hlo, j), j == 0, j == KD - 1)
                    last.then_inc(unit_done, 1)

                units(pe_, 0, COUNT[p], peel_of(p), step)

            def statistics(e):
                if e in STREAMED:
                    pe_.wait_ge(sq_used, sq_base[STREAMED[e]] + KD)
                    pe_.matmul(ps[:, BANK_MS, :], ones[:, :], sumsq[:, :], start=True, stop=True).then_inc(ms_ready, 1)
                    return
                base = 8 * BOUNDARY.index(e)
                if e == 0:
                    pe_.wait_ge(const_0, 1)
                for m in range(KD):
                    pe_.wait_ge(bsq_ready, base + m + 1)
                    last = pe_.matmul(ps[:, BANK_MS, :], ones[:, :], sq[:, m % 2, :], start=m == 0, stop=m == KD - 1)
                    if m < KD - 1:
                        last.then_inc(bsq_used, 1)
                last.then_inc(ms_ready, 1)

            def mix_a():
                pe_.wait_ge(evac["in_a"], COUNT["in_a"])
                pe_.wait_ge(ld_vec, 64)
                for t in range(2):
                    pe_.matmul(ps[:, t, :], wal[:, t * P:t * P + P], za[0:16, 0:S], start=True, stop=True
                               ).then_inc(A["logit"], 1)
                for h in range(4):
                    for b in range(NB):
                        last = pe_.transpose(ps[:, 4 + h, b * P:b * P + P],
                                             za[:, (5 + h) * S + b * P:(5 + h) * S + b * P + P], ident[:, :])
                    last.then_inc(A["gvT"], 1)
                for b in range(NB):
                    last = pe_.transpose(ps[:, 2, b * P:b * P + P], za[:, 18 * S + b * P:18 * S + b * P + P], ident[:, :])
                last.then_inc(A["svT"], 1)
                pe_.wait_ge(const_a, 1)
                pe_.wait_ge(A["gvT_c"], 4)
                for j in range(5):
                    pe_.wait_ge(A["nsq"], j + 1)
                    if j >= 2:
                        pe_.wait_ge(A["nln"], j - 1)
                    pe_.matmul(ps[:, 4 + j % 2, :], blk64[:, :], sq[:, j % 2, :], start=True, stop=True
                               ).then_inc(A["nms"], 1)
                pe_.wait_ge(A["kd"], 1)
                for t in range(2):
                    for b in range(NB):
                        last = pe_.transpose(ps[:, t, b * P:b * P + P], kd[:, t * S + b * P:t * S + b * P + P], ident[:, :])
                    last.then_inc(A["kdT"], 1)
                pe_.wait_ge(A["qke"], 2)
                pe_.wait_ge(A["svT_c"], 1)
                for h in range(4):
                    t, rows = h // 2, slice(HD * (h % 2), HD * (h % 2) + HD)
                    if h >= 2:
                        pe_.wait_ge(A["masked"], h - 1)
                    for b in range(NB):
                        c = t * S + b * P
                        last = pe_.matmul(ps[:, 2 + h % 2, b * P:b * P + P], za[rows, S + c:S + c + P],
                                          za[rows, 3 * S + c:3 * S + c + P], start=True, stop=True)
                    last.then_inc(A["score"], 1)
                pe_.wait_ge(A["kdT_c"], 2)
                pe_.wait_ge(A["nln"], 5)
                for t in range(2):
                    for n in range(NCH - 1):
                        rows = slice(CHUNK * (n % 2), CHUNK * (n % 2) + CHUNK)
                        for half in range(2):
                            h = 2 * t + half
                            c = t * S + (n // 2) * P + half * HD
                            v = h * S + (n // 2) * P
                            last = pe_.matmul(ps[HD * half:HD * half + HD, 4 + 2 * t + n % 2, (n // 2) * P:(n // 2) * P + P],
                                              kdT[rows, c:c + HD], gvT[rows, v:v + P], start=True, stop=True)
                    last.then_inc(A["cs"], 1)
                pe_.wait_ge(A["st"], 1 + 2 * (NCH - 1))
                pe_.wait_ge(A["masked"], 4)
                for h in range(4):
                    t, rows = h // 2, slice(HD * (h % 2), HD * (h % 2) + HD)
                    for b in range(NB):
                        pe_.matmul(ps[:, h, b * P:b * P + P], tile(gvT, h)[:, b * P:b * P + P],
                                   tile(aT, h)[:, b * P:b * P + P], start=True, stop=False)
                        for n in (2 * b, 2 * b + 1):
                            c = t * S + n * CHUNK
                            last = pe_.matmul(ps[:, h, n * CHUNK:n * CHUNK + CHUNK], state[rows, t, n, :],
                                              za[rows, 3 * S + c:3 * S + c + CHUNK], start=False, stop=n % 2 == 1)
                    last.then_inc(A["o"], 1)
                for h in range(4):
                    pe_.wait_ge(A["osq"], h + 1)
                    if h >= 2:
                        pe_.wait_ge(A["oln"], h - 1)
                    pe_.matmul(ps[:, 4 + h % 2, :], ones[:, :], sq[:, h % 2, :], start=True, stop=True
                               ).then_inc(A["oms"], 1)
                pe_.wait_ge(A["nq"], 5)
                pe_.wait_ge(A["olo"], 4)
                for s in range(len(ITEMS_A) + 4):
                    if s < len(ITEMS_A):
                        t, half, b = ITEMS_A[s]
                        rows = slice(HD * half, HD * half + HD)
                        k0 = max(b - 1, 0) * P
                        w = P * min(b + 1, 2)
                        if s >= 2:
                            pe_.wait_ge(A["m"], s - 1)
                        q = (13 + t) * S + b * P
                        pe_.matmul(ps[:, s % 2, 0:w], za[rows, q:q + P], za[rows, 17 * S + k0:17 * S + k0 + w],
                                   start=True, stop=True).then_inc(A["s"], 1)
                    if 0 <= s - 2 < len(ITEMS_A):
                        g = s - 2
                        nk = min(ITEMS_A[g][2] + 1, 2)
                        pe_.wait_ge(A["pn"], g + 1)
                        if g >= 2:
                            pe_.wait_ge(A["tc"], g - 1)
                        for k in range(nk):
                            last = pe_.transpose(ps[:, 2 + g % 2, k * P:k * P + P], pA[:, g % 3, k * P:k * P + P],
                                                 ident[:, :])
                        last.then_inc(A["t"], 1)
                    if 0 <= s - 3 < len(ITEMS_A):
                        g = s - 3
                        t, half, b = ITEMS_A[g]
                        nk = min(b + 1, 2)
                        pe_.wait_ge(A["tc"], g + 1)
                        if g % 8 == 0 and t >= 2:
                            pe_.wait_ge(A["olo"], 4 + t - 1)
                        for k in range(nk):
                            v = (b + 1 - nk + k) * P + HD * half
                            last = pe_.matmul(ps[HD * half:HD * half + HD, 4 + t % 2, b * P:b * P + P],
                                              svT[:, v:v + HD], pTA[:, g % 2, k * P:k * P + P],
                                              start=k == 0, stop=k == nk - 1)
                        last.then_inc(A["pv"], 1)

            def mix_b():
                pe_.wait_ge(evac["in_b"], COUNT["in_b"])
                for j in range(6):
                    if j >= 4:
                        pe_.wait_ge(B["vt_c"], j - 3)
                    for b in range(NB):
                        c = ZV[j] * S + b * P
                        last = pe_.transpose(ps[:, j % 4, b * P:b * P + P], zb[:, c:c + P], ident[:, :])
                    last.then_inc(B["vt"], 1)
                for b in range(NB):
                    last = pe_.transpose(ps[:, 4, b * HD:b * HD + HD], zb[0:HD, b * P:b * P + P], ident[0:HD, 0:HD])
                last.then_inc(B["gt"], 1)
                pe_.wait_ge(B["pe"], 4)
                for kv in range(2):
                    for l in range(32):
                        buf = tile(zb, ZKC + kv) if l < 16 else pTB[:, kv, :]
                        by = buf.rearrange("p (n l) -> p l n", l=16)
                        for g in range(2):
                            rows = slice(HD * g, HD * g + HD)
                            last = pe_.matmul(ps[rows, 5, 32 * kv:32 * kv + NCMP], cw1[rows, kv, l * HD:l * HD + HD],
                                              by[rows, l % 16, l // 16:l // 16 + NCMP], start=l == 0, stop=l == 31)
                    last.then_inc(B["hid"], 1)
                pe_.wait_ge(B["gelu"], 2)
                for g in range(2):
                    rows = slice(HD * g, HD * g + HD)
                    last = pe_.matmul(ps[rows, 6, 0:NCMP], cw2[rows, 0:HD], glu[rows, 0:NCMP], start=True, stop=True)
                last.then_inc(B["kc"], 1)
                pe_.wait_ge(B["vt_c"], 6)
                for g in range(2):
                    rows = slice(HD * g, HD * g + HD)
                    last = pe_.matmul(ps[0:NCMP, 2 + g, 0:HD], glu[rows, 32:32 + NCMP], cw2[rows, HD:2 * HD],
                                      start=True, stop=True)
                last.then_inc(B["kc"], 1)
                pe_.wait_ge(B["fc"], 1)
                pe_.wait_ge(B["kc_c"], 3)
                for h in range(NHEADS):
                    if h >= 4:
                        pe_.wait_ge(B["nc_c"], h - 3)
                    pe_.matmul(ps[:, h % 4, :], ident[0:8, h:h + 1].broadcast_to([8, P]), rstd[0:8, :],
                               start=True, stop=True).then_inc(B["nc"], 1)
                pe_.wait_ge(B["gelu"], 2)
                pe_.wait_ge(B["gx"], 1)
                for h in range(NHEADS):
                    rows = slice(HD * (h // 4), HD * (h // 4) + HD)
                    for b in range(NB):
                        q = (ZQ + h % 4) * S + b * P
                        c = (h % 4) * P + b * 32
                        last = pe_.matmul(ps[:, 4 + h // 4, c:c + 32], zb[rows, q:q + P], kcmp[rows, :],
                                          start=True, stop=True)
                    if h % 4 == 3:
                        last.then_inc(B["cs"], 1)
                pe_.wait_ge(B["cp"], 1)
                for h in range(NHEADS):
                    if h >= 2:
                        pe_.wait_ge(B["ct_c"], h - 1)
                    for b in range(NB):
                        c = h * P + b * 32
                        last = pe_.transpose(ps[0:32, 6 + h % 2, b * P:b * P + P], pc[:, c:c + 32], ident[:, :])
                    last.then_inc(B["ct"], 1)
                n = len(ITEMS_B)
                pe_.wait_ge(B["ct_c"], NHEADS)
                for s in range(n + 4):
                    if s < n:
                        kind, t, half, b = ITEMS_B[s]
                        rows = slice(HD * half, HD * half + HD)
                        q, k = {"slc": (ZQ + t, ZKS), "win": (ZQ + t, ZKW), "fox": (ZFQ + t, ZFK + t)}[kind]
                        w = P * (b + 1)
                        if s >= 2:
                            pe_.wait_ge(B["m"], s - 1)
                        last = pe_.matmul(ps[:, s % 2, 0:w], zb[rows, q * S + b * P:q * S + b * P + P],
                                          zb[rows, k * S:k * S + w], start=True, stop=kind != "fox")
                        if kind == "fox":
                            last = pe_.matmul(ps[:, s % 2, b * P:w], identb[:, :], triang[:, :], start=False, stop=True)
                        last.then_inc(B["s"], 1)
                    if 0 <= s - 2 < n:
                        g = s - 2
                        pe_.wait_ge(B["pn"], g + 1)
                        if g >= 2:
                            pe_.wait_ge(B["tc"], g - 1)
                        for k in range(ITEMS_B[g][3] + 1):
                            last = pe_.transpose(ps[:, 2 + g % 2, k * P:k * P + P], pB[:, g % 3, k * P:k * P + P],
                                                 ident[:, :])
                        last.then_inc(B["t"], 1)
                    if 0 <= s - 3 < n:
                        g = s - 3
                        kind, t, half, b = ITEMS_B[g]
                        j = t if kind != "fox" else 4 + t
                        out = ps[HD * half:HD * half + HD, 4 + j % 2, b * P:b * P + P]
                        pe_.wait_ge(B["tc"], g + 1)
                        if j >= 2 and half == 0 and b == 0 and kind != "win":
                            pe_.wait_ge(B["olo"], j - 1)
                        if kind == "slc":
                            c = (t + 4 * half) * S + b * P
                            pe_.matmul(out, vcmp[:, HD * half:HD * half + HD], pTc[:, c:c + P], start=True, stop=False)
                        v = {"slc": 0, "win": 1, "fox": 2 + t}[kind] * S + HD * half
                        for k in range(b + 1):
                            last = pe_.matmul(out, vT[:, v + k * P:v + k * P + HD], pTB[:, g % 2, k * P:k * P + P],
                                              start=kind == "fox" and k == 0, stop=kind != "slc" and k == b)
                        last.then_inc(B["pv"], 1)

            for kind, what in flow:
                if kind in ("norm", "post"):
                    statistics(what)
                elif kind == "gemm":
                    gemm(what)
                elif kind == "mix_a":
                    mix_a()
                elif kind == "mix_b":
                    mix_b()


def _tiles(w, n):
    return np.ascontiguousarray(w.reshape(KD, P, n, P).transpose(2, 1, 0, 3).reshape(n, P, KD * P))


def _pairs(w, axis):
    shape = w.shape
    w = np.moveaxis(w, axis, 0)
    w = w.reshape(2, 4, HD, -1).transpose(1, 0, 2, 3).reshape(w.shape)
    return np.moveaxis(w, 0, axis).reshape(shape)


def _down(w):
    return np.ascontiguousarray(w.reshape(2, KH, P, KD, P).transpose(3, 0, 2, 1, 4).reshape(16, P, KH * P))


def _up(a, b):
    return np.ascontiguousarray(np.stack([_tiles(a, KF), _tiles(b, KF)], 1).reshape(2 * KF, P, KD * P))


def _cols(v):
    return v.reshape(-1, P).T


def arrays_of(i):
    f = np.float32
    w = i["w_in"][0]
    c = np.cumsum([0, 256, 256, 512, 512, 16, 512, 128, 128])
    gq, gk, gv, gr, glr, sq, sk, sv = [w[:, c[k]:c[k + 1]] for k in range(8)]
    lr = np.zeros((D, P), f)
    lr[:, 0:16] = glr
    in_a = np.concatenate([lr, gk, gq, gv, gr, _pairs(sq, 1), sk, sv], 1)
    wo = i["w_out"][0]
    out_a = np.concatenate([wo[0:512], _pairs(wo[512:1024], 0)], 0)
    w = i["attn_w_in_2"][0]
    c = np.cumsum([0, 512, 512, 512, 8, 512, 128, 128, 128, 128, 128, 128, 24])
    fq, fk, fv, ff, nq, kc, vc, ks, vs, kw, vw, ng = [w[:, c[k]:c[k + 1]] for k in range(12)]
    gt = np.zeros((D, P), f)
    gt[:, 0:8] = ff
    gt[:, 32:56] = ng
    in_b = np.concatenate([gt, _pairs(nq, 1), kc, vc, ks, vs, kw, vw, fq, fk, fv], 1)
    wo = i["attn_w_out_2"][0]
    out_b = np.concatenate([wo[0:512], _pairs(wo[512:1024], 0)], 0)
    pw = i["pool_w_2"][0].reshape(2, 2, 2, P, 2, P).transpose(0, 3, 1, 4, 2, 5)
    weights = {
        "in_a": _tiles(in_a, 19), "out_a": _tiles(out_a, 8),
        "up_a": _up(i["w_up"][0][:, 0:FF], i["w_up"][0][:, FF:]), "down_a": _down(i["w_down"][0]),
        "in_b": _tiles(in_b, 23), "out_b": _tiles(out_b, 8),
        "up_b0": _up(i["ffn_w_gate_2"][0], i["ffn_w_up_2"][0]), "down_b0": _down(i["ffn_w_down_2"][0]),
        "pool": np.ascontiguousarray(pw.reshape(2, P, 8 * P)),
        "up_b1": _up(i["ffn_w_gate_2"][1], i["ffn_w_up_2"][1]), "down_b1": _down(i["ffn_w_down_2"][1]),
    }
    v = {"mix_norm": i["mix_norm"], "ffn_norm": i["ffn_norm"], "pool_scale": i["pool_scale_2"],
         "b_alpha": i["b_alpha"], "gla_norm": i["gla_norm"],
         "q_norm": np.concatenate([i["q_norm"][0], i["q_norm"][0]]),
         "k_norm": np.concatenate([i["k_norm"][0], i["k_norm"][0]]),
         "b_f": np.concatenate([i["fox_b_f_2"][0], np.zeros(P - 8, f)])}
    for layer in range(2):
        for k in range(4):
            v[f"g{layer}{k}"] = i["norm_g_2"][layer, k]
    vecs = np.concatenate([_cols(v[name]) for name in VEC], 1)
    conv = np.concatenate([_cols(i["conv_w"][0, k]) for k in range(3)] + [_cols(i["conv_b"][0])], 1)
    x = i["x"][0].T.reshape(KD, P, S).transpose(1, 0, 2).reshape(P, KD * S)
    out = {"xT": x, "vecs": vecs, "conv": conv, "sinks": np.broadcast_to(i["sinks"][0], (P, NHEADS)),
           "w_alpha2": i["w_alpha2"][0],
           "pe": i["nsa_cmp_pe_2"][0].transpose(0, 2, 1),
           "cmp_w1": i["nsa_cmp_w1_2"][0].reshape(2, 32, HD, HD).transpose(0, 2, 1, 3).reshape(2, HD, 32 * HD),
           "cmp_w2": i["nsa_cmp_w2_2"][0]}
    out = {k: np.ascontiguousarray(a) for k, a in out.items()}
    for p in ORDER:
        out["w_" + p] = weights[p]
    return out


def program(nc, arrays, flow=FLOW):
    f32 = mybir.dt.float32
    args = {k: nc.dram_tensor(k, a.shape, f32, kind="ExternalInput").ap() for k, a in arrays.items()}
    y = nc.dram_tensor("yT", (P, KD * S), f32, kind="ExternalOutput").ap()
    weights = {p: args.pop("w_" + p) for p in ORDER}
    build(nc, weights=weights, yT=y, flow=flow, **args)


def kernel(**inputs):
    import concourse.bacc as _bacc
    from concourse.bass_utils import run_bass_kernel_spmd as _run

    arrays = arrays_of({k: np.asarray(a) for k, a in inputs.items()})
    nc = _bacc.Bacc("TRN2", target_bir_lowering=False, num_devices=1)
    program(nc, arrays)
    r = _run(nc, [arrays], core_ids=[0])
    y = np.asarray(r.results[0]["yT"])
    return np.ascontiguousarray(y.reshape(P, KD, S).transpose(2, 1, 0).reshape(1, S, D))
```

```python
import numpy as np
import concourse.bass as bass
from concourse import mybir
from contextlib import ExitStack


P = 128
S = 512
D = 1024
KD = D // P
FF = 2816
KF = FF // P
KH = KF // 2
EPS = 1e-6
HD = 64
CHUNK = 64
NCH = S // CHUNK
NB = S // P
NCMP = 31
BIG = 1e33
NHEADS = 8
SLOPE = [2.0 ** -(h + 1) for h in range(NHEADS)]
RAW, SPL = 4, 2

PHASES = [("in_a", 19, 8), ("out_a", 8, 8), ("up_a", 44, 8), ("down_a", 16, 11),
          ("in_b", 23, 8), ("out_b", 8, 8), ("up_b0", 44, 8), ("down_b0", 16, 11),
          ("pool", 2, 8), ("up_b1", 44, 8), ("down_b1", 16, 11)]
FIRST, COUNT, BLOCKS, ORDER = {}, {}, {}, [p[0] for p in PHASES]
_n = 0
for _name, _c, _b in PHASES:
    FIRST[_name], COUNT[_name], BLOCKS[_name] = _n, _c, _b
    _n += _c

FLOW = [("norm", 0), ("gemm", "in_a"), ("mix_a", 0), ("gemm", "out_a"), ("norm", 1), ("gemm", "up_a"),
        ("gemm", "down_a"), ("norm", 2), ("gemm", "in_b"), ("mix_b", 0), ("gemm", "out_b"), ("post", 3),
        ("norm", 4), ("gemm", "up_b0"), ("gemm", "down_b0"), ("post", 5), ("norm", 6), ("pooling", 0),
        ("gemm", "pool"), ("post", 7), ("norm", 8), ("gemm", "up_b1"), ("gemm", "down_b1"), ("post", 9)]
GAIN = {0: "mix_norm", 1: "ffn_norm", 2: "g00", 3: "g01", 4: "g02", 5: "g03", 6: "g10", 7: "g11",
        8: "g12", 9: "g13"}
STREAMED = {1: "out_a", 2: "down_a", 3: "out_b", 5: "down_b0", 7: "pool", 9: "down_b1"}
BOUNDARY = [0, 4, 6, 8]
APPLIED = [0, 1, 2, 4, 8]
POSTS = [3, 5, 7, 9]
XMODE = ("out_a", "down_a")

VEC = {}
_c = 0
for _name, _w in [("mix_norm", 8), ("ffn_norm", 8), ("g00", 8), ("g01", 8), ("g02", 8), ("g03", 8),
                  ("g10", 8), ("g11", 8), ("g12", 8), ("g13", 8), ("pool_scale", 8), ("b_alpha", 2),
                  ("gla_norm", 1), ("q_norm", 1), ("k_norm", 1), ("b_f", 1)]:
    VEC[_name] = _c
    _c += _w
NVEC = _c


def build(nc, xT, vecs, conv, sinks, w_alpha2, pe, cmp_w1, cmp_w2, weights, yT, flow=FLOW):
    f32, f32r, bf16, i32 = mybir.dt.float32, mybir.dt.float32r, mybir.dt.bfloat16, mybir.dt.int32
    ALU, ACT, AX = mybir.AluOpType, mybir.ActivationFunctionType, mybir.AxisListType
    names = [w for k, w in flow if k == "gemm"]
    n_units = FIRST[names[-1]] + COUNT[names[-1]]
    has_b = "in_b" in names
    ctx = ExitStack()
    with ctx:
        def sb(name, shape, dt=f32, where=ctx):
            return where.enter_context(nc.sbuf_tensor(name, shape, dt))

        def sem(name):
            return ctx.enter_context(nc.semaphore(name))

        raw = [sb(f"raw{i}", [P, KH * P]) for i in range(RAW)]
        whi = [sb(f"whi{i}", [P, KH * P], f32r) for i in range(SPL)]
        wlo = [sb(f"wlo{i}", [P, KH * P], f32r) for i in range(SPL)]
        x = sb("x", [P, KD * S])
        hhi = sb("hhi", [P, KD * S], f32r)
        hlo = sb("hlo", [P, KD * S], f32r)
        rstd = sb("rstd", [P, S])
        sq = sb("sq", [P, 3, S])
        sumsq = sq[:, 2, :]
        hf = sq
        ident = sb("ident", [P, P])
        ones = sb("ones", [P, P])
        vec = sb("vec", [P, NVEC])
        convw = sb("convw", [P, 4 * 2 * KF])
        epsc = sb("epsc", [P, 1])
        invc = sb("invc", [P, 16])
        identb = sb("identb", [P, P], bf16)
        triang = sb("triang", [P, P], bf16)
        ffn = ExitStack()
        ahi = sb("ahi", [P, KF * S], f32r, ffn)
        alo = sb("alo", [P, KF * S], f32r, ffn)
        tmp = ExitStack()
        pre = sb("pre", [P, 2, S], f32, tmp)
        cvt = sb("cvt", [P, 2, S], f32, tmp)
        sil = sb("sil", [P, S], f32, tmp)
        gated = sb("gated", [P, S], f32, tmp)
        tmp.close()
        mt = sb("mt", [P, KD * S], f32, ffn)
        ffn.close()
        ma = ExitStack()
        za = sb("za", [P, 19 * S], f32, ma)
        la = sb("la", [P, 2 * S], f32, ma)
        cum = sb("cum", [P, 2 * S], f32, ma)
        eb = sb("eb", [P, 2 * S], f32, ma)
        kd = sb("kd", [P, 2 * S], f32, ma)
        segm = sb("segm", [P, S], f32, ma)
        kdT = sb("kdT", [P, 2 * S], f32, ma)
        gvT = sb("gvT", [P, 4 * S], f32, ma)
        aT = sb("aT", [P, 4 * S], f32, ma)
        svT = sb("svT", [P, S], f32, ma)
        state = sb("state", [P, 2, NCH, P], f32, ma)
        blk64 = sb("blk64", [P, P], f32, ma)
        cmask = sb("cmask", [P, P], f32, ma)
        biasA = sb("biasA", [P, NHEADS, 2 * P], f32, ma)
        distA = sb("distA", [P, 2 * P], f32, ma)
        sink = sb("sink", [P, NHEADS], f32, ma)
        nsink = sb("nsink", [P, NHEADS], f32, ma)
        wal = sb("wal", [16, 2 * P], f32, ma)
        pA = sb("pA", [P, 3, 2 * P], f32, ma)
        pTA = sb("pTA", [P, 2, 2 * P], f32, ma)
        statA = sb("statA", [P, 4 * 32], f32, ma)
        ma.close()
        mb = ExitStack()
        zb = sb("zb", [P, 23 * S], f32, mb)
        vT = sb("vT", [P, 6 * S], f32, mb)
        biasB = sb("biasB", [P, NHEADS, S], f32, mb)
        w1m = ExitStack()
        cw1 = sb("cw1", [P, 2, 32 * HD], f32, w1m)
        w1m.close()
        pTc = sb("pTc", [32, NHEADS * S], f32, mb)
        pB = sb("pB", [P, 3, S], f32, mb)
        pTB = sb("pTB", [P, 2, S], f32, mb)
        pc = pB[:, 0:2, :].rearrange("p a s -> p (a s)")
        statB = sb("statB", [P, 3 * 96], f32, mb)
        kcmp = sb("kcmp", [P, 32], f32, mb)
        vcmp = sb("vcmp", [32, P], f32, mb)
        cw2 = sb("cw2", [P, 2 * HD], f32, mb)
        cpe = sb("cpe", [P, 2 * 32], f32, mb)
        glu = sb("glu", [P, 2 * 32], f32, mb)
        cst = sb("cst", [P, 2 * 32], f32, mb)
        gates = sb("gates", [P, NB * HD], f32, mb)
        distC = sb("distC", [P, P], f32, mb)
        maskC = sb("maskC", [P, P], f32, mb)
        mb.close()
        mp = ExitStack()
        pu = sb("pu", [P, KD, 16 + S], f32, mp)
        win = sb("win", [P, 2, 2, 16 + S], f32, mp)
        pooled = sb("pooled", [P, 2, 2, S], f32, mp)
        mp.close()

        ps = ctx.enter_context(nc.psum_tensor("ps", [P, 8, S], f32))

        raw_ready = [sem(f"raw_ready{i}") for i in range(RAW)]
        hi_done, lo_done, unit_done = sem("hi_done"), sem("lo_done"), sem("unit_done")
        evac = {p: sem(f"evac_{p}") for p in names}
        sq_ready, sq_used = sem("sq_ready"), sem("sq_used")
        sq_base = {p: 8 * k for k, p in enumerate(STREAMED.values())}
        zeroed = sem("zeroed")
        hid = {k: sem("hidden_" + k) for k in ("tap2", "tap1", "tap0", "silu", "prod", "ahi", "alo")}
        pair_base = {"up_a": 0, "up_b0": KF, "up_b1": 2 * KF}
        ms_ready, rstd_ln, rstd_ready = sem("ms_ready"), sem("rstd_ln"), sem("rstd_ready")
        bsq_ready, bsq_used = sem("bsq_ready"), sem("bsq_used")
        h_hi, h_lo = sem("h_hi"), sem("h_lo")
        post_done, x_done = sem("post_done"), sem("x_done")
        ld_x, ld_vec, ld_cmp = [sem(f"ld_x{m}") for m in range(KD)], sem("ld_vec"), sem("ld_cmp")
        filled, const_0, const_a, const_b = sem("filled"), sem("const_0"), sem("const_a"), sem("const_b")
        stored = sem("stored")
        A = {k: sem("a_" + k) for k in (
                "logit", "logit_b", "abs", "exp", "log1p", "logsig", "decay", "rest", "eb", "enb", "ed",
                "qke", "kd", "kdT", "kdT_c", "gvT", "gvT_c", "svT", "svT_c", "score", "masked", "cs",
                "st", "o", "osq", "oms", "oln", "orstd", "sig", "on", "og", "ohi", "olo", "nsq", "nms",
                "nln", "nrstd", "nq", "sinkn", "bias", "s", "m", "es", "p", "den", "r", "pn", "t", "tc",
                "pv")}
        B = {}
        if has_b:
            B = {k: sem("b_" + k) for k in (
                "vt", "vt_c", "gt", "gx", "g1", "gate", "fz", "fabs", "fexp", "fln", "fls", "fc", "nc",
                "nc_c", "bias", "pe", "hid", "gelu", "kc", "kc_c", "cs", "cb", "cm", "cd", "ce", "ck",
                "csum", "cf", "cp", "ct", "ct_c", "s", "m", "p", "den", "r", "pn", "t", "tc", "pv",
                "ohi", "olo", "pool_z", "pool_u", "pool_w", "pool_m", "pool_m2", "pool_hi", "pool_lo")}

        BANK_MS = 4
        LN_EXP = "natural_log_exp_and_others"
        RSTD_OF = {"in_a": 0, "up_a": 1, "in_b": 2, "up_b0": 4, "up_b1": 8}
        if flow[-1][0] == "post":
            final_sem, final_count = x_done, 8 * (POSTS.index(flow[-1][1]) + 1)
        else:
            final_sem, final_count = evac[names[-1]], 8
        mix_unit = FIRST["in_b"]

        def split_cols(n):
            return next(BLOCKS[p] * P for p in ORDER if FIRST[p] <= n < FIRST[p] + COUNT[p])

        def units(eng, first, last, peel, step):
            for u in range(first, min(peel, last)):
                step(u, 0)
            first = max(first, peel)
            loops = (last - first) // 4
            if loops >= 2:
                with eng.Fori(0, loops) as i:
                    for u in range(first, first + 4):
                        step(u, i)
                first += 4 * loops
            for u in range(first, last):
                step(u, 0)

        def tile(buf, t):
            return buf[:, bass.ds(t * S, S)]

        def col(name, t=0):
            return vec[:, VEC[name] + t:VEC[name] + t + 1]

        def peel_of(p):
            return 8 if p[:4] == "down" else 4

        ITEMS_A = [(t, half, b) for t in range(4) for half in range(2) for b in range(NB)]
        ITEMS_B = [(br, t, half, b) for t in range(4) for half in range(2) for b in range(NB)
                   for br in ("slc", "win")]
        ITEMS_B += [("fox", t, half, b) for t in range(4) for half in range(2) for b in range(NB)]
        ALONE = {}
        ZQ, ZKC, ZVC, ZKS, ZVS, ZKW, ZVW, ZFQ, ZFK, ZFV = 1, 5, 6, 7, 8, 9, 10, 11, 15, 19
        ZV = [ZVS, ZVW, ZFV, ZFV + 1, ZFV + 2, ZFV + 3]
        ZNC = [ZKC, ZVC, ZVS, ZVW, ZFV, ZFV + 1, ZFV + 2, ZFV + 3]
        GROUPS_B = [(4 + t, 16 * (t + 1)) for t in range(4)] + [(t, 64 + 8 * (t + 1)) for t in range(4)]

        block = ctx.enter_context(nc.Block())

        @block.sync
        def _(sp):
            for m in range(KD):
                sp.dma_start(x[:, m * S:m * S + S], xT[:, m * S:m * S + S]).then_inc(ld_x[m], 16)
            for p in names:
                n0, cols = FIRST[p], BLOCKS[p] * P

                def load(u, i, p=p, n0=n0, cols=cols):
                    n = n0 + u
                    if n >= RAW:
                        sp.wait_ge(lo_done, n - RAW + 1 + 4 * i)
                    sp.dma_start(raw[n % RAW][:, 0:cols],
                                 weights[p][bass.ds(u + 4 * i, 1), :, :].rearrange("a p c -> (a p) c")
                                 ).then_inc(raw_ready[n % RAW], 16)

                units(sp, 0, COUNT[p], 4, load)
            for m in range(KD):
                sp.wait_ge(final_sem, final_count - KD + m + 1)
                sp.dma_start(yT[:, m * S:m * S + S], x[:, m * S:m * S + S]).then_inc(stored, 16)
            sp.wait_ge(stored, 16 * KD)

        @block.gpsimd
        def _(pool):
            pool.dma_start(vec[:, :], vecs).then_inc(ld_vec, 16)
            pool.dma_start(convw[:, :], conv).then_inc(ld_vec, 16)
            pool.dma_start(wal[:, :], w_alpha2).then_inc(ld_vec, 16)
            pool.dma_start(sink[:, :], sinks).then_inc(ld_vec, 16)
            n_filled = [0]

            def fill(ins):
                n_filled[0] += 1
                ins.then_inc(filled, 1)
                pool.wait_ge(filled, n_filled[0])

            def select(out, pattern, base, chan, op, value):
                return pool.affine_select(out=out, in_=out, compare_op=op, fill=value, base=base,
                                          pattern=pattern, channel_multiplier=chan)

            fill(pool.memset(ones[:, :], 1.0 / D))
            fill(pool.memset(epsc[:, :], EPS))
            for c in range(16):
                fill(pool.memset(invc[:, c:c + 1], 1.0 / (c + 1)))
            fill(pool.memset(ident[:, :], 0.0))
            select(ident[:, :], [[-1, P]], 0, 1, ALU.not_equal, 1.0).then_inc(const_0, 1)
            fill(pool.memset(identb[:, :], 0.0))
            fill(select(identb[:, :], [[-1, P]], 0, 1, ALU.not_equal, 1.0))
            fill(pool.memset(triang[:, :], 0.0))
            fill(select(triang[:, :], [[-1, P]], 0, 1, ALU.is_ge, -1e32))
            fill(pool.memset(segm[:, :], 1.0))
            fill(pool.memset(segm[:, :].rearrange("p (n c) -> p n c", c=CHUNK)[:, :, 0:1], 0.0))
            fill(pool.memset(cmask[:, :], 1.0))
            fill(select(cmask[:, :], [[1, P]], 0, -1, ALU.is_ge, 0.0))
            fill(select(cmask[:, CHUNK:P], [[0, P - CHUNK]], -CHUNK, 1, ALU.is_ge, 0.0))
            fill(pool.memset(blk64[:, :], 1.0 / HD))
            fill(select(blk64[:, 0:HD], [[0, HD]], HD - 1, -1, ALU.is_ge, 0.0))
            fill(select(blk64[:, HD:P], [[0, HD]], -HD, 1, ALU.is_ge, 0.0))
            fill(pool.iota(distA[:, :], [[-1, 2 * P]], P, 1, allow_small_or_imprecise_dtypes=True))
            fill(select(distA[:, :], [[-1, 2 * P]], P, 1, ALU.is_ge, BIG))
            select(distA[:, :], [[1, 2 * P]], -1, -1, ALU.is_ge, BIG).then_inc(const_a, 1)
            if has_b:
                pool.wait_ge(unit_done, mix_unit + 1)
                for half in range(2):
                    rows = slice(HD * half, HD * half + HD)
                    for kv in range(2):
                        pool.dma_start(cw1[rows, kv, :], cmp_w1[kv]).then_inc(ld_cmp, 16)
                        pool.dma_start(cw2[rows, kv * HD:kv * HD + HD], cmp_w2[kv]).then_inc(ld_cmp, 16)
                        pool.dma_start(cpe[rows, kv * 32:kv * 32 + 32], pe[kv]).then_inc(ld_cmp, 16)
                fill(pool.iota(biasB[:, 0, :], [[-1, S]], S - P, 1, allow_small_or_imprecise_dtypes=True))
                fill(select(biasB[:, 0, :], [[-1, S]], S - P, 1, ALU.is_ge, BIG))
                dc = distC[:, :].rearrange("p (b n) -> p b n", n=32)
                mc = maskC[:, :].rearrange("p (b n) -> p b n", n=32)
                pat = [[P, NB], [-16, 32]]
                fill(pool.iota(dc, pat, -31, 1, allow_small_or_imprecise_dtypes=True))
                fill(select(dc, pat, -31, 1, ALU.is_ge, BIG))
                fill(pool.memset(dc[:, :, NCMP:32], BIG))
                fill(pool.memset(maskC[:, :], 1.0))
                fill(select(mc, pat, -31, 1, ALU.is_ge, 0.0))
                fill(pool.memset(mc[:, :, NCMP:32], 0.0))
                fill(pool.memset(kcmp[:, :], 0.0))
                pool.memset(vcmp[:, :], 0.0).then_inc(const_b, 1)
        @block.scalar
        def _(act):
            def split_hi(n, i, cols):
                act.wait_ge(raw_ready[n % RAW], 16 * (n // RAW + 1 + i))
                if n >= SPL:
                    act.wait_ge(unit_done, n - SPL + 1 + 4 * i)
                act.activation(whi[n % SPL][:, 0:cols], raw[n % RAW][:, 0:cols], ACT.Copy).then_inc(hi_done, 1)

            def evacuate(p, u, i):
                n = FIRST[p] + u
                if p[:2] == "up":
                    if u % 2:
                        hidden(p, u, i)
                elif p == "pool":
                    act.wait_ge(B["pool_lo"], 4)
                    for j in range(4):
                        act.wait_ge(unit_done, n + 1)
                        normalized(p, 4 * u + j, 0, j, col("pool_scale", 4 * u + j))
                elif p[:4] == "down":
                    if u % 2:
                        act.wait_ge(unit_done, n + 1 + 4 * i)
                        normalized(p, u // 2, 2 * i, (u // 2) % 2, None)
                elif p[:3] == "out":
                    act.wait_ge(unit_done, n + 1)
                    normalized(p, u, 0, u % 4, None)

            def normalized(p, m, i, bank, scale):
                src = x
                if p not in XMODE:
                    act.activation(tile(mt, m + i), ps[:, bank, :], ACT.Copy,
                                   scale=1.0 if scale is None else scale).then_inc(evac[p], 1)
                    src = mt
                act.wait_ge(evac[p], m + 1 + i)
                if m >= 2:
                    act.wait_ge(sq_used, sq_base[p] + m - 1 + i)
                act.activation(sq[:, m % 2, :], tile(src, m + i), ACT.Square).then_inc(sq_ready, 1)

            def hidden(p, u, i):
                k, f, fi = hid, u // 2, 2 * i
                done = pair_base[p] + f + fi
                if f >= 1 or p != "up_a":
                    act.wait_ge(k["prod"], done)
                if p == "up_a":
                    for s in range(2):
                        c = f + s * KF
                        act.wait_ge(evac[p], u + s + 4 * i)
                        act.activation(cvt[:, s, :], pre[:, s, :], ACT.Identity,
                                       bias=convw[:, bass.ds(3 * 2 * KF + c + fi, 1)],
                                       scale=convw[:, bass.ds(2 * 2 * KF + c + fi, 1)]).then_inc(k["tap2"], 1)
                    act.wait_ge(k["tap0"], 2 * f + 1 + 2 * fi)
                    act.activation(sil[:, :], cvt[:, 0, :], ACT.Silu).then_inc(k["silu"], 1)
                else:
                    act.wait_ge(evac[p], u + 4 * i)
                    act.activation(sil[:, :], pre[:, 0, :], ACT.Silu).then_inc(k["silu"], 1)
                act.wait_ge(k["prod"], done + 1)
                act.activation(tile(ahi, f + fi), gated[:, :], ACT.Copy).then_inc(k["ahi"], 1)

            def gemm(p):
                n0, count = FIRST[p], ALONE.get(p, COUNT[p])
                if p[:2] == "up":
                    act.preload_act_table(ACT.Silu)
                if p[:4] == "down":
                    act.preload_act_table_set(LN_EXP)

                def step(u, i):
                    split_hi(n0 + u, i, BLOCKS[p] * P)
                    evacuate(p, u - 2, i)

                units(act, 2, count, count if p[:4] == "down" else peel_of(p), step)
                for k in range(2):
                    n = n0 + count + k
                    if n < n_units:
                        split_hi(n, 0, split_cols(n))
                    evacuate(p, count - 2 + k, 0)

            def beside(p, u):
                n = FIRST[p] + u + 2
                if n < n_units:
                    split_hi(n, 0, split_cols(n))

            def statistics(e):
                act.wait_ge(ms_ready, e + 1)
                act.activation(rstd[:, :], ps[:, BANK_MS, :], ACT.Ln, bias=epsc[:, :]).then_inc(rstd_ln, 1)
                act.wait_ge(rstd_ln, e + 1)
                act.activation(rstd[:, :], rstd[:, :], ACT.Exp, scale=-0.5).then_inc(rstd_ready, 1)

            def norm(e):
                for m in range(KD):
                    if e == 0:
                        act.wait_ge(ld_x[m], 16)
                    elif e in BOUNDARY:
                        act.wait_ge(x_done, 8 * POSTS.index(e - 1) + m + 1)
                    if e in BOUNDARY:
                        if m >= 2:
                            act.wait_ge(bsq_used, 7 * BOUNDARY.index(e) + m - 1)
                        act.activation(sq[:, m % 2, :], tile(x, m), ACT.Square).then_inc(bsq_ready, 1)
                    if e in APPLIED:
                        if m == 0 and e == 0:
                            act.wait_ge(ld_vec, 64)
                        act.activation(tile(hhi, m), tile(x, m), ACT.Copy, scale=col(GAIN[e], m)).then_inc(h_hi, 1)
                statistics(e)

            def mix_a():
                act.preload_act_table_set(LN_EXP)
                act.wait_ge(evac["in_a"], COUNT["in_a"])
                act.wait_ge(A["logit_b"], 2)
                act.activation(eb[:, :], la[:, :], ACT.Abs).then_inc(A["abs"], 1)
                act.wait_ge(A["abs"], 1)
                act.activation(eb[:, :], eb[:, :], ACT.Exp, scale=-1.0).then_inc(A["exp"], 1)
                act.wait_ge(A["exp"], 1)
                act.activation(eb[:, :], eb[:, :], ACT.Ln, bias=1.0).then_inc(A["log1p"], 1)
                for h in range(4):
                    act.wait_ge(A["gvT"], h + 1)
                    act.activation(tile(gvT, h), ps[:, 4 + h, :], ACT.Copy).then_inc(A["gvT_c"], 1)
                act.wait_ge(A["svT"], 1)
                act.activation(svT[:, :], ps[:, 2, :], ACT.Copy).then_inc(A["svT_c"], 1)
                act.wait_ge(A["decay"], 2)
                act.activation(eb[:, :], cum[:, :], ACT.Exp, scale=1 / 16).then_inc(A["eb"], 1)
                act.activation(la[:, :], cum[:, :], ACT.Exp, scale=-1 / 16).then_inc(A["enb"], 1)
                act.wait_ge(A["rest"], 2)
                act.activation(kd[:, :], kd[:, :], ACT.Exp, scale=1 / 16).then_inc(A["ed"], 1)
                for j in range(5):
                    if j >= 2:
                        act.wait_ge(A["nms"], j - 1)
                    act.activation(sq[:, j % 2, :], tile(za, 13 + j), ACT.Square).then_inc(A["nsq"], 1)
                    act.wait_ge(A["nms"], j + 1)
                    if j >= 1:
                        act.wait_ge(A["nq"], j)
                    act.activation(rstd[:, :], ps[:, 4 + j % 2, :], ACT.Ln, bias=epsc[:, :]).then_inc(A["nln"], 1)
                    act.wait_ge(A["nln"], j + 1)
                    act.activation(rstd[:, :], rstd[:, :], ACT.Exp, scale=-0.5).then_inc(A["nrstd"], 1)
                for t in range(2):
                    act.wait_ge(A["kdT"], t + 1)
                    act.activation(tile(kdT, t), ps[:, t, :], ACT.Copy).then_inc(A["kdT_c"], 1)
                act.wait_ge(const_a, 1)
                for h in range(NHEADS):
                    act.activation(biasA[:, h, :], distA[:, :], ACT.Copy, scale=-8 * SLOPE[h]).then_inc(A["bias"], 1)
                act.activation(za[:, 9 * S:13 * S], za[:, 9 * S:13 * S], ACT.Silu).then_inc(A["sig"], 1)
                for h in range(4):
                    act.wait_ge(A["o"], h + 1)
                    if h >= 2:
                        act.wait_ge(A["oms"], h - 1)
                    act.activation(sq[:, h % 2, :], ps[:, h, :], ACT.Square).then_inc(A["osq"], 1)
                    act.wait_ge(A["oms"], h + 1)
                    if h >= 1:
                        act.wait_ge(A["on"], h)
                    act.activation(rstd[:, :], ps[:, 4 + h % 2, :], ACT.Ln, bias=epsc[:, :],
                                   scale=float(D // P)).then_inc(A["oln"], 1)
                    act.wait_ge(A["oln"], h + 1)
                    act.activation(rstd[:, :], rstd[:, :], ACT.Exp, scale=-0.5).then_inc(A["orstd"], 1)
                    act.wait_ge(A["og"], h + 1)
                    act.activation(tile(hhi, h), tile(aT, h), ACT.Copy).then_inc(A["ohi"], 1)
                for s in range(len(ITEMS_A) + 4):
                    if s < len(ITEMS_A):
                        t, half, b = ITEMS_A[s]
                        w = P * min(b + 1, 2)
                        act.wait_ge(A["m"], s + 1)
                        act.activation(statA[:, 4 * s + 3:4 * s + 4], sink[:, t + 4 * half:t + 4 * half + 1], ACT.Exp,
                                       bias=statA[:, 4 * s:4 * s + 1]).then_inc(A["es"], 1)
                        act.activation(pA[:, s % 3, 0:w], pA[:, s % 3, 0:w], ACT.Exp, scale=-1.0,
                                       bias=statA[:, 4 * s:4 * s + 1],
                                       accum_out=statA[:, 4 * s + 1:4 * s + 2]).then_inc(A["p"], 1)
                    if 0 <= s - 2 < len(ITEMS_A):
                        g = s - 2
                        w = P * min(ITEMS_A[g][2] + 1, 2)
                        act.wait_ge(A["t"], g + 1)
                        if g >= 2:
                            act.wait_ge(A["pv"], g - 1)
                        act.activation(pTA[:, g % 2, 0:w], ps[:, 2 + g % 2, 0:w], ACT.Copy).then_inc(A["tc"], 1)
                    if s % 8 == 3 and s > 8:
                        t = s // 8 - 1
                        act.wait_ge(A["pv"], 8 * (t + 1))
                        act.activation(tile(hhi, 4 + t), ps[:, 4 + t % 2, :], ACT.Copy).then_inc(A["ohi"], 1)

            def mix_b():
                for j in range(6):
                    if j == 0:
                        act.preload_act_table_set(LN_EXP)
                    act.wait_ge(B["vt"], j + 1)
                    act.activation(tile(vT, j), ps[:, j % 4, :], ACT.Copy).then_inc(B["vt_c"], 1)
                act.wait_ge(B["gt"], 1)
                act.activation(gates[:, :], ps[:, 4, 0:NB * HD], ACT.Exp, scale=-1.0).then_inc(B["gx"], 1)
                act.wait_ge(B["fz"], 1)
                act.activation(sq[0:8, 1, :], sq[0:8, 0, :], ACT.Abs).then_inc(B["fabs"], 1)
                act.wait_ge(B["fabs"], 1)
                act.activation(sq[0:8, 1, :], sq[0:8, 1, :], ACT.Exp, scale=-1.0).then_inc(B["fexp"], 1)
                act.wait_ge(B["fexp"], 1)
                act.activation(sq[0:8, 1, :], sq[0:8, 1, :], ACT.Ln, bias=1.0).then_inc(B["fln"], 1)
                act.wait_ge(B["hid"], 2)
                for kv in range(2):
                    act.activation(glu[:, 32 * kv:32 * kv + NCMP], ps[:, 5, 32 * kv:32 * kv + NCMP],
                                   ACT.Gelu_apprx_tanh).then_inc(B["gelu"], 1)
                act.preload_act_table_set(LN_EXP)
                act.wait_ge(const_b, 1)
                act.wait_ge(B["kc"], 2)
                act.activation(kcmp[:, 0:NCMP], ps[:, 6, 0:NCMP], ACT.Copy).then_inc(B["kc_c"], 1)
                for g in range(2):
                    act.activation(vcmp[0:NCMP, HD * g:HD * g + HD], ps[0:NCMP, 2 + g, 0:HD], ACT.Copy
                                   ).then_inc(B["kc_c"], 1)
                for h in [1, 2, 3, 4, 5, 6, 7, 0]:
                    if h == 0:
                        act.wait_ge(B["bias"], 7)
                    act.activation(biasB[:, h, :], biasB[:, 0, :], ACT.Copy, scale=-8 * SLOPE[h]).then_inc(B["bias"], 1)
                for h in range(NHEADS):
                    act.wait_ge(B["nc"], h + 1)
                    act.activation(tile(zb, ZNC[h]), ps[:, h % 4, :], ACT.Copy, scale=-8.0).then_inc(B["nc_c"], 1)
                act.wait_ge(B["cd"], 2)
                act.activation(pc[:, :], pc[:, :], ACT.Exp, scale=0.125).then_inc(B["ce"], 1)
                for h in range(NHEADS):
                    act.wait_ge(B["ct"], h + 1)
                    act.activation(pTc[:, h * S:h * S + S], ps[0:32, 6 + h % 2, :], ACT.Copy).then_inc(B["ct_c"], 1)
                n = len(ITEMS_B)
                for s in range(n + 4):
                    if s < n:
                        w = P * (ITEMS_B[s][3] + 1)
                        act.wait_ge(B["m"], s + 1)
                        act.activation(pB[:, s % 3, 0:w], pB[:, s % 3, 0:w], ACT.Exp, scale=-1.0,
                                       bias=statB[:, 3 * s:3 * s + 1],
                                       accum_out=statB[:, 3 * s + 1:3 * s + 2]).then_inc(B["p"], 1)
                    if 0 <= s - 2 < n:
                        g = s - 2
                        w = P * (ITEMS_B[g][3] + 1)
                        act.wait_ge(B["t"], g + 1)
                        if g >= 2:
                            act.wait_ge(B["pv"], g - 1)
                        act.activation(pTB[:, g % 2, 0:w], ps[:, 2 + g % 2, 0:w], ACT.Copy).then_inc(B["tc"], 1)
                    for j, (row, end) in enumerate(GROUPS_B):
                        if s == end + 3:
                            act.wait_ge(B["pv"], end)
                            act.activation(tile(hhi, row), ps[:, 4 + j % 2, :], ACT.Copy).then_inc(B["ohi"], 1)

            def pooling():
                for g in range(4):
                    act.wait_ge(B["pool_m"], g + 1)
                    act.activation(hhi[:, 2 * g * S:2 * g * S + 2 * S],
                                   pooled[:, g % 2, :, :].rearrange("p a s -> p (a s)"), ACT.Copy
                                   ).then_inc(B["pool_hi"], 1)

            act.preload_act_table_set(LN_EXP)
            act.wait_ge(const_0, 1)
            for kind, what in flow:
                if kind == "norm":
                    if what == 0:
                        for n in range(2):
                            split_hi(n, 0, split_cols(n))
                    norm(what)
                elif kind == "gemm":
                    gemm(what)
                elif kind == "post":
                    statistics(what)
                elif kind == "mix_a":
                    mix_a()
                elif kind == "mix_b":
                    mix_b()
                elif kind == "pooling":
                    pooling()

        @block.vector
        def _(dve):
            def split_lo(n, i, cols):
                dve.wait_ge(hi_done, n + 1 + 4 * i)
                dve.tensor_tensor(wlo[n % SPL][:, 0:cols], raw[n % RAW][:, 0:cols],
                                  whi[n % SPL][:, 0:cols].bitcast(f32), ALU.subtract).then_inc(lo_done, 1)

            def summed(p, m, i):
                dve.wait_ge(sq_ready, sq_base[p] + m + 1 + i)
                if m >= 1:
                    dve.wait_ge(sq_used, sq_base[p] + m + i)
                dve.tensor_tensor(sumsq[:, :], sumsq[:, :], sq[:, m % 2, :], ALU.add).then_inc(sq_used, 1)

            def residual(p, m, i, bank):
                if p in XMODE:
                    dve.tensor_tensor(tile(x, m + i), ps[:, bank, :], tile(x, m + i), ALU.add).then_inc(evac[p], 1)
                summed(p, m, i)

            def evacuate(p, u, i):
                n = FIRST[p] + u
                if p[:2] == "in":
                    z = za if p == "in_a" else zb
                    if u == 0:
                        dve.wait_ge(rstd_ready, RSTD_OF[p] + 1)
                    dve.wait_ge(unit_done, n + 1 + 4 * i)
                    bank = u % 4 if u < ALONE.get(p, COUNT[p]) else 6
                    dve.tensor_tensor(tile(z, u + 4 * i), ps[:, bank, :], rstd[:, :], ALU.mult
                                      ).then_inc(evac[p], 1)
                elif p[:2] == "up":
                    hidden(p, u, i)
                elif p == "pool":
                    for j in range(4):
                        residual(p, 4 * u + j, 0, j)
                elif p[:4] == "down":
                    if u % 2:
                        dve.wait_ge(unit_done, n + 1 + 4 * i)
                        residual(p, u // 2, 2 * i, (u // 2) % 2)
                elif p[:3] == "out":
                    dve.wait_ge(unit_done, n + 1)
                    residual(p, u, 0, u % 4)

            def hidden(p, u, i):
                k, f, fi = hid, u // 2, 2 * i
                done = pair_base[p] + f + fi
                if u == 0:
                    dve.wait_ge(rstd_ready, RSTD_OF[p] + 1)
                if u % 2 == 0 and f >= 1 and p != "up_a":
                    dve.wait_ge(k["silu"], done)
                if p == "up_a" and f >= 1:
                    dve.wait_ge(k["tap2"], u - 1 + 4 * i)
                dve.wait_ge(unit_done, FIRST[p] + u + 1 + 4 * i)
                dve.tensor_tensor(pre[:, u % 2, :], ps[:, u % 4, :], rstd[:, :], ALU.mult).then_inc(evac[p], 1)
                if u % 2 == 0:
                    return
                if p == "up_a":
                    for s in range(2):
                        c = f + s * KF
                        dve.wait_ge(k["tap2"], 2 * f + s + 1 + 2 * fi)
                        dve.scalar_tensor_tensor(out=cvt[:, s, 1:S], in0=pre[:, s, 0:S - 1],
                                                 scalar=convw[:, bass.ds(2 * KF + c + fi, 1)],
                                                 in1=cvt[:, s, 1:S], op0=ALU.mult, op1=ALU.add
                                                 ).then_inc(k["tap1"], 1)
                        dve.wait_ge(k["tap1"], 2 * f + s + 1 + 2 * fi)
                        dve.scalar_tensor_tensor(out=cvt[:, s, 2:S], in0=pre[:, s, 0:S - 2],
                                                 scalar=convw[:, bass.ds(c + fi, 1)],
                                                 in1=cvt[:, s, 2:S], op0=ALU.mult, op1=ALU.add
                                                 ).then_inc(k["tap0"], 1)
                    dve.wait_ge(k["tap0"], 2 * f + 2 + 2 * fi)
                    other = cvt[:, 1, :]
                else:
                    dve.wait_ge(evac[p], u + 1 + 4 * i)
                    other = pre[:, 1, :]
                dve.wait_ge(k["silu"], done + 1)
                if f >= 1 or p != "up_a":
                    dve.wait_ge(k["alo"], done)
                dve.tensor_tensor(gated[:, :], other, sil[:, :], ALU.mult).then_inc(k["prod"], 1)
                dve.wait_ge(k["ahi"], done + 1)
                dve.tensor_tensor(tile(alo, f + fi), gated[:, :], tile(ahi, f + fi).bitcast(f32),
                                  ALU.subtract).then_inc(k["alo"], 1)

            def gemm(p):
                n0, count = FIRST[p], ALONE.get(p, COUNT[p])
                if p in sq_base:
                    e = next(e for e, q in STREAMED.items() if q == p)
                    dve.memset(sumsq[:, :], 0.0).then_inc(zeroed, 1)
                    dve.wait_ge(zeroed, sorted(STREAMED).index(e) + 1)

                def step(u, i):
                    split_lo(n0 + u, i, BLOCKS[p] * P)
                    evacuate(p, u - 2, i)

                units(dve, 2, count, peel_of(p), step)
                for k in range(2):
                    n = n0 + count + k
                    if n < n_units:
                        split_lo(n, 0, split_cols(n))
                    evacuate(p, count - 2 + k, 0)

            def beside(p, u):
                evacuate(p, u, 0)
                n = FIRST[p] + u + 2
                if n < n_units:
                    split_lo(n, 0, split_cols(n))

            def norm(e):
                if e == 6:
                    dve.wait_ge(unit_done, FIRST["down_b0"] + COUNT["down_b0"])
                    dve.memset(pu[:, :, 0:16], 0.0).then_inc(B["pool_z"], 1)
                    dve.memset(win[:, :, :, 0:16], 0.0).then_inc(B["pool_z"], 1)
                    dve.wait_ge(rstd_ready, e + 1)
                    for m in range(KD):
                        dve.scalar_tensor_tensor(out=pu[:, m, 16:16 + S], in0=tile(x, m), scalar=col(GAIN[e], m),
                                                 in1=rstd[:, :], op0=ALU.mult, op1=ALU.mult
                                                 ).then_inc(B["pool_u"], 1)
                    return
                base = 8 * APPLIED.index(e)
                if e == 0:
                    dve.wait_ge(ld_vec, 64)
                for m in range(KD):
                    if e - 1 not in POSTS:
                        lower(e, base, m)

            def lower(e, base, m):
                dve.wait_ge(h_hi, base + m + 1)
                dve.scalar_tensor_tensor(out=tile(hlo, m), in0=tile(x, m), scalar=col(GAIN[e], m),
                                         in1=tile(hhi, m).bitcast(f32), op0=ALU.mult, op1=ALU.subtract
                                         ).then_inc(h_lo, 1)

            def post(e):
                dve.wait_ge(rstd_ready, e + 1)
                base = 8 * POSTS.index(e)
                split = e + 1 in APPLIED
                for m in range(KD + 1):
                    if m < KD:
                        dve.scalar_tensor_tensor(out=tile(mt, m), in0=tile(mt, m), scalar=col(GAIN[e], m),
                                                 in1=rstd[:, :], op0=ALU.mult, op1=ALU.mult).then_inc(post_done, 1)
                    if m >= 1 and split:
                        lower(e + 1, 8 * APPLIED.index(e + 1), m - 1)
                    if m < KD:
                        dve.wait_ge(post_done, base + m + 1)
                        dve.tensor_tensor(tile(x, m), tile(x, m), tile(mt, m), ALU.add).then_inc(x_done, 1)

            def mix_a():
                dve.wait_ge(evac["in_a"], COUNT["in_a"])
                for t in range(2):
                    dve.wait_ge(A["logit"], t + 1)
                    dve.tensor_scalar(tile(la, t), ps[:, t, :], col("b_alpha", t), None, ALU.add
                                      ).then_inc(A["logit_b"], 1)
                dve.wait_ge(A["log1p"], 1)
                dve.wait_ge(A["logit_b"], 2)
                dve.scalar_tensor_tensor(out=la[:, :], in0=la[:, :], scalar=0.0, in1=eb[:, :], op0=ALU.min,
                                         op1=ALU.subtract).then_inc(A["logsig"], 1)
                dve.wait_ge(A["logsig"], 1)
                dve.wait_ge(const_a, 1)
                for t in range(2):
                    dve.tensor_tensor_scan(tile(cum, t), segm[:, :], tile(la, t), 0.0, ALU.mult, ALU.add
                                           ).then_inc(A["decay"], 1)
                dve.wait_ge(A["decay"], 2)
                for t in range(2):
                    cv = tile(cum, t).rearrange("p (n c) -> p n c", c=CHUNK)
                    ev = tile(kd, t).rearrange("p (n c) -> p n c", c=CHUNK)
                    dve.tensor_tensor(ev, cv[:, :, CHUNK - 1:CHUNK].broadcast_to([P, NCH, CHUNK]), cv,
                                      ALU.subtract).then_inc(A["rest"], 1)
                dve.wait_ge(A["eb"], 1)
                dve.scalar_tensor_tensor(out=za[:, 3 * S:5 * S], in0=za[:, 3 * S:5 * S], scalar=HD ** -0.5,
                                         in1=eb[:, :], op0=ALU.mult, op1=ALU.mult).then_inc(A["qke"], 1)
                dve.wait_ge(A["ed"], 1)
                dve.wait_ge(A["enb"], 1)
                dve.tensor_tensor(kd[:, :], za[:, S:3 * S], kd[:, :], ALU.mult).then_inc(A["kd"], 1)
                dve.tensor_tensor(za[:, S:3 * S], za[:, S:3 * S], la[:, :], ALU.mult).then_inc(A["qke"], 1)
                for j in range(5):
                    dve.wait_ge(A["nrstd"], j + 1)
                    dve.scalar_tensor_tensor(out=tile(za, 13 + j), in0=tile(za, 13 + j),
                                             scalar=col("q_norm" if j < 4 else "k_norm"), in1=rstd[:, :],
                                             op0=ALU.mult, op1=ALU.mult).then_inc(A["nq"], 1)
                dve.tensor_scalar(nsink[:, :], sink[:, :], -1.0, None, ALU.mult).then_inc(A["sinkn"], 1)
                for h in range(4):
                    dve.wait_ge(A["score"], h + 1)
                    dve.tensor_tensor(tile(aT, h).rearrange("p (b c) -> p b c", c=P),
                                      ps[:, 2 + h % 2, :].rearrange("p (b c) -> p b c", c=P),
                                      cmask[:, :].rearrange("p (b c) -> p b c", b=1).broadcast_to([P, NB, P]),
                                      ALU.mult).then_inc(A["masked"], 1)
                dve.memset(state[:, :, 0, :], 0.0).then_inc(A["st"], 1)
                for n in range(NCH - 1):
                    for t in range(2):
                        if n == 0:
                            dve.wait_ge(A["cs"], t + 1)
                        dve.wait_ge(A["st"], 1 + (0 if n == 0 else 2 * n - 1 + t))
                        c = t * S + n * CHUNK + CHUNK - 1
                        dve.scalar_tensor_tensor(out=state[:, t, n + 1, :], in0=state[:, t, n, :],
                                                 scalar=eb[:, c:c + 1],
                                                 in1=ps[:, 4 + 2 * t + n % 2, (n // 2) * P:(n // 2) * P + P],
                                                 op0=ALU.mult, op1=ALU.add).then_inc(A["st"], 1)
                dve.wait_ge(A["sig"], 1)
                for h in range(4):
                    dve.wait_ge(A["orstd"], h + 1)
                    dve.scalar_tensor_tensor(out=tile(aT, h), in0=ps[:, h, :], scalar=col("gla_norm"),
                                             in1=rstd[:, :], op0=ALU.mult, op1=ALU.mult).then_inc(A["on"], 1)
                    dve.wait_ge(A["on"], h + 1)
                    dve.tensor_tensor(tile(aT, h), tile(aT, h), tile(za, 9 + h), ALU.mult).then_inc(A["og"], 1)
                    dve.wait_ge(A["ohi"], h + 1)
                    dve.tensor_tensor(tile(hlo, h), tile(aT, h), tile(hhi, h).bitcast(f32), ALU.subtract
                                      ).then_inc(A["olo"], 1)
                dve.wait_ge(A["bias"], NHEADS)
                dve.wait_ge(A["sinkn"], 1)
                for s in range(len(ITEMS_A) + 4):
                    if s < len(ITEMS_A):
                        t, half, b = ITEMS_A[s]
                        h, w = t + 4 * half, P * min(b + 1, 2)
                        dve.wait_ge(A["s"], s + 1)
                        if s >= 3:
                            dve.wait_ge(A["t"], s - 2)
                        dve.tensor_tensor_reduce(out=pA[:, s % 3, 0:w], in0=ps[:, s % 2, 0:w],
                                                 in1=biasA[:, h, 2 * P - w:2 * P], scale=-0.125,
                                                 scalar=nsink[:, h:h + 1], op0=ALU.add, op1=ALU.min,
                                                 accum_out=statA[:, 4 * s:4 * s + 1]).then_inc(A["m"], 1)
                    if 0 <= s - 1 < len(ITEMS_A):
                        g = s - 1
                        w = P * min(ITEMS_A[g][2] + 1, 2)
                        dve.wait_ge(A["p"], g + 1)
                        dve.wait_ge(A["es"], g + 1)
                        c = 4 * g
                        dve.tensor_tensor(statA[:, c + 2:c + 3], statA[:, c + 1:c + 2], statA[:, c + 3:c + 4], ALU.add
                                          ).then_inc(A["den"], 1)
                        dve.wait_ge(A["den"], g + 1)
                        dve.reciprocal(statA[:, c + 2:c + 3], statA[:, c + 2:c + 3]).then_inc(A["r"], 1)
                        dve.wait_ge(A["r"], g + 1)
                        dve.tensor_scalar(pA[:, g % 3, 0:w], pA[:, g % 3, 0:w], statA[:, c + 2:c + 3], None, ALU.mult
                                          ).then_inc(A["pn"], 1)
                    if s % 8 == 3 and s > 8:
                        t = s // 8 - 1
                        dve.wait_ge(A["ohi"], 4 + t + 1)
                        dve.tensor_tensor(tile(hlo, 4 + t), ps[:, 4 + t % 2, :], tile(hhi, 4 + t).bitcast(f32),
                                          ALU.subtract).then_inc(A["olo"], 1)

            def mix_b():
                dve.wait_ge(evac["in_b"], COUNT["in_b"])
                dve.tensor_scalar(sq[0:8, 0, :], zb[0:8, 0:S], vec[0:8, VEC["b_f"]:VEC["b_f"] + 1], None, ALU.add
                                  ).then_inc(B["fz"], 1)
                dve.wait_ge(ld_cmp, 16 * 12)
                for kv in range(2):
                    zt = tile(zb, ZKC + kv)
                    for part in (1, 0):
                        out = zt if part == 0 else pTB[:, kv, :]
                        add = cpe[:, 32 * kv + 16 * part:32 * kv + 16 * part + 16]
                        dve.tensor_tensor(out.rearrange("p (n l) -> p n l", l=16),
                                          zt.rearrange("p (n l) -> p n l", l=16),
                                          add.rearrange("p (n l) -> p n l", n=1).broadcast_to([P, 32, 16]),
                                          ALU.add).then_inc(B["pe"], 1)
                dve.wait_ge(B["gx"], 1)
                dve.tensor_scalar(gates[:, :], gates[:, :], 1.0, None, ALU.add).then_inc(B["g1"], 1)
                dve.wait_ge(B["g1"], 1)
                dve.reciprocal(gates[:, :], gates[:, :]).then_inc(B["gate"], 1)
                dve.wait_ge(B["fln"], 1)
                dve.scalar_tensor_tensor(out=sq[0:8, 0, :], in0=sq[0:8, 0, :], scalar=0.0, in1=sq[0:8, 1, :],
                                         op0=ALU.min, op1=ALU.subtract).then_inc(B["fls"], 1)
                dve.memset(sumsq[0:8, :], 1.0).then_inc(B["fls"], 1)
                dve.wait_ge(B["fls"], 2)
                dve.tensor_tensor_scan(rstd[0:8, :], sumsq[0:8, :], sq[0:8, 0, :], 0.0, ALU.mult, ALU.add
                                       ).then_inc(B["fc"], 1)
                dve.wait_ge(const_b, 1)
                pc4 = pc.rearrange("p (h c) -> p h c", c=P)
                pg = pc.rearrange("p (g n) -> p g n", n=32)
                for h in range(NHEADS):
                    if h % 4 == 0:
                        dve.wait_ge(B["cs"], h // 4 + 1)
                    dve.scalar_tensor_tensor(out=pc4[:, h, :], in0=distC[:, :], scalar=-8 * SLOPE[h],
                                             in1=ps[:, 4 + h // 4, (h % 4) * P:(h % 4) * P + P],
                                             op0=ALU.mult, op1=ALU.add).then_inc(B["cb"], 1)
                dve.wait_ge(B["cb"], NHEADS)
                dve.tensor_reduce(cst[:, 0:32], pg, AX.X, ALU.max).then_inc(B["cm"], 1)
                dve.wait_ge(B["cm"], 1)
                for k in range(2):
                    dve.tensor_tensor(pg[:, 16 * k:16 * k + 16, :], pg[:, 16 * k:16 * k + 16, :],
                                      cst[:, 16 * k:16 * k + 16].rearrange("p (g n) -> p g n", n=1)
                                      .broadcast_to([P, 16, 32]), ALU.subtract).then_inc(B["cd"], 1)
                dve.wait_ge(B["ce"], 1)
                dve.tensor_tensor(pc4, pc4, maskC[:, :].rearrange("p (h c) -> p h c", h=1)
                                  .broadcast_to([P, NHEADS, P]), ALU.mult).then_inc(B["ck"], 1)
                dve.wait_ge(B["ck"], 1)
                dve.tensor_reduce(cst[:, 32:64], pg, AX.X, ALU.add).then_inc(B["csum"], 1)
                dve.wait_ge(B["csum"], 1)
                dve.tensor_scalar(cst[:, 32:64], cst[:, 32:64], 1e-30, None, ALU.max).then_inc(B["cf"], 1)
                dve.wait_ge(B["cf"], 1)
                dve.reciprocal(cst[:, 32:64], cst[:, 32:64]).then_inc(B["cf"], 1)
                dve.wait_ge(B["cf"], 2)
                dve.wait_ge(B["gate"], 1)
                gv = gates[:, :].rearrange("p (b c) -> p b c", c=HD)
                for h in range(NHEADS):
                    dve.tensor_tensor(cst[:, 32 + 4 * h:36 + 4 * h], cst[:, 32 + 4 * h:36 + 4 * h],
                                      gv[:, :, 32 + 3 * h:33 + 3 * h].rearrange("p b c -> p (b c)"), ALU.mult
                                      ).then_inc(B["cf"], 1)
                dve.wait_ge(B["cf"], 2 + NHEADS)
                dve.tensor_tensor(pg, pg, cst[:, 32:64].rearrange("p (g n) -> p g n", n=1)
                                  .broadcast_to([P, 32, 32]), ALU.mult).then_inc(B["cp"], 1)
                n = len(ITEMS_B)
                dve.wait_ge(B["bias"], NHEADS)
                dve.wait_ge(B["ct"], NHEADS)
                for s in range(n + 4):
                    if s < n:
                        kind, t, half, b = ITEMS_B[s]
                        w = P * (b + 1)
                        if kind == "fox":
                            h = 2 * t + half
                            dve.wait_ge(B["nc_c"], h + 1)
                            bias = zb[:, ZNC[h] * S:ZNC[h] * S + w]
                        else:
                            bias = biasB[:, t + 4 * half, S - w:S]
                        dve.wait_ge(B["s"], s + 1)
                        if s >= 3:
                            dve.wait_ge(B["t"], s - 2)
                        dve.tensor_tensor_reduce(out=pB[:, s % 3, 0:w], in0=ps[:, s % 2, 0:w], in1=bias,
                                                 scale=-0.125, scalar=3e38, op0=ALU.add, op1=ALU.min,
                                                 accum_out=statB[:, 3 * s:3 * s + 1]).then_inc(B["m"], 1)
                    if 0 <= s - 1 < n:
                        g = s - 1
                        kind, t, half, b = ITEMS_B[g]
                        w, c = P * (b + 1), 3 * g
                        dve.wait_ge(B["p"], g + 1)
                        dve.tensor_scalar(statB[:, c + 2:c + 3], statB[:, c + 1:c + 2], 1e-30, None, ALU.max
                                          ).then_inc(B["den"], 1)
                        dve.wait_ge(B["den"], g + 1)
                        dve.reciprocal(statB[:, c + 2:c + 3], statB[:, c + 2:c + 3]).then_inc(B["r"], 1)
                        dve.wait_ge(B["r"], g + 1)
                        if kind == "fox":
                            dve.tensor_scalar(pB[:, g % 3, 0:w], pB[:, g % 3, 0:w], statB[:, c + 2:c + 3], None,
                                              ALU.mult).then_inc(B["pn"], 1)
                        else:
                            gc = HD * b + 32 + 3 * (t + 4 * half) + (1 if kind == "slc" else 2)
                            dve.tensor_scalar(pB[:, g % 3, 0:w], pB[:, g % 3, 0:w], statB[:, c + 2:c + 3],
                                              gates[:, gc:gc + 1], ALU.mult, ALU.mult).then_inc(B["pn"], 1)
                    for j, (row, end) in enumerate(GROUPS_B):
                        if s == end + 3:
                            dve.wait_ge(B["ohi"], j + 1)
                            dve.tensor_tensor(tile(hlo, row), ps[:, 4 + j % 2, :], tile(hhi, row).bitcast(f32),
                                              ALU.subtract).then_inc(B["olo"], 1)

            def pooling():
                count = [0]

                def link(ins):
                    count[0] += 1
                    ins.then_inc(B["pool_w"], 1)
                    dve.wait_ge(B["pool_w"], count[0])

                def lower_pooled(g):
                    dve.wait_ge(B["pool_hi"], g + 1)
                    dve.tensor_tensor(hlo[:, 2 * g * S:2 * g * S + 2 * S],
                                      pooled[:, g % 2, :, :].rearrange("p a s -> p (a s)"),
                                      hhi[:, 2 * g * S:2 * g * S + 2 * S].bitcast(f32), ALU.subtract
                                      ).then_inc(B["pool_lo"], 1)

                dve.wait_ge(B["pool_z"], 2)
                for g in range(4):
                    w = 2 << g
                    dve.wait_ge(B["pool_u"], 2 * g + 2)
                    if g:
                        dve.wait_ge(B["pool_m"], g)
                    u = pu[:, 2 * g:2 * g + 2, :]
                    a = u
                    for k in range(g + 1):
                        c, sh = win[:, k % 2, :, :], 1 << k
                        link(dve.tensor_tensor(c[:, :, 16:16 + S], a[:, :, 16:16 + S],
                                               a[:, :, 16 - sh:16 - sh + S], ALU.add))
                        a = c
                    if g >= 2:
                        dve.wait_ge(B["pool_lo"], g - 1)
                    out = pooled[:, g % 2, :, :]
                    dve.scalar_tensor_tensor(out=out[:, :, w - 1:S], in0=a[:, :, 16 + w - 1:16 + S],
                                             scalar=1.0 / w, in1=u[:, :, 16 + w - 1:16 + S],
                                             op0=ALU.mult, op1=ALU.subtract).then_inc(B["pool_m2"], 1)
                    link(dve.tensor_tensor(a[:, :, 16:16 + w - 1], a[:, :, 16:16 + w - 1],
                                           invc[:, 0:w - 1].rearrange("p (a c) -> p a c", a=1)
                                           .broadcast_to([P, 2, w - 1]), ALU.mult))
                    dve.wait_ge(B["pool_m2"], g + 1)
                    dve.tensor_tensor(out[:, :, 0:w - 1], a[:, :, 16:16 + w - 1], u[:, :, 16:16 + w - 1],
                                      ALU.subtract).then_inc(B["pool_m"], 1)
                    if g >= 1:
                        lower_pooled(g - 1)
                lower_pooled(3)

            for kind, what in flow:
                if kind == "norm":
                    if what == 0:
                        for n in range(2):
                            split_lo(n, 0, split_cols(n))
                    norm(what)
                elif kind == "gemm":
                    gemm(what)
                elif kind == "post":
                    post(what)
                elif kind == "mix_a":
                    mix_a()
                elif kind == "mix_b":
                    mix_b()
                elif kind == "pooling":
                    pooling()

        @block.tensor
        def _(pe_):
            def three(out, slot, j, hi, lo, start, stop):
                wh, wl = whi[slot][:, j * P:j * P + P], wlo[slot][:, j * P:j * P + P]
                pe_.matmul(out, wh, hi, start=start, stop=False)
                pe_.matmul(out, wh, lo, start=False, stop=False)
                return pe_.matmul(out, wl, hi, start=False, stop=stop)

            def operand_ready(p, k):
                if p in RSTD_OF:
                    pe_.wait_ge(h_lo, 8 * list(RSTD_OF).index(p) + k + 1)
                else:
                    pe_.wait_ge(A["olo"] if p == "out_a" else B["olo"], k + 1 if p == "out_a" else 8)

            def block_mm(p, u, j, bank, first, last):
                return three(ps[:, bank, :], (FIRST[p] + u) % SPL, j, tile(hhi, j), tile(hlo, j), first, last)

            def beside(p, start, end):
                for g in range(start, end):
                    u, j = ALONE[p] + g // 8, g % 8
                    if j == 0:
                        pe_.wait_ge(lo_done, FIRST[p] + u + 1)
                        if u > ALONE[p]:
                            pe_.wait_ge(evac[p], u)
                    last = block_mm(p, u, j, 6, j == 0, j == 7)
                    if j == 7:
                        last.then_inc(unit_done, 1)

            def gemm(p):
                n0 = FIRST[p]
                up = {"down_a": "up_a", "down_b0": "up_b0", "down_b1": "up_b1"}.get(p)

                def step(u, i):
                    n = n0 + u
                    slot = n % SPL
                    pe_.wait_ge(lo_done, n + 1 + 4 * i)
                    if p == "pool":
                        for j in range(4):
                            m = 4 * u + j
                            pe_.wait_ge(B["pool_lo"], m // 2 + 1)
                            if u:
                                pe_.wait_ge(evac[p], j + 1)
                            for k in range(2):
                                r = 2 * (m // 2) + k
                                last = three(ps[:, j, :], slot, 2 * j + k, tile(hhi, r), tile(hlo, r), k == 0, k == 1)
                        last.then_inc(unit_done, 1)
                        return
                    if up:
                        m, half = u // 2, u % 2
                        bank = m % 2
                        if u == 0:
                            pe_.wait_ge(hid["alo"], pair_base[up] + KF - 1)
                        if u == 1:
                            pe_.wait_ge(hid["alo"], pair_base[up] + KF)
                        if half == 0 and m >= 2:
                            pe_.wait_ge(evac[p], m - 1 + 2 * i)
                        for j in range(KH):
                            r = half * KH + j
                            last = three(ps[:, bank, :], slot, j, tile(ahi, r), tile(alo, r),
                                         half == 0 and j == 0, half == 1 and j == KH - 1)
                        last.then_inc(unit_done, 1)
                        return
                    if u >= 4:
                        pe_.wait_ge(evac[p], u - 3 + 4 * i)
                    e = RSTD_OF.get(p)
                    order = range(KD)
                    for k, j in enumerate(order):
                        if u == 0:
                            operand_ready(p, k)
                        last = block_mm(p, u, j, u % 4, k == 0, k == KD - 1)
                        if u == 0 and e in BOUNDARY:
                            if k == KD - 1:
                                last.then_inc(unit_done, 1)
                            squares(e, k)
                    if u == 0 and e in BOUNDARY:
                        return
                    last.then_inc(unit_done, 1)
                    if u == 0 and e is not None:
                        statistics(e)

                units(pe_, 0, ALONE.get(p, COUNT[p]), peel_of(p), step)

            def statistics(e):
                if e in STREAMED:
                    pe_.wait_ge(sq_used, sq_base[STREAMED[e]] + KD)
                    pe_.matmul(ps[:, BANK_MS, :], ones[:, :], sumsq[:, :], start=True, stop=True).then_inc(ms_ready, 1)
                    return
                for m in range(KD):
                    squares(e, m)

            def squares(e, m):
                if e == 0 and m == 0:
                    pe_.wait_ge(const_0, 1)
                pe_.wait_ge(bsq_ready, 8 * BOUNDARY.index(e) + m + 1)
                last = pe_.matmul(ps[:, BANK_MS, :], ones[:, :], sq[:, m % 2, :], start=m == 0, stop=m == KD - 1)
                last.then_inc(ms_ready if m == KD - 1 else bsq_used, 1)

            def mix_a():
                pe_.wait_ge(evac["in_a"], COUNT["in_a"])
                pe_.wait_ge(ld_vec, 64)
                for t in range(2):
                    pe_.matmul(ps[:, t, :], wal[:, t * P:t * P + P], za[0:16, 0:S], start=True, stop=True
                               ).then_inc(A["logit"], 1)
                for h in range(4):
                    for b in range(NB):
                        last = pe_.transpose(ps[:, 4 + h, b * P:b * P + P],
                                             za[:, (5 + h) * S + b * P:(5 + h) * S + b * P + P], ident[:, :])
                    last.then_inc(A["gvT"], 1)
                for b in range(NB):
                    last = pe_.transpose(ps[:, 2, b * P:b * P + P], za[:, 18 * S + b * P:18 * S + b * P + P], ident[:, :])
                last.then_inc(A["svT"], 1)
                pe_.wait_ge(const_a, 1)
                pe_.wait_ge(A["gvT_c"], 4)
                for j in range(5):
                    pe_.wait_ge(A["nsq"], j + 1)
                    if j >= 2:
                        pe_.wait_ge(A["nln"], j - 1)
                    pe_.matmul(ps[:, 4 + j % 2, :], blk64[:, :], sq[:, j % 2, :], start=True, stop=True
                               ).then_inc(A["nms"], 1)
                pe_.wait_ge(A["kd"], 1)
                for t in range(2):
                    for b in range(NB):
                        last = pe_.transpose(ps[:, t, b * P:b * P + P], kd[:, t * S + b * P:t * S + b * P + P], ident[:, :])
                    last.then_inc(A["kdT"], 1)
                pe_.wait_ge(A["qke"], 2)
                pe_.wait_ge(A["svT_c"], 1)
                for h in range(4):
                    t, rows = h // 2, slice(HD * (h % 2), HD * (h % 2) + HD)
                    if h >= 2:
                        pe_.wait_ge(A["masked"], h - 1)
                    for b in range(NB):
                        c = t * S + b * P
                        last = pe_.matmul(ps[:, 2 + h % 2, b * P:b * P + P], za[rows, S + c:S + c + P],
                                          za[rows, 3 * S + c:3 * S + c + P], start=True, stop=True)
                    last.then_inc(A["score"], 1)
                pe_.wait_ge(A["kdT_c"], 2)
                pe_.wait_ge(A["nln"], 5)
                for t in range(2):
                    for n in range(NCH - 1):
                        rows = slice(CHUNK * (n % 2), CHUNK * (n % 2) + CHUNK)
                        for half in range(2):
                            h = 2 * t + half
                            c = t * S + (n // 2) * P + half * HD
                            v = h * S + (n // 2) * P
                            last = pe_.matmul(ps[HD * half:HD * half + HD, 4 + 2 * t + n % 2, (n // 2) * P:(n // 2) * P + P],
                                              kdT[rows, c:c + HD], gvT[rows, v:v + P], start=True, stop=True)
                    last.then_inc(A["cs"], 1)
                pe_.wait_ge(A["st"], 1 + 2 * (NCH - 1))
                pe_.wait_ge(A["masked"], 4)
                for h in range(4):
                    t, rows = h // 2, slice(HD * (h % 2), HD * (h % 2) + HD)
                    for b in range(NB):
                        pe_.matmul(ps[:, h, b * P:b * P + P], tile(gvT, h)[:, b * P:b * P + P],
                                   tile(aT, h)[:, b * P:b * P + P], start=True, stop=False)
                        for n in (2 * b, 2 * b + 1):
                            c = t * S + n * CHUNK
                            last = pe_.matmul(ps[:, h, n * CHUNK:n * CHUNK + CHUNK], state[rows, t, n, :],
                                              za[rows, 3 * S + c:3 * S + c + CHUNK], start=False, stop=n % 2 == 1)
                    last.then_inc(A["o"], 1)
                for h in range(4):
                    pe_.wait_ge(A["osq"], h + 1)
                    if h >= 2:
                        pe_.wait_ge(A["oln"], h - 1)
                    pe_.matmul(ps[:, 4 + h % 2, :], ones[:, :], sq[:, h % 2, :], start=True, stop=True
                               ).then_inc(A["oms"], 1)
                pe_.wait_ge(A["nq"], 5)
                pe_.wait_ge(A["olo"], 4)
                for s in range(len(ITEMS_A) + 4):
                    if s < len(ITEMS_A):
                        t, half, b = ITEMS_A[s]
                        rows = slice(HD * half, HD * half + HD)
                        k0 = max(b - 1, 0) * P
                        w = P * min(b + 1, 2)
                        if s >= 2:
                            pe_.wait_ge(A["m"], s - 1)
                        q = (13 + t) * S + b * P
                        pe_.matmul(ps[:, s % 2, 0:w], za[rows, q:q + P], za[rows, 17 * S + k0:17 * S + k0 + w],
                                   start=True, stop=True).then_inc(A["s"], 1)
                    if 0 <= s - 2 < len(ITEMS_A):
                        g = s - 2
                        nk = min(ITEMS_A[g][2] + 1, 2)
                        pe_.wait_ge(A["pn"], g + 1)
                        if g >= 2:
                            pe_.wait_ge(A["tc"], g - 1)
                        for k in range(nk):
                            last = pe_.transpose(ps[:, 2 + g % 2, k * P:k * P + P], pA[:, g % 3, k * P:k * P + P],
                                                 ident[:, :])
                        last.then_inc(A["t"], 1)
                    if 0 <= s - 3 < len(ITEMS_A):
                        g = s - 3
                        t, half, b = ITEMS_A[g]
                        nk = min(b + 1, 2)
                        pe_.wait_ge(A["tc"], g + 1)
                        if g % 8 == 0 and t >= 2:
                            pe_.wait_ge(A["olo"], 4 + t - 1)
                        for k in range(nk):
                            v = (b + 1 - nk + k) * P + HD * half
                            last = pe_.matmul(ps[HD * half:HD * half + HD, 4 + t % 2, b * P:b * P + P],
                                              svT[:, v:v + HD], pTA[:, g % 2, k * P:k * P + P],
                                              start=k == 0, stop=k == nk - 1)
                        last.then_inc(A["pv"], 1)

            def mix_b():
                pe_.wait_ge(evac["in_b"], COUNT["in_b"])
                for j in range(6):
                    if j >= 4:
                        pe_.wait_ge(B["vt_c"], j - 3)
                    for b in range(NB):
                        c = ZV[j] * S + b * P
                        last = pe_.transpose(ps[:, j % 4, b * P:b * P + P], zb[:, c:c + P], ident[:, :])
                    last.then_inc(B["vt"], 1)
                for b in range(NB):
                    last = pe_.transpose(ps[:, 4, b * HD:b * HD + HD], zb[0:HD, b * P:b * P + P], ident[0:HD, 0:HD])
                last.then_inc(B["gt"], 1)
                pe_.wait_ge(B["pe"], 4)
                for kv in range(2):
                    for l in range(32):
                        buf = tile(zb, ZKC + kv) if l < 16 else pTB[:, kv, :]
                        by = buf.rearrange("p (n l) -> p l n", l=16)
                        for g in range(2):
                            rows = slice(HD * g, HD * g + HD)
                            last = pe_.matmul(ps[rows, 5, 32 * kv:32 * kv + NCMP], cw1[rows, kv, l * HD:l * HD + HD],
                                              by[rows, l % 16, l // 16:l // 16 + NCMP], start=l == 0, stop=l == 31)
                    last.then_inc(B["hid"], 1)
                pe_.wait_ge(B["gelu"], 2)
                for g in range(2):
                    rows = slice(HD * g, HD * g + HD)
                    last = pe_.matmul(ps[rows, 6, 0:NCMP], cw2[rows, 0:HD], glu[rows, 0:NCMP], start=True, stop=True)
                last.then_inc(B["kc"], 1)
                pe_.wait_ge(B["vt_c"], 6)
                for g in range(2):
                    rows = slice(HD * g, HD * g + HD)
                    last = pe_.matmul(ps[0:NCMP, 2 + g, 0:HD], glu[rows, 32:32 + NCMP], cw2[rows, HD:2 * HD],
                                      start=True, stop=True)
                last.then_inc(B["kc"], 1)
                pe_.wait_ge(B["fc"], 1)
                pe_.wait_ge(B["kc_c"], 3)
                for h in range(NHEADS):
                    if h >= 4:
                        pe_.wait_ge(B["nc_c"], h - 3)
                    pe_.matmul(ps[:, h % 4, :], ident[0:8, h:h + 1].broadcast_to([8, P]), rstd[0:8, :],
                               start=True, stop=True).then_inc(B["nc"], 1)
                pe_.wait_ge(B["gelu"], 2)
                pe_.wait_ge(B["gx"], 1)
                for h in range(NHEADS):
                    rows = slice(HD * (h // 4), HD * (h // 4) + HD)
                    for b in range(NB):
                        q = (ZQ + h % 4) * S + b * P
                        c = (h % 4) * P + b * 32
                        last = pe_.matmul(ps[:, 4 + h // 4, c:c + 32], zb[rows, q:q + P], kcmp[rows, :],
                                          start=True, stop=True)
                    if h % 4 == 3:
                        last.then_inc(B["cs"], 1)
                pe_.wait_ge(B["cp"], 1)
                for h in range(NHEADS):
                    if h >= 2:
                        pe_.wait_ge(B["ct_c"], h - 1)
                    for b in range(NB):
                        c = h * P + b * 32
                        last = pe_.transpose(ps[0:32, 6 + h % 2, b * P:b * P + P], pc[:, c:c + 32], ident[:, :])
                    last.then_inc(B["ct"], 1)
                n = len(ITEMS_B)
                pe_.wait_ge(B["ct_c"], NHEADS)
                for s in range(n + 4):
                    if s < n:
                        kind, t, half, b = ITEMS_B[s]
                        rows = slice(HD * half, HD * half + HD)
                        q, k = {"slc": (ZQ + t, ZKS), "win": (ZQ + t, ZKW), "fox": (ZFQ + t, ZFK + t)}[kind]
                        w = P * (b + 1)
                        if s >= 2:
                            pe_.wait_ge(B["m"], s - 1)
                        last = pe_.matmul(ps[:, s % 2, 0:w], zb[rows, q * S + b * P:q * S + b * P + P],
                                          zb[rows, k * S:k * S + w], start=True, stop=kind != "fox")
                        if kind == "fox":
                            last = pe_.matmul(ps[:, s % 2, b * P:w], identb[:, :], triang[:, :], start=False, stop=True)
                        last.then_inc(B["s"], 1)
                    if 0 <= s - 2 < n:
                        g = s - 2
                        pe_.wait_ge(B["pn"], g + 1)
                        if g >= 2:
                            pe_.wait_ge(B["tc"], g - 1)
                        for k in range(ITEMS_B[g][3] + 1):
                            last = pe_.transpose(ps[:, 2 + g % 2, k * P:k * P + P], pB[:, g % 3, k * P:k * P + P],
                                                 ident[:, :])
                        last.then_inc(B["t"], 1)
                    if 0 <= s - 3 < n:
                        g = s - 3
                        kind, t, half, b = ITEMS_B[g]
                        j = t if kind != "fox" else 4 + t
                        out = ps[HD * half:HD * half + HD, 4 + j % 2, b * P:b * P + P]
                        pe_.wait_ge(B["tc"], g + 1)
                        if j >= 2 and half == 0 and b == 0 and kind != "win":
                            pe_.wait_ge(B["olo"], j - 1)
                        if kind == "slc":
                            c = (t + 4 * half) * S + b * P
                            pe_.matmul(out, vcmp[:, HD * half:HD * half + HD], pTc[:, c:c + P], start=True, stop=False)
                        v = {"slc": 0, "win": 1, "fox": 2 + t}[kind] * S + HD * half
                        for k in range(b + 1):
                            last = pe_.matmul(out, vT[:, v + k * P:v + k * P + HD], pTB[:, g % 2, k * P:k * P + P],
                                              start=kind == "fox" and k == 0, stop=kind != "slc" and k == b)
                        last.then_inc(B["pv"], 1)

            for kind, what in flow:
                if kind == "post" or (kind, what) == ("norm", 6):
                    statistics(what)
                elif kind == "gemm":
                    gemm(what)
                elif kind == "mix_a":
                    mix_a()
                elif kind == "mix_b":
                    mix_b()


def _tiles(w, n):
    return np.ascontiguousarray(w.reshape(KD, P, n, P).transpose(2, 1, 0, 3).reshape(n, P, KD * P))


def _pairs(w, axis):
    shape = w.shape
    w = np.moveaxis(w, axis, 0)
    w = w.reshape(2, 4, HD, -1).transpose(1, 0, 2, 3).reshape(w.shape)
    return np.moveaxis(w, 0, axis).reshape(shape)


def _down(w):
    return np.ascontiguousarray(w.reshape(2, KH, P, KD, P).transpose(3, 0, 2, 1, 4).reshape(16, P, KH * P))


def _up(a, b):
    return np.ascontiguousarray(np.stack([_tiles(a, KF), _tiles(b, KF)], 1).reshape(2 * KF, P, KD * P))


def _cols(v):
    return v.reshape(-1, P).T


def arrays_of(i):
    f = np.float32
    w = i["w_in"][0]
    c = np.cumsum([0, 256, 256, 512, 512, 16, 512, 128, 128])
    gq, gk, gv, gr, glr, sq, sk, sv = [w[:, c[k]:c[k + 1]] for k in range(8)]
    lr = np.zeros((D, P), f)
    lr[:, 0:16] = glr
    in_a = np.concatenate([lr, gk, gq, gv, gr, _pairs(sq, 1), sk, sv], 1)
    wo = i["w_out"][0]
    out_a = np.concatenate([wo[0:512], _pairs(wo[512:1024], 0)], 0)
    w = i["attn_w_in_2"][0]
    c = np.cumsum([0, 512, 512, 512, 8, 512, 128, 128, 128, 128, 128, 128, 24])
    fq, fk, fv, ff, nq, kc, vc, ks, vs, kw, vw, ng = [w[:, c[k]:c[k + 1]] for k in range(12)]
    gt = np.zeros((D, P), f)
    gt[:, 0:8] = ff
    gt[:, 32:56] = ng
    in_b = np.concatenate([gt, _pairs(nq, 1), kc, vc, ks, vs, kw, vw, fq, fk, fv], 1)
    wo = i["attn_w_out_2"][0]
    out_b = np.concatenate([wo[0:512], _pairs(wo[512:1024], 0)], 0)
    pw = i["pool_w_2"][0].reshape(2, 2, 2, P, 2, P).transpose(0, 3, 1, 4, 2, 5)
    weights = {
        "in_a": _tiles(in_a, 19), "out_a": _tiles(out_a, 8),
        "up_a": _up(i["w_up"][0][:, 0:FF], i["w_up"][0][:, FF:]), "down_a": _down(i["w_down"][0]),
        "in_b": _tiles(in_b, 23), "out_b": _tiles(out_b, 8),
        "up_b0": _up(i["ffn_w_gate_2"][0], i["ffn_w_up_2"][0]), "down_b0": _down(i["ffn_w_down_2"][0]),
        "pool": np.ascontiguousarray(pw.reshape(2, P, 8 * P)),
        "up_b1": _up(i["ffn_w_gate_2"][1], i["ffn_w_up_2"][1]), "down_b1": _down(i["ffn_w_down_2"][1]),
    }
    v = {"mix_norm": i["mix_norm"], "ffn_norm": i["ffn_norm"], "pool_scale": i["pool_scale_2"],
         "b_alpha": i["b_alpha"], "gla_norm": i["gla_norm"],
         "q_norm": np.concatenate([i["q_norm"][0], i["q_norm"][0]]),
         "k_norm": np.concatenate([i["k_norm"][0], i["k_norm"][0]]),
         "b_f": np.concatenate([i["fox_b_f_2"][0], np.zeros(P - 8, f)])}
    for layer in range(2):
        for k in range(4):
            v[f"g{layer}{k}"] = i["norm_g_2"][layer, k]
    vecs = np.concatenate([_cols(v[name]) for name in VEC], 1)
    conv = np.concatenate([_cols(i["conv_w"][0, k]) for k in range(3)] + [_cols(i["conv_b"][0])], 1)
    x = i["x"][0].T.reshape(KD, P, S).transpose(1, 0, 2).reshape(P, KD * S)
    out = {"xT": x, "vecs": vecs, "conv": conv, "sinks": np.broadcast_to(i["sinks"][0], (P, NHEADS)),
           "w_alpha2": i["w_alpha2"][0],
           "pe": i["nsa_cmp_pe_2"][0].transpose(0, 2, 1),
           "cmp_w1": i["nsa_cmp_w1_2"][0].reshape(2, 32, HD, HD).transpose(0, 2, 1, 3).reshape(2, HD, 32 * HD),
           "cmp_w2": i["nsa_cmp_w2_2"][0]}
    out = {k: np.ascontiguousarray(a) for k, a in out.items()}
    for p in ORDER:
        out["w_" + p] = weights[p]
    return out


def program(nc, arrays, flow=FLOW):
    f32 = mybir.dt.float32
    args = {k: nc.dram_tensor(k, a.shape, f32, kind="ExternalInput").ap() for k, a in arrays.items()}
    y = nc.dram_tensor("yT", (P, KD * S), f32, kind="ExternalOutput").ap()
    weights = {p: args.pop("w_" + p) for p in ORDER}
    build(nc, weights=weights, yT=y, flow=flow, **args)


def kernel(**inputs):
    import concourse.bacc as _bacc
    from concourse.bass_utils import run_bass_kernel_spmd as _run

    arrays = arrays_of({k: np.asarray(a) for k, a in inputs.items()})
    nc = _bacc.Bacc("TRN2", target_bir_lowering=False, num_devices=1)
    program(nc, arrays)
    r = _run(nc, [arrays], core_ids=[0])
    y = np.asarray(r.results[0]["yT"])
    return np.ascontiguousarray(y.reshape(P, KD, S).transpose(2, 1, 0).reshape(1, S, D))
```

```python
import numpy as np
import concourse.bass as bass
from concourse import mybir
from contextlib import ExitStack


P = 128
S = 512
D = 1024
KD = D // P
FF = 2816
KF = FF // P
KH = KF // 2
EPS = 1e-6
HD = 64
CHUNK = 64
NCH = S // CHUNK
NB = S // P
NCMP = 31
BIG = 1e33
NHEADS = 8
SLOPE = [2.0 ** -(h + 1) for h in range(NHEADS)]
NPOOL, MAXW = 4, 16
GW = D // NPOOL
RAW, SPL = 4, 2

PHASES = [("in_a", 19, 8), ("out_a", 8, 8), ("up_a", 44, 8), ("down_a", 16, 11),
          ("in_b", 23, 8), ("out_b", 8, 8), ("up_b0", 44, 8), ("down_b0", 16, 11),
          ("pool", 2, 8), ("up_b1", 44, 8), ("down_b1", 16, 11)]
FIRST, COUNT, BLOCKS, ORDER = {}, {}, {}, [p[0] for p in PHASES]
_n = 0
for _name, _c, _b in PHASES:
    FIRST[_name], COUNT[_name], BLOCKS[_name] = _n, _c, _b
    _n += _c

FLOW = [("norm", 0), ("gemm", "in_a"), ("mix_a", 0), ("gemm", "out_a"), ("norm", 1), ("gemm", "up_a"),
        ("gemm", "down_a"), ("norm", 2), ("gemm", "in_b"), ("mix_b", 0), ("gemm", "out_b"), ("post", 3),
        ("norm", 4), ("gemm", "up_b0"), ("gemm", "down_b0"), ("post", 5), ("norm", 6), ("gemm", "pool"),
        ("post", 7), ("norm", 8), ("gemm", "up_b1"), ("gemm", "down_b1"), ("post", 9)]
GAIN = {0: "mix_norm", 1: "ffn_norm", 2: "g00", 3: "g01", 4: "g02", 5: "g03", 6: "g10", 7: "g11",
        8: "g12", 9: "g13"}
STREAMED = {1: "out_a", 2: "down_a", 3: "out_b", 5: "down_b0", 7: "pool", 9: "down_b1"}
BOUNDARY = [0, 4, 6, 8]
APPLIED = [0, 1, 2, 4, 6, 8]
POSTS = [3, 5, 7, 9]
XMODE = ("out_a", "down_a")

VEC = {}
_c = 0
for _name, _w in [("mix_norm", 8), ("ffn_norm", 8), ("g00", 8), ("g01", 8), ("g02", 8), ("g03", 8),
                  ("g10", 8), ("g11", 8), ("g12", 8), ("g13", 8), ("pool_scale", 8), ("b_alpha", 2),
                  ("gla_norm", 1), ("q_norm", 1), ("k_norm", 1), ("b_f", 1)]:
    VEC[_name] = _c
    _c += _w
NVEC = _c


def build(nc, xT, vecs, conv, sinks, w_alpha2, pe, cmp_w1, cmp_w2, weights, yT, flow=FLOW):
    f32, f32r, bf16 = mybir.dt.float32, mybir.dt.float32r, mybir.dt.bfloat16
    ALU, ACT, AX = mybir.AluOpType, mybir.ActivationFunctionType, mybir.AxisListType
    names = [w for k, w in flow if k == "gemm"]
    n_units = FIRST[names[-1]] + COUNT[names[-1]]
    has_b = "in_b" in names
    ctx = ExitStack()
    with ctx:
        def sb(name, shape, dt=f32, where=ctx):
            return where.enter_context(nc.sbuf_tensor(name, shape, dt))

        def sem(name):
            return ctx.enter_context(nc.semaphore(name))

        raw = [sb(f"raw{i}", [P, KH * P]) for i in range(RAW)]
        whi = [sb(f"whi{i}", [P, KH * P], f32r) for i in range(SPL)]
        wlo = [sb(f"wlo{i}", [P, KH * P], f32r) for i in range(SPL)]
        x = sb("x", [P, KD * S])
        hhi = sb("hhi", [P, KD * S], f32r)
        hlo = sb("hlo", [P, KD * S], f32r)
        rstd = sb("rstd", [P, S])
        sq = sb("sq", [P, 3, S])
        sumsq = sq[:, 2, :]
        ident = sb("ident", [P, P])
        ones = sb("ones", [P, P])
        vec = sb("vec", [P, NVEC])
        convw = sb("convw", [P, 4 * 2 * KF])
        epsc = sb("epsc", [P, 1])
        invc = sb("invc", [P, MAXW])
        identb = sb("identb", [P, P], bf16)
        triang = sb("triang", [P, P], bf16)
        ffn = ExitStack()
        ahi = sb("ahi", [P, KF * S], f32r, ffn)
        alo = sb("alo", [P, KF * S], f32r, ffn)
        tmp = ExitStack()
        pre = sb("pre", [P, 2, S], f32, tmp)
        cvt = sb("cvt", [P, 2, S], f32, tmp)
        sil = sb("sil", [P, S], f32, tmp)
        gated = sb("gated", [P, S], f32, tmp)
        tmp.close()
        mt = sb("mt", [P, KD * S], f32, ffn)
        ffn.close()
        ma = ExitStack()
        za = sb("za", [P, 19 * S], f32, ma)
        la = sb("la", [P, 2 * S], f32, ma)
        cum = sb("cum", [P, 2 * S], f32, ma)
        eb = sb("eb", [P, 2 * S], f32, ma)
        kd = sb("kd", [P, 2 * S], f32, ma)
        segm = sb("segm", [P, S], f32, ma)
        kdT = sb("kdT", [P, 2 * S], f32, ma)
        gvT = sb("gvT", [P, 4 * S], f32, ma)
        aT = sb("aT", [P, 4 * S], f32, ma)
        svT = sb("svT", [P, S], f32, ma)
        state = sb("state", [P, 2, NCH, P], f32, ma)
        blk64 = sb("blk64", [P, P], f32, ma)
        cmask = sb("cmask", [P, P], f32, ma)
        biasA = sb("biasA", [P, NHEADS, 2 * P], f32, ma)
        distA = sb("distA", [P, 2 * P], f32, ma)
        sink = sb("sink", [P, NHEADS], f32, ma)
        nsink = sb("nsink", [P, NHEADS], f32, ma)
        wal = sb("wal", [16, 2 * P], f32, ma)
        swa = sb("swa", [P, 5, 2 * P], f32, ma)
        pA, pTA = swa[:, 0:3, :], swa[:, 3:5, :]
        rst2 = swa[:, 0:4, :].rearrange("p (a b) s -> p a (b s)", a=2)
        nmA = sb("nmA", [P, 32], f32, ma)
        smA = sb("smA", [P, 32], f32, ma)
        fcA = sb("fcA", [P, 32], f32, ma)
        onA = sb("onA", [P, S], f32, ma)
        ma.close()
        mb = ExitStack()
        zb = sb("zb", [P, 23 * S], f32, mb)
        vT = sb("vT", [P, 6 * S], f32, mb)
        biasB = sb("biasB", [P, NHEADS, S], f32, mb)
        w1m = ExitStack()
        cw1 = sb("cw1", [P, 2, 32 * HD], f32, w1m)
        w1m.close()
        pTc = sb("pTc", [32, NHEADS * S], f32, mb)
        pB = sb("pB", [P, 3, S], f32, mb)
        pTB = sb("pTB", [P, 2, S], f32, mb)
        pc = zb[:, 21 * S:23 * S]
        nmB = sb("nmB", [P, 96], f32, mb)
        smB = sb("smB", [P, 96], f32, mb)
        fcB = sb("fcB", [P, 96], f32, mb)
        kcmp = sb("kcmp", [P, 32], f32, mb)
        vcmp = sb("vcmp", [32, P], f32, mb)
        cw2 = sb("cw2", [P, 2 * HD], f32, mb)
        cpe = sb("cpe", [P, 2 * 32], f32, mb)
        glu = sb("glu", [P, 2 * 32], f32, mb)
        cst = sb("cst", [P, 2 * 32], f32, mb)
        gates = sb("gates", [P, NB * HD], f32, mb)
        distC = sb("distC", [P, P], f32, mb)
        maskC = sb("maskC", [P, P], f32, mb)
        mb.close()
        mp = ExitStack()
        zt = sb("zt", [P, NB, D], f32, mp)
        band = sb("band", [P, 2 * NPOOL, P], f32, mp)
        spill = sb("spill", [P, NPOOL, MAXW], f32, mp)
        rcol = sb("rcol", [P, NB], f32, mp)
        mp.close()

        ps = ctx.enter_context(nc.psum_tensor("ps", [P, 8, S], f32))

        raw_ready = [sem(f"raw_ready{i}") for i in range(RAW)]
        hi_done, lo_done, unit_done = sem("hi_done"), sem("lo_done"), sem("unit_done")
        evac = {p: sem(f"evac_{p}") for p in names}
        sq_ready, sq_used = sem("sq_ready"), sem("sq_used")
        sq_base = {p: 8 * k for k, p in enumerate(STREAMED.values())}
        zeroed = sem("zeroed")
        hid = {k: sem("hidden_" + k) for k in ("tap2", "tap1", "tap0", "silu", "prod", "ahi", "alo")}
        pair_base = {"up_a": 0, "up_b0": KF, "up_b1": 2 * KF}
        ms_ready, rstd_ln, rstd_ready = sem("ms_ready"), sem("rstd_ln"), sem("rstd_ready")
        bsq_ready, bsq_used = sem("bsq_ready"), sem("bsq_used")
        h_hi, h_lo = sem("h_hi"), sem("h_lo")
        post_done, x_done = sem("post_done"), sem("x_done")
        ld_x, ld_gain, ld_vec, ld_cmp = [sem(f"ld_x{m}") for m in range(KD)], sem("ld_gain"), sem("ld_vec"), sem("ld_cmp")
        filled, const_0, const_a, const_b = sem("filled"), sem("const_0"), sem("const_a"), sem("const_b")
        stored = sem("stored")
        A = {k: sem("a_" + k) for k in (
            "svT", "svT_c", "nsq", "nms", "nln", "nrstd", "nq", "nsink", "bias", "logit", "logit_b", "lsig",
            "decay", "rest", "eb", "enb", "ed", "qe", "ke", "kd", "kdT", "kdT_c", "score", "masked", "gvT",
            "gvT_c", "cs", "st", "sig", "o", "osq", "oms", "oln", "orstd", "on", "og", "ohi", "olo",
            "s", "m", "p", "t", "tc", "pv", "arg", "es", "den", "swon", "ot", "oc")}
        B = {}
        if has_b:
            B = {k: sem("b_" + k) for k in (
                "vt", "vt_c", "gt", "gx", "gate", "fz", "fln", "fls", "fc", "nc", "nc_c", "bias", "pe",
                "hid", "gelu", "kc", "kc_c", "cs", "cb", "cm", "cd", "ce", "ck", "csum", "cf", "cp", "ct",
                "ct_c", "s", "m", "p", "t", "tc", "pv", "fac", "prod", "on", "ot", "oc", "ohi", "olo",
                "band", "rt", "rcol", "z", "zc_act", "zc_dve", "mean")}

        BANK_MS = 4
        LN_EXP = "natural_log_exp_and_others"
        RSTD_OF = {"in_a": 0, "up_a": 1, "in_b": 2, "up_b0": 4, "pool": 6, "up_b1": 8}
        POOL_BANK, MEAN_BANK = [0, 2, 5, 0], [4, 7, 2, 3, 5, 6, 0, 1]
        if flow[-1][0] == "post":
            final_sem, final_count = x_done, 8 * (POSTS.index(flow[-1][1]) + 1)
        else:
            final_sem, final_count = evac[names[-1]], 8
        mix_unit = FIRST["in_b"]

        def split_cols(n):
            return next(BLOCKS[p] * P for p in ORDER if FIRST[p] <= n < FIRST[p] + COUNT[p])

        def units(eng, first, last, peel, step):
            for u in range(first, min(peel, last)):
                step(u, 0)
            first = max(first, peel)
            loops = (last - first) // 4
            if loops >= 2:
                with eng.Fori(0, loops) as i:
                    for u in range(first, first + 4):
                        step(u, i)
                first += 4 * loops
            for u in range(first, last):
                step(u, 0)

        def tile(buf, t):
            return buf[:, bass.ds(t * S, S)]

        def col(name, t=0):
            return vec[:, VEC[name] + t:VEC[name] + t + 1]

        def peel_of(p):
            return 8 if p[:4] == "down" else 4

        ITEMS_A = [(t, half, b) for t in range(4) for half in range(2) for b in range(NB)]
        ITEMS_B = [(br, t, half, b) for t in range(4) for half in range(2) for b in range(NB)
                   for br in ("slc", "win")]
        ITEMS_B += [("fox", t, half, b) for t in range(4) for half in range(2) for b in range(NB)]
        ZSQ, ZSK, ZSV, ZLR, ZGK, ZGQ, ZGV, ZGR = 0, 4, 5, 6, 7, 9, 11, 15
        ALONE = {"in_a": 6, "in_b": 11}
        LEAD = {"in_a": 20, "in_b": 16}
        LOOPED = {"in_a": 92, "in_b": 96}
        SPREAD = {"in_a": 34, "in_b": 86}

        NORMS_SWA = [4, 7, 10, 13, 16, 20]
        AFTER_SWA = [92, 100, 102, 104]

        BESIDE_B = [3, 2, 1, 0]

        def blocks_by(p, s):
            if p == "in_b":
                weight = [BESIDE_B[item[3]] for item in ITEMS_B[0:SPREAD[p]]]
                done = sum(weight[0:s + 1]) if s >= 0 else 0
                return LEAD[p] + (LOOPED[p] - LEAD[p]) * done // sum(weight)
            return min(LOOPED[p], LEAD[p] - (-(LOOPED[p] - LEAD[p]) * (s + 1) // SPREAD[p]))

        def finished_at(p, s):
            a = ALONE[p]
            return range(a + blocks_by(p, s - 1) // 8, a + blocks_by(p, s) // 8)

        GLA_LOGIT, GLA_KDT, GLA_SCORE, GLA_GVT = [0, 2], [9, 11], [13, 15, 17, 19], [21, 23, 25, 27]
        GLA_BANK = [4, 5, 7, 3]
        ZQ, ZKC, ZVC, ZKS, ZVS, ZKW, ZVW, ZFV, ZFQ, ZFK = 1, 5, 6, 7, 8, 9, 10, 11, 15, 19
        ZV = [ZVS, ZVW, ZFV, ZFV + 1, ZFV + 2, ZFV + 3]
        ZNC = [ZKC, ZVC, ZVS, ZVW, ZFV, ZFV + 1, ZFV + 2, ZFV + 3]
        GROUPS_B = [("nsa", t, half) for t in range(4) for half in range(2)] + [("fox", t, 0) for t in range(4)]
        NSA_KC, NSA_VC, NSA_CS, FOX_V = 1, [3, 5], [7, 9], [11, 13, 15, 17]
        NSA_CT, CT_HEADS = [18, 19, 22, 23, 26, 27, 30, 31], [0, 4, 1, 5, 2, 6, 3, 7]
        FOX_NC = [33 + 2 * h for h in range(NHEADS)]
        STORED = [(4 + t, ZQ + t) for t in range(4)] + [(t, ZFQ + t) for t in range(2)]
        SPLIT_AT = [88, 89, 89, 90, 90, 91]
        N_ITEMS_B = len(ITEMS_B)

        block = ctx.enter_context(nc.Block())

        @block.sync
        def _(sp):
            for p in names:
                n0, cols = FIRST[p], BLOCKS[p] * P

                def load(u, i, p=p, n0=n0, cols=cols):
                    n = n0 + u
                    if n >= RAW:
                        sp.wait_ge(lo_done, n - RAW + 1 + 4 * i)
                    sp.dma_start(raw[n % RAW][:, 0:cols],
                                 weights[p][bass.ds(u + 4 * i, 1), :, :].rearrange("a p c -> (a p) c")
                                 ).then_inc(raw_ready[n % RAW], 16)
                    if n == 0:
                        for m in range(1, KD, 2):
                            sp.dma_start(x[:, m * S:m * S + S], xT[:, m * S:m * S + S]).then_inc(ld_x[m], 16)

                units(sp, 0, COUNT[p], 4, load)
            for m in range(KD):
                sp.wait_ge(final_sem, final_count - KD + m + 1)
                sp.dma_start(yT[:, m * S:m * S + S], x[:, m * S:m * S + S]).then_inc(stored, 16)
            sp.wait_ge(stored, 16 * KD)

        @block.gpsimd
        def _(pool):
            pool.dma_start(convw[:, :], conv).then_inc(ld_vec, 16)
            pool.dma_start(wal[:, :], w_alpha2).then_inc(ld_vec, 16)
            pool.dma_start(sink[:, :], sinks).then_inc(ld_vec, 16)
            n_filled = [0]

            def fill(ins):
                n_filled[0] += 1
                ins.then_inc(filled, 1)
                pool.wait_ge(filled, n_filled[0])

            def select(out, pattern, base, chan, op, value):
                return pool.affine_select(out=out, in_=out, compare_op=op, fill=value, base=base,
                                          pattern=pattern, channel_multiplier=chan)

            fill(pool.memset(ones[:, :], 1.0 / D))
            fill(pool.memset(epsc[:, :], EPS))
            fill(pool.memset(ident[:, :], 0.0))
            select(ident[:, :], [[-1, P]], 0, 1, ALU.not_equal, 1.0).then_inc(const_0, 1)
            for c in range(MAXW):
                fill(pool.memset(invc[:, c:c + 1], 1.0 / (c + 1)))
            fill(pool.memset(identb[:, :], 0.0))
            fill(select(identb[:, :], [[-1, P]], 0, 1, ALU.not_equal, 1.0))
            fill(pool.memset(triang[:, :], 0.0))
            fill(select(triang[:, :], [[-1, P]], 0, 1, ALU.is_ge, -1e32))
            fill(pool.memset(segm[:, :], 1.0))
            fill(pool.memset(segm[:, :].rearrange("p (n c) -> p n c", c=CHUNK)[:, :, 0:1], 0.0))
            fill(pool.memset(cmask[:, :], 1.0))
            fill(select(cmask[:, :], [[1, P]], 0, -1, ALU.is_ge, 0.0))
            fill(select(cmask[:, CHUNK:P], [[0, P - CHUNK]], -CHUNK, 1, ALU.is_ge, 0.0))
            fill(pool.memset(blk64[:, :], 1.0 / HD))
            fill(select(blk64[:, 0:HD], [[0, HD]], HD - 1, -1, ALU.is_ge, 0.0))
            fill(select(blk64[:, HD:P], [[0, HD]], -HD, 1, ALU.is_ge, 0.0))
            fill(pool.iota(distA[:, :], [[-1, 2 * P]], P, 1, allow_small_or_imprecise_dtypes=True))
            fill(select(distA[:, :], [[-1, 2 * P]], P, 1, ALU.is_ge, BIG))
            select(distA[:, :], [[1, 2 * P]], -1, -1, ALU.is_ge, BIG).then_inc(const_a, 1)
            if has_b:
                pool.wait_ge(unit_done, mix_unit + 1)
                for half in range(2):
                    rows = slice(HD * half, HD * half + HD)
                    for kv in range(2):
                        pool.dma_start(cw1[rows, kv, :], cmp_w1[kv]).then_inc(ld_cmp, 16)
                        pool.dma_start(cw2[rows, kv * HD:kv * HD + HD], cmp_w2[kv]).then_inc(ld_cmp, 16)
                        pool.dma_start(cpe[rows, kv * 32:kv * 32 + 32], pe[kv]).then_inc(ld_cmp, 16)
                fill(pool.iota(biasB[:, 0, :], [[-1, S]], S - P, 1, allow_small_or_imprecise_dtypes=True))
                fill(select(biasB[:, 0, :], [[-1, S]], S - P, 1, ALU.is_ge, BIG))
                dc = distC[:, :].rearrange("p (b n) -> p b n", n=32)
                mc = maskC[:, :].rearrange("p (b n) -> p b n", n=32)
                pat = [[P, NB], [-16, 32]]
                fill(pool.iota(dc, pat, -31, 1, allow_small_or_imprecise_dtypes=True))
                fill(select(dc, pat, -31, 1, ALU.is_ge, BIG))
                fill(pool.memset(dc[:, :, NCMP:32], BIG))
                fill(pool.memset(maskC[:, :], 1.0))
                fill(select(mc, pat, -31, 1, ALU.is_ge, 0.0))
                fill(pool.memset(mc[:, :, NCMP:32], 0.0))
                fill(pool.memset(kcmp[:, :], 0.0))
                pool.memset(vcmp[:, :], 0.0).then_inc(const_b, 1)
            if "pool" in names:
                pool.wait_ge(unit_done, FIRST["down_b0"] + COUNT["down_b0"])
                for g in range(NPOOL):
                    w = 2 << g
                    fill(pool.memset(band[:, 2 * g:2 * g + 2, :], 1.0 / w))
                    fill(pool.tensor_copy(band[:, 2 * g + 1, 0:w - 1], invc[:, 0:w - 1]))
                    pair = band[:, 2 * g:2 * g + 2, :]
                    fill(select(pair, [[0, 2], [-1, P]], w - 1, 1, ALU.is_ge, 0.0))
                    fill(pool.memset(spill[:, g, :], 1.0 / w))
                    fill(select(spill[:, g, :], [[-1, MAXW]], w - 1 - P, 1, ALU.is_ge, 0.0))
                fill(select(band[:, :, :], [[0, 2 * NPOOL], [1, P]], 0, -1, ALU.is_ge, 0.0))
                pool.tensor_tensor(band[:, :, :], band[:, :, :],
                                   ident[:, :].rearrange("p (a t) -> p a t", a=1).broadcast_to([P, 2 * NPOOL, P]),
                                   ALU.subtract).then_inc(B["band"], 1)
        @block.scalar
        def _(act):
            def split_hi(n, i, cols):
                act.wait_ge(raw_ready[n % RAW], 16 * (n // RAW + 1 + i))
                if n >= SPL:
                    act.wait_ge(unit_done, n - SPL + 1 + 4 * i)
                act.activation(whi[n % SPL][:, 0:cols], raw[n % RAW][:, 0:cols], ACT.Copy).then_inc(hi_done, 1)

            def evacuate(p, u, i):
                n = FIRST[p] + u
                if p[:2] == "in":
                    return
                if p[:2] == "up":
                    if u % 2:
                        hidden(p, u, i)
                elif p[:4] == "down":
                    if u % 2:
                        act.wait_ge(unit_done, n + 1 + 4 * i)
                        normalized(p, u // 2, 2 * i, (u // 2) % 2, None)
                elif p[:3] == "out":
                    act.wait_ge(unit_done, n + 1)
                    normalized(p, u, 0, u % 4, None)

            def normalized(p, m, i, bank, scale):
                if p in XMODE:
                    act.wait_ge(evac[p], m + 1 + i)
                if m >= 2:
                    act.wait_ge(sq_used, sq_base[p] + m - 1 + i)
                src = tile(x, m + i) if p in XMODE else ps[:, bank, :]
                scale = 1.0 if scale is None else scale
                act.activation(sq[:, m % 2, :], src, ACT.Square, scale=scale).then_inc(sq_ready, 1)
                if p not in XMODE:
                    act.activation(tile(mt, m + i), ps[:, bank, :], ACT.Copy, scale=scale).then_inc(evac[p], 1)
                if p == "down_a":
                    act.activation(tile(hhi, m), tile(x, m), ACT.Copy, scale=col(GAIN[2], m)).then_inc(h_hi, 1)

            def hidden(p, u, i):
                k, f, fi = hid, u // 2, 2 * i
                done = pair_base[p] + f + fi
                if f >= 1 or p != "up_a":
                    act.wait_ge(k["prod"], done)
                if p == "up_a":
                    for s in range(2):
                        c = f + s * KF
                        act.wait_ge(evac[p], u + s + 4 * i)
                        act.activation(cvt[:, s, :], pre[:, s, :], ACT.Identity,
                                       bias=convw[:, bass.ds(3 * 2 * KF + c + fi, 1)],
                                       scale=convw[:, bass.ds(2 * 2 * KF + c + fi, 1)]).then_inc(k["tap2"], 1)
                    act.wait_ge(k["tap0"], 2 * f + 1 + 2 * fi)
                    act.activation(sil[:, :], cvt[:, 0, :], ACT.Silu).then_inc(k["silu"], 1)
                else:
                    act.wait_ge(evac[p], u + 4 * i)
                    act.activation(sil[:, :], pre[:, 0, :], ACT.Silu).then_inc(k["silu"], 1)
                act.wait_ge(k["prod"], done + 1)
                act.activation(tile(ahi, f + fi), gated[:, :], ACT.Copy).then_inc(k["ahi"], 1)

            def gemm(p):
                n0, count = FIRST[p], ALONE.get(p, COUNT[p])
                if p[:2] == "up":
                    act.preload_act_table(ACT.Silu)
                if p[:4] == "down":
                    act.preload_act_table_set(LN_EXP)

                def step(u, i):
                    split_hi(n0 + u, i, BLOCKS[p] * P)
                    evacuate(p, u - 2, i)

                units(act, 2, count, count if p[:4] == "down" else peel_of(p), step)
                for k in range(2):
                    evacuate(p, count - 2 + k, 0)
                    n = n0 + count + k
                    if n < n_units:
                        split_hi(n, 0, split_cols(n))

            def beside(p, u):
                n = FIRST[p] + u + 2
                if n < n_units:
                    split_hi(n, 0, split_cols(n))

            def statistics(e):
                act.wait_ge(ms_ready, e + 1)
                act.activation(rstd[:, :], ps[:, BANK_MS, :], ACT.Ln, bias=epsc[:, :]).then_inc(rstd_ln, 1)
                act.wait_ge(rstd_ln, e + 1)
                act.activation(rstd[:, :], rstd[:, :], ACT.Exp, scale=-0.5).then_inc(rstd_ready, 1)

            def norm(e):
                for m in range(KD if e != 2 else 0):
                    if e == 0:
                        act.wait_ge(ld_x[m], 16)
                    elif e in BOUNDARY:
                        act.wait_ge(x_done, 8 * POSTS.index(e - 1) + m + 1)
                    if m == 0 and e == 0:
                        act.wait_ge(ld_gain, 16)
                    act.activation(tile(hhi, m), tile(x, m), ACT.Copy, scale=col(GAIN[e], m)).then_inc(h_hi, 1)
                    if e in BOUNDARY:
                        if m >= 2:
                            act.wait_ge(bsq_used, 7 * BOUNDARY.index(e) + m - 1)
                        act.activation(sq[:, m % 2, :], tile(x, m), ACT.Square).then_inc(bsq_ready, 1)
                if e == 0:
                    split_hi(1, 0, split_cols(1))
                statistics(e)

            def mix_a():
                p = "in_a"
                act.wait_ge(ld_vec, 48)
                act.wait_ge(const_a, 1)
                for j in range(6):
                    if j < 5:
                        act.wait_ge(evac[p], ZSQ + j + 1)
                        if j >= 2:
                            act.wait_ge(A["nms"], j - 1)
                        act.activation(sq[:, j % 2, :], tile(za, ZSQ + j), ACT.Square).then_inc(A["nsq"], 1)
                    k = j - 1
                    if k >= 0:
                        act.wait_ge(A["nms"], k + 1)
                        if k >= 2:
                            act.wait_ge(A["nq"], k - 1)
                        act.activation(rst2[:, k % 2, :], ps[:, 4 + k % 2, :], ACT.Ln, bias=epsc[:, :]
                                       ).then_inc(A["nln"], 1)
                        act.wait_ge(A["nln"], k + 1)
                        act.activation(rst2[:, k % 2, :], rst2[:, k % 2, :], ACT.Exp, scale=-0.5
                                       ).then_inc(A["nrstd"], 1)
                    if k == 0:
                        act.wait_ge(A["svT"], 1)
                        act.activation(svT[:, :], ps[:, 7, :], ACT.Copy).then_inc(A["svT_c"], 1)
                    for h in range(2 * k, 2 * k + 2) if 0 <= k < NHEADS // 2 else []:
                        act.activation(biasA[:, h, :], distA[:, :], ACT.Copy, scale=-8 * SLOPE[h]
                                       ).then_inc(A["bias"], 1)
                    if k in (1, 3):
                        beside(p, ALONE[p] + k // 2)
                for s in range(len(ITEMS_A) + 6):
                    if s < len(ITEMS_A):
                        w = P * min(ITEMS_A[s][2] + 1, 2)
                        act.wait_ge(A["m"], s + 1)
                        act.activation(pA[:, s % 3, 0:w], pA[:, s % 3, 0:w], ACT.Exp, scale=-1.0,
                                       bias=nmA[:, s:s + 1], accum_out=smA[:, s:s + 1]).then_inc(A["p"], 1)
                    if s % 8 == 1 and s > 8:
                        t = s // 8 - 1
                        act.wait_ge(A["arg"], 2 * t + 2)
                        act.activation(fcA[:, 8 * t:8 * t + 8], fcA[:, 8 * t:8 * t + 8], ACT.Exp
                                       ).then_inc(A["es"], 1)
                    if 0 <= s - 2 < len(ITEMS_A):
                        g = s - 2
                        w = P * min(ITEMS_A[g][2] + 1, 2)
                        act.wait_ge(A["t"], g + 1)
                        if g >= 2:
                            act.wait_ge(A["pv"], g - 1)
                        act.activation(pTA[:, g % 2, 0:w], ps[:, 2 + g % 2, 0:w], ACT.Copy).then_inc(A["tc"], 1)
                    if s % 8 == 5 and s > 8:
                        t = s // 8 - 1
                        act.wait_ge(A["ot"], t + 1)
                        act.activation(tile(za, ZSQ + t), ps[:, 4 + t % 2, :], ACT.Copy).then_inc(A["oc"], 1)
                    if s == 3:
                        act.wait_ge(A["logit_b"], 2)
                        act.activation(eb[:, :], la[:, :], ACT.Abs).then_inc(A["lsig"], 1)
                        act.wait_ge(A["lsig"], 1)
                        act.activation(eb[:, :], eb[:, :], ACT.Exp, scale=-1.0).then_inc(A["lsig"], 1)
                        act.wait_ge(A["lsig"], 2)
                        act.activation(eb[:, :], eb[:, :], ACT.Ln, bias=1.0).then_inc(A["lsig"], 1)
                    if s == 5:
                        act.wait_ge(A["decay"], 3)
                        act.activation(eb[:, :], cum[:, :], ACT.Exp, scale=1 / 16).then_inc(A["eb"], 1)
                        act.activation(la[:, :], cum[:, :], ACT.Exp, scale=-1 / 16).then_inc(A["enb"], 1)
                    if s == 6:
                        act.wait_ge(A["rest"], 2)
                        act.activation(kd[:, :], kd[:, :], ACT.Exp, scale=1 / 16).then_inc(A["ed"], 1)
                    if s - 1 in GLA_KDT:
                        t = GLA_KDT.index(s - 1)
                        act.wait_ge(A["kdT"], t + 1)
                        act.activation(tile(kdT, t), ps[:, 7, :], ACT.Copy).then_inc(A["kdT_c"], 1)
                    if s - 1 in GLA_GVT:
                        h = GLA_GVT.index(s - 1)
                        act.wait_ge(A["gvT"], h + 1)
                        act.activation(tile(gvT, h), ps[:, 7, :], ACT.Copy).then_inc(A["gvT_c"], 1)
                    for u in finished_at(p, s):
                        beside(p, u)
                beside(p, 17)
                for h in range(5):
                    if h < 4:
                        act.wait_ge(A["o"], h + 1)
                        if h >= 2:
                            act.wait_ge(A["oms"], h - 1)
                        act.activation(sq[:, h % 2, :], ps[:, GLA_BANK[h], :], ACT.Square).then_inc(A["osq"], 1)
                    k = h - 1
                    if k >= 0:
                        act.wait_ge(A["oms"], k + 1)
                        if k >= 2:
                            act.wait_ge(A["on"], k - 1)
                        act.activation(rst2[:, k % 2, :], ps[:, k % 2, :], ACT.Ln, bias=epsc[:, :],
                                       scale=float(D // P)).then_inc(A["oln"], 1)
                        act.wait_ge(A["oln"], k + 1)
                        act.activation(rst2[:, k % 2, :], rst2[:, k % 2, :], ACT.Exp, scale=-0.5
                                       ).then_inc(A["orstd"], 1)
                    if k == 0:
                        beside(p, 18)
                for t in range(4):
                    act.wait_ge(A["oc"], t + 1)
                    act.activation(tile(hhi, 4 + t), tile(za, ZSQ + t), ACT.Copy).then_inc(A["ohi"], 1)
                act.wait_ge(evac[p], COUNT[p])
                for h in range(4):
                    act.activation(tile(za, ZGR + h), tile(za, ZGR + h), ACT.Silu).then_inc(A["sig"], 1)
                for h in range(4):
                    act.wait_ge(A["og"], h + 1)
                    act.activation(tile(hhi, h), tile(aT, h), ACT.Copy).then_inc(A["ohi"], 1)

            def mix_b():
                p = "in_b"
                act.preload_act_table_set(LN_EXP)
                for j in range(2):
                    act.wait_ge(B["vt"], j + 1)
                    act.activation(tile(vT, j), ps[:, j, :], ACT.Copy).then_inc(B["vt_c"], 1)
                act.wait_ge(B["gt"], 1)
                act.activation(gates[:, :], ps[:, 2, 0:NB * HD], ACT.Exp, scale=-1.0).then_inc(B["gx"], 1)
                act.wait_ge(B["fz"], 1)
                act.activation(sq[0:8, 1, :], sq[0:8, 0, :], ACT.Abs).then_inc(B["fln"], 1)
                act.wait_ge(B["fln"], 1)
                act.activation(sq[0:8, 1, :], sq[0:8, 1, :], ACT.Exp, scale=-1.0).then_inc(B["fln"], 1)
                act.wait_ge(B["fln"], 2)
                act.activation(sq[0:8, 1, :], sq[0:8, 1, :], ACT.Ln, bias=1.0).then_inc(B["fln"], 1)
                act.wait_ge(const_b, 1)
                for h in [1, 2, 3, 4, 5, 6, 7, 0]:
                    if h == 0:
                        act.wait_ge(B["bias"], 7)
                    act.activation(biasB[:, h, :], biasB[:, 0, :], ACT.Copy, scale=-8 * SLOPE[h]).then_inc(B["bias"], 1)
                beside(p, 11)
                act.preload_act_table(ACT.Gelu_apprx_tanh)
                act.wait_ge(B["hid"], 2)
                for kv in range(2):
                    act.activation(glu[:, 32 * kv:32 * kv + NCMP], ps[:, 3, 32 * kv:32 * kv + NCMP],
                                   ACT.Gelu_apprx_tanh).then_inc(B["gelu"], 1)
                act.preload_act_table_set(LN_EXP)
                beside(p, 12)
                for s in range(N_ITEMS_B + 6):
                    if s < N_ITEMS_B:
                        w = P * (ITEMS_B[s][3] + 1)
                        act.wait_ge(B["m"], s + 1)
                        act.activation(pB[:, s % 3, 0:w], pB[:, s % 3, 0:w], ACT.Exp, scale=-1.0,
                                       bias=nmB[:, s:s + 1], accum_out=smB[:, s:s + 1]).then_inc(B["p"], 1)
                    if 0 <= s - 2 < N_ITEMS_B:
                        g = s - 2
                        w = P * (ITEMS_B[g][3] + 1)
                        act.wait_ge(B["t"], g + 1)
                        if g >= 2:
                            act.wait_ge(B["pv"], g - 1)
                        act.activation(pTB[:, g % 2, 0:w], ps[:, 2 + g % 2, 0:w], ACT.Copy).then_inc(B["tc"], 1)
                    if s == NSA_KC + 1:
                        act.wait_ge(B["kc"], 1)
                        act.activation(kcmp[:, 0:NCMP], ps[:, 7, 0:NCMP], ACT.Copy).then_inc(B["kc_c"], 1)
                    if s - 1 in NSA_VC:
                        g = NSA_VC.index(s - 1)
                        act.wait_ge(B["kc"], 2 + g)
                        act.activation(vcmp[0:NCMP, HD * g:HD * g + HD], ps[0:NCMP, 7, 0:HD], ACT.Copy
                                       ).then_inc(B["kc_c"], 1)
                    if s == 13:
                        act.wait_ge(B["cd"], 1)
                        act.activation(pc, pc, ACT.Exp, scale=0.125).then_inc(B["ce"], 1)
                    if s - 1 in FOX_V:
                        j = FOX_V.index(s - 1)
                        act.wait_ge(B["vt"], 3 + j)
                        act.activation(tile(vT, 2 + j), ps[:, 7, :], ACT.Copy).then_inc(B["vt_c"], 1)
                    if s in NSA_CT:
                        k = NSA_CT.index(s)
                        h = CT_HEADS[k]
                        act.wait_ge(B["ct"], k + 1)
                        act.activation(pTc[:, h * S:h * S + S], ps[0:32, 7, :], ACT.Copy).then_inc(B["ct_c"], 1)
                    if s - 1 in FOX_NC:
                        h = FOX_NC.index(s - 1)
                        act.wait_ge(B["nc"], h + 1)
                        act.activation(tile(zb, ZNC[h]), ps[:, 7, :], ACT.Copy, scale=-8.0).then_inc(B["nc_c"], 1)
                    for j, (kind, t, half) in enumerate(GROUPS_B):
                        if s != 8 * (j + 1) + 5:
                            continue
                        if kind == "nsa" and half == 1:
                            act.wait_ge(B["ot"], t + 1)
                            act.activation(tile(zb, ZQ + t), ps[:, 5, :], ACT.Copy).then_inc(B["oc"], 1)
                        if kind == "fox" and t < 2:
                            act.wait_ge(B["ot"], 4 + t + 1)
                            act.activation(tile(zb, ZFQ + t), ps[:, 4 + t % 2, :], ACT.Copy).then_inc(B["oc"], 1)
                        if kind == "fox" and t >= 2:
                            act.wait_ge(B["ot"], 4 + t + 1)
                            act.activation(tile(hhi, t), ps[:, 4 + t % 2, :], ACT.Copy).then_inc(B["ohi"], 1)
                    for k, (row, t) in enumerate(STORED):
                        if SPLIT_AT[k] == s:
                            act.wait_ge(unit_done, FIRST[p] + COUNT[p])
                            act.wait_ge(B["oc"], k + 1)
                            act.activation(tile(hhi, row), tile(zb, t), ACT.Copy).then_inc(B["ohi"], 1)
                    for u in finished_at(p, s):
                        beside(p, u)

            def pool_layer():
                p = "pool"
                act.wait_ge(B["rt"], 1)
                act.activation(rcol[:, :], ps[:, 7, 0:NB], ACT.Copy).then_inc(B["rcol"], 1)
                act.wait_ge(B["rcol"], 1)
                for g in range(NPOOL):
                    if g % 2:
                        act.wait_ge(unit_done, FIRST[p] + g // 2 + 1)
                    else:
                        act.wait_ge(B["z"], g // 2 + 1)
                    for b in range(2):
                        act.activation(zt[:, b, g * GW:g * GW + GW], ps[:, POOL_BANK[g], b * GW:b * GW + GW],
                                       ACT.Copy, scale=rcol[:, b:b + 1]).then_inc(B["zc_act"], 1)
                    if g == 1:
                        split_hi(FIRST[p] + 2, 0, split_cols(FIRST[p] + 2))
                for m in range(KD):
                    act.wait_ge(B["mean"], m + 1)
                    normalized(p, m, 0, MEAN_BANK[m], col("pool_scale", m))
                    if m == 0:
                        split_hi(FIRST[p] + 3, 0, split_cols(FIRST[p] + 3))

            act.dma_start(vec[:, :], vecs).then_inc(ld_gain, 16)
            for m in range(0, KD, 2):
                act.dma_start(x[:, m * S:m * S + S], xT[:, m * S:m * S + S]).then_inc(ld_x[m], 16)
            act.preload_act_table_set(LN_EXP)
            act.wait_ge(const_0, 1)
            for kind, what in flow:
                if kind == "norm":
                    if what == 0:
                        split_hi(0, 0, split_cols(0))
                    norm(what)
                elif what == "pool":
                    pool_layer()
                elif kind == "gemm":
                    gemm(what)
                elif kind == "post":
                    statistics(what)
                elif kind == "mix_a":
                    mix_a()
                elif kind == "mix_b":
                    mix_b()

        @block.vector
        def _(dve):
            def split_lo(n, i, cols):
                dve.wait_ge(hi_done, n + 1 + 4 * i)
                dve.tensor_tensor(wlo[n % SPL][:, 0:cols], raw[n % RAW][:, 0:cols],
                                  whi[n % SPL][:, 0:cols].bitcast(f32), ALU.subtract).then_inc(lo_done, 1)

            def summed(p, m, i):
                dve.wait_ge(sq_ready, sq_base[p] + m + 1 + i)
                if m >= 1:
                    dve.wait_ge(sq_used, sq_base[p] + m + i)
                dve.tensor_tensor(sumsq[:, :], sumsq[:, :], sq[:, m % 2, :], ALU.add).then_inc(sq_used, 1)

            def residual(p, m, i, bank):
                if p in XMODE:
                    dve.tensor_tensor(tile(x, m + i), ps[:, bank, :], tile(x, m + i), ALU.add).then_inc(evac[p], 1)
                summed(p, m, i)
                if p == "down_a":
                    lower(2, 8 * APPLIED.index(2), m, i)

            def evacuate(p, u, i):
                n = FIRST[p] + u
                if p[:2] == "in":
                    z = za if p == "in_a" else zb
                    if u == 0:
                        dve.wait_ge(rstd_ready, RSTD_OF[p] + 1)
                    dve.wait_ge(unit_done, n + 1 + 4 * i)
                    bank = u % 4 if u < ALONE.get(p, COUNT[p]) else 6
                    dve.tensor_tensor(tile(z, u + 4 * i), ps[:, bank, :], rstd[:, :], ALU.mult
                                      ).then_inc(evac[p], 1)
                elif p[:2] == "up":
                    hidden(p, u, i)
                elif p[:4] == "down":
                    if u % 2:
                        dve.wait_ge(unit_done, n + 1 + 4 * i)
                        residual(p, u // 2, 2 * i, (u // 2) % 2)
                elif p[:3] == "out":
                    dve.wait_ge(unit_done, n + 1)
                    residual(p, u, 0, u % 4)

            def hidden(p, u, i):
                k, f, fi = hid, u // 2, 2 * i
                done = pair_base[p] + f + fi
                if u == 0:
                    dve.wait_ge(rstd_ready, RSTD_OF[p] + 1)
                if u % 2 == 0 and f >= 1 and p != "up_a":
                    dve.wait_ge(k["silu"], done)
                if p == "up_a" and f >= 1:
                    dve.wait_ge(k["tap2"], u - 1 + 4 * i)
                dve.wait_ge(unit_done, FIRST[p] + u + 1 + 4 * i)
                dve.tensor_tensor(pre[:, u % 2, :], ps[:, u % 4, :], rstd[:, :], ALU.mult).then_inc(evac[p], 1)
                if u % 2 == 0:
                    return
                if p == "up_a":
                    for s in range(2):
                        c = f + s * KF
                        dve.wait_ge(k["tap2"], 2 * f + s + 1 + 2 * fi)
                        dve.scalar_tensor_tensor(out=cvt[:, s, 1:S], in0=pre[:, s, 0:S - 1],
                                                 scalar=convw[:, bass.ds(2 * KF + c + fi, 1)],
                                                 in1=cvt[:, s, 1:S], op0=ALU.mult, op1=ALU.add
                                                 ).then_inc(k["tap1"], 1)
                        dve.wait_ge(k["tap1"], 2 * f + s + 1 + 2 * fi)
                        dve.scalar_tensor_tensor(out=cvt[:, s, 2:S], in0=pre[:, s, 0:S - 2],
                                                 scalar=convw[:, bass.ds(c + fi, 1)],
                                                 in1=cvt[:, s, 2:S], op0=ALU.mult, op1=ALU.add
                                                 ).then_inc(k["tap0"], 1)
                    dve.wait_ge(k["tap0"], 2 * f + 2 + 2 * fi)
                    other = cvt[:, 1, :]
                else:
                    dve.wait_ge(evac[p], u + 1 + 4 * i)
                    other = pre[:, 1, :]
                dve.wait_ge(k["silu"], done + 1)
                if f >= 1 or p != "up_a":
                    dve.wait_ge(k["alo"], done)
                dve.tensor_tensor(gated[:, :], other, sil[:, :], ALU.mult).then_inc(k["prod"], 1)
                dve.wait_ge(k["ahi"], done + 1)
                dve.tensor_tensor(tile(alo, f + fi), gated[:, :], tile(ahi, f + fi).bitcast(f32),
                                  ALU.subtract).then_inc(k["alo"], 1)

            def gemm(p):
                n0, count = FIRST[p], ALONE.get(p, COUNT[p])
                if p in sq_base:
                    clear_sum(p)

                def step(u, i):
                    split_lo(n0 + u, i, BLOCKS[p] * P)
                    evacuate(p, u - 2, i)

                units(dve, 2, count, peel_of(p), step)
                for k in range(2):
                    evacuate(p, count - 2 + k, 0)
                    n = n0 + count + k
                    if n < n_units:
                        split_lo(n, 0, split_cols(n))

            def clear_sum(p):
                e = next(e for e, q in STREAMED.items() if q == p)
                dve.memset(sumsq[:, :], 0.0).then_inc(zeroed, 1)
                dve.wait_ge(zeroed, sorted(STREAMED).index(e) + 1)

            def beside(p, u):
                evacuate(p, u, 0)
                n = FIRST[p] + u + 2
                if n < n_units:
                    split_lo(n, 0, split_cols(n))

            def norm(e):
                if e == 0:
                    dve.wait_ge(ld_gain, 16)
                if e - 1 not in POSTS and e != 2:
                    for m in range(KD):
                        lower(e, 8 * APPLIED.index(e), m)
                if e == 0:
                    split_lo(1, 0, split_cols(1))

            def lower(e, base, m, i=0):
                dve.wait_ge(h_hi, base + m + 1 + i)
                g = VEC[GAIN[e]] + m
                dve.scalar_tensor_tensor(out=tile(hlo, m + i), in0=tile(x, m + i), scalar=vec[:, bass.ds(g + i, 1)],
                                         in1=tile(hhi, m + i).bitcast(f32), op0=ALU.mult, op1=ALU.subtract
                                         ).then_inc(h_lo, 1)

            def post(e):
                dve.wait_ge(rstd_ready, e + 1)
                base = 8 * POSTS.index(e)
                split = e + 1 in APPLIED
                for m in range(KD + 1):
                    if m < KD:
                        dve.scalar_tensor_tensor(out=tile(mt, m), in0=tile(mt, m), scalar=col(GAIN[e], m),
                                                 in1=rstd[:, :], op0=ALU.mult, op1=ALU.mult).then_inc(post_done, 1)
                    if m >= 1 and split:
                        lower(e + 1, 8 * APPLIED.index(e + 1), m - 1)
                    if m < KD:
                        dve.wait_ge(post_done, base + m + 1)
                        dve.tensor_tensor(tile(x, m), tile(x, m), tile(mt, m), ALU.add).then_inc(x_done, 1)

            def mix_a():
                p = "in_a"
                for j in range(5):
                    dve.wait_ge(A["nrstd"], j + 1)
                    dve.wait_ge(evac[p], ZSQ + j + 1)
                    dve.scalar_tensor_tensor(out=tile(za, ZSQ + j), in0=tile(za, ZSQ + j),
                                             scalar=col("q_norm" if j < 4 else "k_norm"), in1=rst2[:, j % 2, :],
                                             op0=ALU.mult, op1=ALU.mult).then_inc(A["nq"], 1)
                    if j in (1, 3):
                        beside(p, ALONE[p] + j // 2)
                dve.wait_ge(ld_vec, 48)
                dve.tensor_scalar(nsink[:, :], sink[:, :], -1.0, None, ALU.mult).then_inc(A["nsink"], 1)
                dve.wait_ge(A["bias"], NHEADS)
                dve.wait_ge(A["nsink"], 1)
                dve.wait_ge(A["nq"], 5)
                for s in range(len(ITEMS_A) + 6):
                    if s < len(ITEMS_A):
                        t, half, b = ITEMS_A[s]
                        h, w = t + 4 * half, P * min(b + 1, 2)
                        dve.wait_ge(A["s"], s + 1)
                        if s >= 3:
                            dve.wait_ge(A["t"], s - 2)
                        dve.tensor_tensor_reduce(out=pA[:, s % 3, 0:w], in0=ps[:, s % 2, 0:w],
                                                 in1=biasA[:, h, 2 * P - w:2 * P], scale=-0.125,
                                                 scalar=nsink[:, h:h + 1], op0=ALU.add, op1=ALU.min,
                                                 accum_out=nmA[:, s:s + 1]).then_inc(A["m"], 1)
                    t = s // 8 - 1
                    if t >= 0 and s % 8 == 1:
                        dve.wait_ge(A["m"], 8 * t + 8)
                        for half in range(2):
                            h, c = t + 4 * half, 8 * t + 4 * half
                            dve.tensor_scalar(fcA[:, c:c + 4], nmA[:, c:c + 4], sink[:, h:h + 1], None, ALU.add
                                              ).then_inc(A["arg"], 1)
                    if t >= 0 and s % 8 == 2:
                        c = slice(8 * t, 8 * t + 8)
                        dve.wait_ge(A["es"], t + 1)
                        dve.wait_ge(A["p"], 8 * t + 8)
                        dve.tensor_tensor(fcA[:, c], fcA[:, c], smA[:, c], ALU.add).then_inc(A["den"], 1)
                        dve.wait_ge(A["den"], 2 * t + 1)
                        dve.reciprocal(fcA[:, c], fcA[:, c]).then_inc(A["den"], 1)
                    if t >= 0 and s % 8 == 3:
                        dve.wait_ge(A["pv"], 8 * t + 8)
                        dve.wait_ge(A["den"], 2 * t + 2)
                        if t:
                            dve.wait_ge(A["ot"], t)
                        for half in range(2):
                            c = 8 * t + 4 * half
                            view = [v.rearrange("p (b h d) -> p b h d", h=2, d=HD)[:, :, half, :]
                                    for v in (onA[:, :], ps[:, 4 + t % 2, :])]
                            dve.tensor_tensor(view[0], view[1],
                                              fcA[:, c:c + 4].rearrange("p (b d) -> p b d", d=1)
                                              .broadcast_to([P, NB, HD]), ALU.mult).then_inc(A["swon"], 1)
                    if s in GLA_LOGIT:
                        t = GLA_LOGIT.index(s)
                        dve.wait_ge(A["logit"], t + 1)
                        dve.tensor_scalar(tile(la, t), ps[:, 7, :], col("b_alpha", t), None, ALU.add
                                          ).then_inc(A["logit_b"], 1)
                    if s == 4:
                        dve.wait_ge(A["lsig"], 3)
                        dve.scalar_tensor_tensor(out=la[:, :], in0=la[:, :], scalar=0.0, in1=eb[:, :], op0=ALU.min,
                                                 op1=ALU.subtract).then_inc(A["decay"], 1)
                        dve.wait_ge(A["decay"], 1)
                        for t in range(2):
                            dve.tensor_tensor_scan(tile(cum, t), segm[:, :], tile(la, t), 0.0, ALU.mult, ALU.add
                                                   ).then_inc(A["decay"], 1)
                    if s == 5:
                        dve.wait_ge(A["decay"], 3)
                        for t in range(2):
                            cv = tile(cum, t).rearrange("p (n c) -> p n c", c=CHUNK)
                            ev = tile(kd, t).rearrange("p (n c) -> p n c", c=CHUNK)
                            dve.tensor_tensor(ev, cv[:, :, CHUNK - 1:CHUNK].broadcast_to([P, NCH, CHUNK]), cv,
                                              ALU.subtract).then_inc(A["rest"], 1)
                    gk, gq = za[:, ZGK * S:ZGK * S + 2 * S], za[:, ZGQ * S:ZGQ * S + 2 * S]
                    if s == 7:
                        dve.wait_ge(A["ed"], 1)
                        dve.wait_ge(evac[p], ZGK + 2)
                        dve.tensor_tensor(kd[:, :], gk, kd[:, :], ALU.mult).then_inc(A["kd"], 1)
                    if s == 8:
                        dve.wait_ge(A["enb"], 1)
                        dve.wait_ge(A["kd"], 1)
                        dve.tensor_tensor(gk, gk, la[:, :], ALU.mult).then_inc(A["ke"], 1)
                    if s == 11:
                        dve.wait_ge(A["eb"], 1)
                        dve.wait_ge(evac[p], ZGQ + 2)
                        dve.scalar_tensor_tensor(out=gq, in0=gq, scalar=HD ** -0.5, in1=eb[:, :], op0=ALU.mult,
                                                 op1=ALU.mult).then_inc(A["qe"], 1)
                    if s - 1 in GLA_SCORE:
                        h = GLA_SCORE.index(s - 1)
                        dve.wait_ge(A["score"], h + 1)
                        dve.tensor_tensor(tile(aT, h).rearrange("p (b c) -> p b c", c=P),
                                          ps[:, 7, :].rearrange("p (b c) -> p b c", c=P),
                                          cmask[:, :].rearrange("p (b c) -> p b c", b=1).broadcast_to([P, NB, P]),
                                          ALU.mult).then_inc(A["masked"], 1)
                    for u in finished_at(p, s):
                        beside(p, u)
                dve.memset(state[:, :, 0, :], 0.0).then_inc(A["st"], 1)
                for n in range(NCH - 1):
                    for t in range(2):
                        if n == 0:
                            dve.wait_ge(A["cs"], t + 1)
                        dve.wait_ge(A["st"], 1 + (0 if n == 0 else 2 * n - 1 + t))
                        c = t * S + n * CHUNK + CHUNK - 1
                        dve.scalar_tensor_tensor(out=state[:, t, n + 1, :], in0=state[:, t, n, :],
                                                 scalar=eb[:, c:c + 1],
                                                 in1=ps[:, 2 * t + n % 2, (n // 2) * P:(n // 2) * P + P],
                                                 op0=ALU.mult, op1=ALU.add).then_inc(A["st"], 1)
                beside(p, 17)
                for h in range(4):
                    if h == 1:
                        beside(p, 18)
                    dve.wait_ge(A["orstd"], h + 1)
                    dve.scalar_tensor_tensor(out=tile(aT, h), in0=ps[:, GLA_BANK[h], :], scalar=col("gla_norm"),
                                             in1=rst2[:, h % 2, :], op0=ALU.mult, op1=ALU.mult).then_inc(A["on"], 1)
                for t in range(4):
                    dve.wait_ge(A["ohi"], t + 1)
                    dve.tensor_tensor(tile(hlo, 4 + t), tile(za, ZSQ + t), tile(hhi, 4 + t).bitcast(f32),
                                      ALU.subtract).then_inc(A["olo"], 1)
                for h in range(5):
                    if h < 4:
                        dve.wait_ge(A["on"], h + 1)
                        dve.wait_ge(A["sig"], h + 1)
                        dve.tensor_tensor(tile(aT, h), tile(aT, h), tile(za, ZGR + h), ALU.mult).then_inc(A["og"], 1)
                    if h:
                        dve.wait_ge(A["ohi"], 4 + h)
                        dve.tensor_tensor(tile(hlo, h - 1), tile(aT, h - 1), tile(hhi, h - 1).bitcast(f32),
                                          ALU.subtract).then_inc(A["olo"], 1)

            def mix_b():
                p = "in_b"
                dve.wait_ge(evac[p], ALONE[p])
                dve.tensor_scalar(sq[0:8, 0, :], zb[0:8, 0:S], vec[0:8, VEC["b_f"]:VEC["b_f"] + 1], None, ALU.add
                                  ).then_inc(B["fz"], 1)
                dve.wait_ge(ld_cmp, 16 * 12)
                for kv in range(2):
                    zt = tile(zb, ZKC + kv)
                    for part in (1, 0):
                        out = zt if part == 0 else pTB[:, kv, :]
                        add = cpe[:, 32 * kv + 16 * part:32 * kv + 16 * part + 16]
                        dve.tensor_tensor(out.rearrange("p (n l) -> p n l", l=16),
                                          zt.rearrange("p (n l) -> p n l", l=16),
                                          add.rearrange("p (n l) -> p n l", n=1).broadcast_to([P, 32, 16]),
                                          ALU.add).then_inc(B["pe"], 1)
                dve.wait_ge(B["gx"], 1)
                dve.tensor_scalar(gates[:, :], gates[:, :], 1.0, None, ALU.add).then_inc(B["gate"], 1)
                dve.wait_ge(B["gate"], 1)
                dve.reciprocal(gates[:, :], gates[:, :]).then_inc(B["gate"], 1)
                dve.wait_ge(B["fln"], 3)
                dve.scalar_tensor_tensor(out=sq[0:8, 0, :], in0=sq[0:8, 0, :], scalar=0.0, in1=sq[0:8, 1, :],
                                         op0=ALU.min, op1=ALU.subtract).then_inc(B["fls"], 1)
                dve.wait_ge(B["fls"], 1)
                dve.tensor_tensor_scan(sq[0:8, 2, :], invc[0:8, 0:1].broadcast_to([8, S]), sq[0:8, 0, :], 0.0,
                                       ALU.mult, ALU.add).then_inc(B["fc"], 1)
                beside(p, 11)
                beside(p, 12)
                gv = gates[:, :].rearrange("p (b c) -> p b c", c=HD)
                pc4 = pc.rearrange("p (h c) -> p h c", c=P)
                pg = pc.rearrange("p (g n) -> p g n", n=32)
                cmax, csum = cst[:, 0:32], cst[:, 32:64]

                def over_keys(v):
                    return v.rearrange("p (g n) -> p g n", n=1).broadcast_to([P, 32, 32])

                dve.wait_ge(const_b, 1)
                dve.wait_ge(B["bias"], NHEADS)
                dve.wait_ge(B["hid"], 2)
                for s in range(N_ITEMS_B + 6):
                    if s < N_ITEMS_B:
                        kind, t, half, b = ITEMS_B[s]
                        w = P * (b + 1)
                        if kind == "fox":
                            h = 2 * t + half
                            dve.wait_ge(B["nc_c"], h + 1)
                            bias = zb[:, ZNC[h] * S:ZNC[h] * S + w]
                        else:
                            bias = biasB[:, t + 4 * half, S - w:S]
                        dve.wait_ge(B["s"], s + 1)
                        if s >= 3:
                            dve.wait_ge(B["t"], s - 2)
                        dve.tensor_tensor_reduce(out=pB[:, s % 3, 0:w], in0=ps[:, s % 2, 0:w], in1=bias,
                                                 scale=-0.125, scalar=3e38, op0=ALU.add, op1=ALU.min,
                                                 accum_out=nmB[:, s:s + 1]).then_inc(B["m"], 1)
                    if s - 1 in NSA_CS:
                        g = NSA_CS.index(s - 1)
                        dve.wait_ge(B["cs"], g + 1)
                        for k in range(4):
                            h = 4 * g + k
                            dve.scalar_tensor_tensor(out=pc4[:, h, :], in0=distC[:, :], scalar=-8 * SLOPE[h],
                                                     in1=ps[:, 7, k * P:k * P + P],
                                                     op0=ALU.mult, op1=ALU.add).then_inc(B["cb"], 1)
                    if s == 11:
                        dve.wait_ge(B["cb"], NHEADS)
                        dve.tensor_reduce(cmax, pg, AX.X, ALU.max).then_inc(B["cm"], 1)
                    if s == 12:
                        dve.wait_ge(B["cm"], 1)
                        dve.tensor_tensor(pg, pg, over_keys(cmax), ALU.subtract).then_inc(B["cd"], 1)
                    if s == 14:
                        dve.wait_ge(B["ce"], 1)
                        dve.tensor_tensor(pc4, pc4, maskC[:, :].rearrange("p (h c) -> p h c", h=1)
                                          .broadcast_to([P, NHEADS, P]), ALU.mult).then_inc(B["ck"], 1)
                    if s == 15:
                        dve.wait_ge(B["ck"], 1)
                        dve.tensor_reduce(csum, pg, AX.X, ALU.add).then_inc(B["csum"], 1)
                    if s == 16:
                        dve.wait_ge(B["csum"], 1)
                        dve.tensor_scalar(csum, csum, 1e-30, None, ALU.max).then_inc(B["cf"], 1)
                        dve.wait_ge(B["cf"], 1)
                        dve.reciprocal(csum, csum).then_inc(B["cf"], 1)
                        dve.wait_ge(B["cf"], 2)
                        dve.wait_ge(B["gate"], 2)
                        cg = gv[:, :, 32:56].rearrange("p b (h r) -> p h b r", r=3)[:, :, :, 0]
                        cv = csum.rearrange("p (h b) -> p h b", b=NB)
                        dve.tensor_tensor(cv, cv, cg, ALU.mult).then_inc(B["cf"], 1)
                    if s == 17:
                        dve.wait_ge(B["cf"], 3)
                        dve.tensor_tensor(pg, pg, over_keys(csum), ALU.mult).then_inc(B["cp"], 1)
                    for j, (kind, t, half) in enumerate(GROUPS_B):
                        end = 8 * (j + 1)
                        f = fcB[:, end - 8:end]
                        if s == end + 1:
                            dve.wait_ge(B["p"], end)
                            dve.tensor_scalar(f, smB[:, end - 8:end], 1e-30, None, ALU.max).then_inc(B["fac"], 1)
                            dve.wait_ge(B["fac"], 3 * min(j, 8) + 2 * max(j - 8, 0) + 1)
                            dve.reciprocal(f, f).then_inc(B["fac"], 1)
                            if kind == "nsa":
                                h = t + 4 * half
                                dve.wait_ge(B["fac"], 3 * j + 2)
                                dve.wait_ge(B["gate"], 2)
                                fv = f.rearrange("p (b r) -> p b r", r=2)
                                dve.tensor_tensor(fv, fv, gv[:, :, 33 + 3 * h:35 + 3 * h], ALU.mult
                                                  ).then_inc(B["fac"], 1)
                        if s == end + 3:
                            dve.wait_ge(B["pv"], end)
                            dve.wait_ge(B["fac"], 3 * min(j + 1, 8) + 2 * max(j - 7, 0))
                            if kind == "nsa":
                                if j:
                                    dve.wait_ge(B["on"], j)
                                pr = sq[:, 0, :].rearrange("p (r b d) -> p r b d", r=2, b=NB)
                                dve.tensor_tensor(pr, ps[:, 4 + half, :].rearrange("p (r b d) -> p r b d", r=2, b=NB),
                                                  f.rearrange("p (b r d) -> p r b d", r=2, d=1)
                                                  .broadcast_to([P, 2, NB, HD]), ALU.mult).then_inc(B["prod"], 1)
                                dve.wait_ge(B["prod"], j + 1)
                                if t and half == 0:
                                    dve.wait_ge(B["ot"], t)
                                dve.tensor_tensor(sq[:, 1, :].rearrange("p (b h d) -> p b h d", h=2, d=HD)[:, :, half, :],
                                                  pr[:, 0, :, :], pr[:, 1, :, :], ALU.add).then_inc(B["on"], 1)
                            else:
                                dve.wait_ge(B["ot"], 4 + t)
                                for half in range(2):
                                    view = [v.rearrange("p (b h d) -> p b h d", h=2, d=HD)[:, :, half, :]
                                            for v in (sq[:, 1, :], ps[:, 4 + t % 2, :])]
                                    dve.tensor_tensor(view[0], view[1],
                                                      f[:, 4 * half:4 * half + 4].rearrange("p (b d) -> p b d", d=1)
                                                      .broadcast_to([P, NB, HD]), ALU.mult).then_inc(B["on"], 1)
                        if s == end + 5 and kind == "fox" and t >= 2:
                            dve.wait_ge(B["ohi"], 4 + t + 1)
                            dve.tensor_tensor(tile(hlo, t), ps[:, 4 + t % 2, :], tile(hhi, t).bitcast(f32),
                                              ALU.subtract).then_inc(B["olo"], 1)
                    for k, (row, t) in enumerate(STORED):
                        if SPLIT_AT[k] == s:
                            dve.wait_ge(B["ohi"], k + 1)
                            dve.tensor_tensor(tile(hlo, row), tile(zb, t), tile(hhi, row).bitcast(f32),
                                              ALU.subtract).then_inc(B["olo"], 1)
                    for u in finished_at(p, s):
                        beside(p, u)

            def pool_layer():
                p = "pool"
                clear_sum(p)
                dve.wait_ge(B["rcol"], 1)
                for g in range(NPOOL):
                    if g % 2:
                        dve.wait_ge(unit_done, FIRST[p] + g // 2 + 1)
                    else:
                        dve.wait_ge(B["z"], g // 2 + 1)
                    for b in range(2, NB):
                        dve.tensor_scalar(zt[:, b, g * GW:g * GW + GW],
                                          ps[:, POOL_BANK[g] + 1, (b - 2) * GW:(b - 2) * GW + GW],
                                          rcol[:, b:b + 1], None, ALU.mult).then_inc(B["zc_dve"], 1)
                    if g == 1:
                        split_lo(FIRST[p] + 2, 0, split_cols(FIRST[p] + 2))
                for m in range(KD):
                    residual(p, m, 0, MEAN_BANK[m])
                    if m == 0:
                        split_lo(FIRST[p] + 3, 0, split_cols(FIRST[p] + 3))

            for kind, what in flow:
                if kind == "norm":
                    if what == 0:
                        split_lo(0, 0, split_cols(0))
                    norm(what)
                elif what == "pool":
                    pool_layer()
                elif kind == "gemm":
                    gemm(what)
                elif kind == "post":
                    post(what)
                elif kind == "mix_a":
                    mix_a()
                elif kind == "mix_b":
                    mix_b()

        @block.tensor
        def _(pe_):
            def three(out, slot, j, hi, lo, start, stop):
                wh, wl = whi[slot][:, j * P:j * P + P], wlo[slot][:, j * P:j * P + P]
                pe_.matmul(out, wh, hi, start=start, stop=False)
                pe_.matmul(out, wh, lo, start=False, stop=False)
                return pe_.matmul(out, wl, hi, start=False, stop=stop)

            def operand_ready(p, k):
                if p in RSTD_OF:
                    pe_.wait_ge(h_lo, 8 * list(RSTD_OF).index(p) + k + 1)
                else:
                    pe_.wait_ge(A["olo"] if p == "out_a" else B["olo"], k + 1)

            def block_mm(p, u, j, bank, first, last):
                return three(ps[:, bank, :], (FIRST[p] + u) % SPL, j, tile(hhi, j), tile(hlo, j), first, last)

            def beside(p, start, end):
                for g in range(start, end):
                    u, j = ALONE[p] + g // 8, g % 8
                    if j == 0:
                        pe_.wait_ge(lo_done, FIRST[p] + u + 1)
                        if u > ALONE[p]:
                            pe_.wait_ge(evac[p], u)
                    last = block_mm(p, u, j, 6, j == 0, j == 7)
                    if j == 7:
                        last.then_inc(unit_done, 1)

            def gemm(p):
                n0 = FIRST[p]
                up = {"down_a": "up_a", "down_b0": "up_b0", "down_b1": "up_b1"}.get(p)

                def step(u, i):
                    n = n0 + u
                    slot = n % SPL
                    pe_.wait_ge(lo_done, n + 1 + 4 * i)
                    if up:
                        m, half = u // 2, u % 2
                        bank = m % 2
                        if u == 0:
                            pe_.wait_ge(hid["alo"], pair_base[up] + KF - 1)
                        if u == 1:
                            pe_.wait_ge(hid["alo"], pair_base[up] + KF)
                        if half == 0 and m >= 2:
                            pe_.wait_ge(evac[p], m - 1 + 2 * i)
                        for j in range(KH):
                            r = half * KH + j
                            last = three(ps[:, bank, :], slot, j, tile(ahi, r), tile(alo, r),
                                         half == 0 and j == 0, half == 1 and j == KH - 1)
                        last.then_inc(unit_done, 1)
                        return
                    if u >= 4:
                        pe_.wait_ge(evac[p], u - 3 + 4 * i)
                    e = RSTD_OF.get(p)
                    order = [4, 5, 6, 7, 0, 1, 2, 3] if p[:3] == "out" else range(KD)
                    for k, j in enumerate(order):
                        if u == 0:
                            operand_ready(p, k)
                        last = block_mm(p, u, j, u % 4, k == 0, k == KD - 1)
                        if u == 0 and e in BOUNDARY:
                            if k == KD - 1:
                                last.then_inc(unit_done, 1)
                            squares(e, k)
                    if u == 0 and e in BOUNDARY:
                        return
                    last.then_inc(unit_done, 1)
                    if u == 0 and e is not None:
                        statistics(e)

                units(pe_, 0, ALONE.get(p, COUNT[p]), peel_of(p), step)

            def statistics(e):
                if e in STREAMED:
                    pe_.wait_ge(sq_used, sq_base[STREAMED[e]] + KD)
                    pe_.matmul(ps[:, BANK_MS, :], ones[:, :], sumsq[:, :], start=True, stop=True).then_inc(ms_ready, 1)
                    return
                for m in range(KD):
                    squares(e, m)

            def squares(e, m):
                if e == 0 and m == 0:
                    pe_.wait_ge(const_0, 1)
                pe_.wait_ge(bsq_ready, 8 * BOUNDARY.index(e) + m + 1)
                last = pe_.matmul(ps[:, BANK_MS, :], ones[:, :], sq[:, m % 2, :], start=m == 0, stop=m == KD - 1)
                last.then_inc(ms_ready if m == KD - 1 else bsq_used, 1)

            def mix_a():
                p = "in_a"
                pe_.wait_ge(ld_vec, 48)
                beside(p, 0, NORMS_SWA[0])
                pe_.wait_ge(evac[p], ZSV + 1)
                for b in range(NB):
                    last = pe_.transpose(ps[:, 7, b * P:b * P + P], za[:, ZSV * S + b * P:ZSV * S + b * P + P],
                                         ident[:, :])
                last.then_inc(A["svT"], 1)
                pe_.wait_ge(const_a, 1)
                for j in range(5):
                    pe_.wait_ge(A["nsq"], j + 1)
                    if j >= 2:
                        pe_.wait_ge(A["nln"], j - 1)
                    pe_.matmul(ps[:, 4 + j % 2, :], blk64[:, :], sq[:, j % 2, :], start=True, stop=True
                               ).then_inc(A["nms"], 1)
                    beside(p, NORMS_SWA[j], NORMS_SWA[j + 1])
                pe_.wait_ge(A["nq"], 5)
                pe_.wait_ge(A["nln"], 5)
                pe_.wait_ge(A["svT_c"], 1)
                for s in range(len(ITEMS_A) + 6):
                    if s < len(ITEMS_A):
                        t, half, b = ITEMS_A[s]
                        rows = slice(HD * half, HD * half + HD)
                        k0 = max(b - 1, 0) * P
                        w = P * min(b + 1, 2)
                        if s >= 2:
                            pe_.wait_ge(A["m"], s - 1)
                        q = (ZSQ + t) * S + b * P
                        pe_.matmul(ps[:, s % 2, 0:w], za[rows, q:q + P], za[rows, ZSK * S + k0:ZSK * S + k0 + w],
                                   start=True, stop=True).then_inc(A["s"], 1)
                    if 0 <= s - 2 < len(ITEMS_A):
                        g = s - 2
                        pe_.wait_ge(A["p"], g + 1)
                        if g >= 2:
                            pe_.wait_ge(A["tc"], g - 1)
                        for k in range(min(ITEMS_A[g][2] + 1, 2)):
                            last = pe_.transpose(ps[:, 2 + g % 2, k * P:k * P + P], pA[:, g % 3, k * P:k * P + P],
                                                 ident[:, :])
                        last.then_inc(A["t"], 1)
                    if 0 <= s - 3 < len(ITEMS_A):
                        g = s - 3
                        t, half, b = ITEMS_A[g]
                        nk = min(b + 1, 2)
                        pe_.wait_ge(A["tc"], g + 1)
                        if g % 8 == 0 and t >= 2:
                            pe_.wait_ge(A["oc"], t - 1)
                        o = b * P + half * HD
                        for k in range(nk):
                            v = (b + 1 - nk + k) * P + HD * half
                            last = pe_.matmul(ps[:, 4 + t % 2, o:o + HD], pTA[:, g % 2, k * P:k * P + P],
                                              svT[:, v:v + HD], start=k == 0, stop=k == nk - 1)
                        last.then_inc(A["pv"], 1)
                    if s % 8 == 4 and s > 8:
                        t = s // 8 - 1
                        pe_.wait_ge(A["swon"], 2 * t + 2)
                        for b in range(NB):
                            last = pe_.transpose(ps[:, 4 + t % 2, b * P:b * P + P], onA[:, b * P:b * P + P], ident[:, :])
                        last.then_inc(A["ot"], 1)
                    if s in GLA_LOGIT:
                        t = GLA_LOGIT.index(s)
                        pe_.wait_ge(evac[p], ZLR + 1)
                        if t:
                            pe_.wait_ge(A["logit_b"], 1)
                        pe_.matmul(ps[:, 7, :], wal[:, t * P:t * P + P], za[0:16, ZLR * S:ZLR * S + S],
                                   start=True, stop=True).then_inc(A["logit"], 1)
                    if s in GLA_KDT:
                        t = GLA_KDT.index(s)
                        if t == 0:
                            pe_.wait_ge(A["kd"], 1)
                            pe_.wait_ge(A["logit_b"], 2)
                        else:
                            pe_.wait_ge(A["kdT_c"], 1)
                        for b in range(NB):
                            c = t * S + b * P
                            last = pe_.transpose(ps[:, 7, b * P:b * P + P], kd[:, c:c + P], ident[:, :])
                        last.then_inc(A["kdT"], 1)
                    if s in GLA_SCORE:
                        h = GLA_SCORE.index(s)
                        t, rows = h // 2, slice(HD * (h % 2), HD * (h % 2) + HD)
                        if h == 0:
                            pe_.wait_ge(A["kdT_c"], 2)
                            pe_.wait_ge(A["ke"], 1)
                            pe_.wait_ge(A["qe"], 1)
                        else:
                            pe_.wait_ge(A["masked"], h)
                        for b in range(NB):
                            c = t * S + b * P
                            last = pe_.matmul(ps[:, 7, b * P:b * P + P], za[rows, ZGK * S + c:ZGK * S + c + P],
                                              za[rows, ZGQ * S + c:ZGQ * S + c + P], start=True, stop=True)
                        last.then_inc(A["score"], 1)
                    if s in GLA_GVT:
                        h = GLA_GVT.index(s)
                        pe_.wait_ge(evac[p], ZGV + h + 1)
                        if h == 0:
                            pe_.wait_ge(A["masked"], 4)
                        else:
                            pe_.wait_ge(A["gvT_c"], h)
                        for b in range(NB):
                            c = (ZGV + h) * S + b * P
                            last = pe_.transpose(ps[:, 7, b * P:b * P + P], za[:, c:c + P], ident[:, :])
                        last.then_inc(A["gvT"], 1)
                    beside(p, blocks_by(p, s - 1), blocks_by(p, s))
                pe_.wait_ge(A["m"], len(ITEMS_A))
                pe_.wait_ge(A["tc"], len(ITEMS_A))
                pe_.wait_ge(A["gvT_c"], 4)
                for t in range(2):
                    for n in range(NCH - 1):
                        rows = slice(CHUNK * (n % 2), CHUNK * (n % 2) + CHUNK)
                        for half in range(2):
                            h = 2 * t + half
                            c = t * S + (n // 2) * P + half * HD
                            v = h * S + (n // 2) * P
                            last = pe_.matmul(ps[HD * half:HD * half + HD, 2 * t + n % 2, (n // 2) * P:(n // 2) * P + P],
                                              kdT[rows, c:c + HD], gvT[rows, v:v + P], start=True, stop=True)
                    last.then_inc(A["cs"], 1)
                beside(p, AFTER_SWA[0], AFTER_SWA[1])
                pe_.wait_ge(A["st"], 1 + 2 * (NCH - 1))
                pe_.wait_ge(A["oc"], 4)
                for h in range(4):
                    t, rows = h // 2, slice(HD * (h % 2), HD * (h % 2) + HD)
                    for b in range(NB):
                        out = ps[:, GLA_BANK[h], :]
                        pe_.matmul(out[:, b * P:b * P + P], tile(gvT, h)[:, b * P:b * P + P],
                                   tile(aT, h)[:, b * P:b * P + P], start=True, stop=False)
                        for n in (2 * b, 2 * b + 1):
                            c = ZGQ * S + t * S + n * CHUNK
                            last = pe_.matmul(out[:, n * CHUNK:n * CHUNK + CHUNK], state[rows, t, n, :],
                                              za[rows, c:c + CHUNK], start=False, stop=n % 2 == 1)
                    last.then_inc(A["o"], 1)
                beside(p, AFTER_SWA[1], AFTER_SWA[2])
                for h in range(4):
                    pe_.wait_ge(A["osq"], h + 1)
                    if h >= 2:
                        pe_.wait_ge(A["oln"], h - 1)
                    pe_.matmul(ps[:, h % 2, :], ones[:, :], sq[:, h % 2, :], start=True, stop=True
                               ).then_inc(A["oms"], 1)
                    if h == 0:
                        beside(p, AFTER_SWA[2], AFTER_SWA[3])

            def mix_b():
                p = "in_b"

                def transposed(t, bank):
                    for b in range(NB):
                        c = t * S + b * P
                        last = pe_.transpose(ps[:, bank, b * P:b * P + P], zb[:, c:c + P], ident[:, :])
                    last.then_inc(B["vt"], 1)

                pe_.wait_ge(evac[p], ALONE[p])
                for j in range(2):
                    transposed(ZV[j], j)
                for b in range(NB):
                    last = pe_.transpose(ps[:, 2, b * HD:b * HD + HD], zb[0:HD, b * P:b * P + P], ident[0:HD, 0:HD])
                last.then_inc(B["gt"], 1)
                beside(p, 0, 8)
                pe_.wait_ge(B["pe"], 4)
                for kv in range(2):
                    for l in range(32):
                        buf = tile(zb, ZKC + kv) if l < 16 else pTB[:, kv, :]
                        by = buf.rearrange("p (n l) -> p l n", l=16)
                        for g in range(2):
                            rows = slice(HD * g, HD * g + HD)
                            last = pe_.matmul(ps[rows, 3, 32 * kv:32 * kv + NCMP], cw1[rows, kv, l * HD:l * HD + HD],
                                              by[rows, l % 16, l // 16:l // 16 + NCMP], start=l == 0, stop=l == 31)
                    last.then_inc(B["hid"], 1)
                beside(p, 8, 16)
                pe_.wait_ge(B["vt_c"], 2)
                pe_.wait_ge(B["gx"], 1)
                pe_.wait_ge(B["gelu"], 2)
                for s in range(N_ITEMS_B + 6):
                    if s < N_ITEMS_B:
                        kind, t, half, b = ITEMS_B[s]
                        rows = slice(HD * half, HD * half + HD)
                        q, k = {"slc": (ZQ + t, ZKS), "win": (ZQ + t, ZKW), "fox": (ZFQ + t, ZFK + t)}[kind]
                        w = P * (b + 1)
                        if s >= 2:
                            pe_.wait_ge(B["m"], s - 1)
                        if kind == "fox":
                            pe_.wait_ge(evac[p], ZFK + t + 1)
                        last = pe_.matmul(ps[:, s % 2, 0:w], zb[rows, q * S + b * P:q * S + b * P + P],
                                          zb[rows, k * S:k * S + w], start=True, stop=kind != "fox")
                        if kind == "fox":
                            last = pe_.matmul(ps[:, s % 2, b * P:w], identb[:, :], triang[:, :], start=False, stop=True)
                        last.then_inc(B["s"], 1)
                    if 0 <= s - 2 < N_ITEMS_B:
                        g = s - 2
                        pe_.wait_ge(B["p"], g + 1)
                        if g >= 2:
                            pe_.wait_ge(B["tc"], g - 1)
                        for k in range(ITEMS_B[g][3] + 1):
                            last = pe_.transpose(ps[:, 2 + g % 2, k * P:k * P + P], pB[:, g % 3, k * P:k * P + P],
                                                 ident[:, :])
                        last.then_inc(B["t"], 1)
                    if 0 <= s - 3 < N_ITEMS_B:
                        g = s - 3
                        kind, t, half, b = ITEMS_B[g]
                        if kind == "fox":
                            v, bank, o = 2 + t, 4 + t % 2, b * P + half * HD
                        else:
                            v, bank, o = (0 if kind == "slc" else 1), 4 + half, b * HD + (0 if kind == "slc" else 4 * HD)
                        v = v * S + HD * half
                        pe_.wait_ge(B["tc"], g + 1)
                        j = g // 8
                        if g % 8 == 0 and j >= 2:
                            if kind == "fox" and t >= 2:
                                pe_.wait_ge(B["oc"], 4 + t - 1)
                            elif (kind == "fox" and t == 1) or (kind != "fox" and half == 1):
                                pe_.wait_ge(B["oc"], j // 2)
                            else:
                                pe_.wait_ge(B["on"], j - 1)
                        if kind == "fox" and g % 8 == 0:
                            pe_.wait_ge(B["vt_c"], 3 + t)
                        for k in range(b + 1):
                            last = pe_.matmul(ps[:, bank, o:o + HD], pTB[:, g % 2, k * P:k * P + P],
                                              vT[:, v + k * P:v + k * P + HD], start=k == 0, stop=k == b)
                        last.then_inc(B["pv"], 1)
                    for j, (kind, t, half) in enumerate(GROUPS_B):
                        if s != 8 * (j + 1) + 4:
                            continue
                        if kind == "nsa" and half == 1:
                            pe_.wait_ge(B["ct_c"], 2 * t + 2)
                            pe_.wait_ge(B["on"], j + 1)
                            for b in range(NB):
                                pe_.matmul(ps[:, 5, b * P:b * P + P], sq[:, 1, b * P:b * P + P], ident[:, :],
                                           start=True, stop=False)
                                for half in range(2):
                                    c = (t + 4 * half) * S + b * P
                                    last = pe_.matmul(ps[HD * half:HD * half + HD, 5, b * P:b * P + P],
                                                      vcmp[:, HD * half:HD * half + HD], pTc[:, c:c + P],
                                                      start=False, stop=True)
                            last.then_inc(B["ot"], 1)
                        if kind == "fox":
                            pe_.wait_ge(B["on"], 8 + 2 * t + 2)
                            for b in range(NB):
                                last = pe_.transpose(ps[:, 4 + t % 2, b * P:b * P + P], sq[:, 1, b * P:b * P + P],
                                                     ident[:, :])
                            last.then_inc(B["ot"], 1)
                    if s == NSA_KC:
                        for g in range(2):
                            rows = slice(HD * g, HD * g + HD)
                            last = pe_.matmul(ps[rows, 7, 0:NCMP], cw2[rows, 0:HD], glu[rows, 0:NCMP], start=True, stop=True)
                        last.then_inc(B["kc"], 1)
                    if s in NSA_VC:
                        g = NSA_VC.index(s)
                        rows = slice(HD * g, HD * g + HD)
                        pe_.wait_ge(B["kc_c"], 1 + g)
                        pe_.matmul(ps[0:NCMP, 7, 0:HD], glu[rows, 32:32 + NCMP], cw2[rows, HD:2 * HD],
                                   start=True, stop=True).then_inc(B["kc"], 1)
                    if s in NSA_CS:
                        g = NSA_CS.index(s)
                        rows = slice(HD * g, HD * g + HD)
                        if g == 0:
                            pe_.wait_ge(B["kc_c"], 3)
                        else:
                            pe_.wait_ge(B["cb"], 4)
                        for k in range(4):
                            for b in range(NB):
                                q = (ZQ + k) * S + b * P
                                c = k * P + b * 32
                                last = pe_.matmul(ps[:, 7, c:c + 32], zb[rows, q:q + P], kcmp[rows, :],
                                                  start=True, stop=True)
                        last.then_inc(B["cs"], 1)
                    if s in FOX_V:
                        j = FOX_V.index(s)
                        pe_.wait_ge(evac[p], ZFV + j + 1)
                        if j == 0:
                            pe_.wait_ge(B["cb"], 8)
                        else:
                            pe_.wait_ge(B["vt_c"], 2 + j)
                        transposed(ZFV + j, 7)
                    if s in NSA_CT:
                        k = NSA_CT.index(s)
                        h = CT_HEADS[k]
                        if k == 0:
                            pe_.wait_ge(B["vt_c"], 6)
                            pe_.wait_ge(B["cp"], 1)
                        else:
                            pe_.wait_ge(B["ct_c"], k)
                        for b in range(NB):
                            c = h * P + b * 32
                            last = pe_.transpose(ps[0:32, 7, b * P:b * P + P], pc[:, c:c + 32], ident[:, :])
                        last.then_inc(B["ct"], 1)
                    if s in FOX_NC:
                        h = FOX_NC.index(s)
                        if h == 0:
                            pe_.wait_ge(B["fc"], 1)
                            pe_.wait_ge(B["ct_c"], 8)
                        else:
                            pe_.wait_ge(B["nc_c"], h)
                        pe_.matmul(ps[:, 7, :], ident[0:8, h:h + 1].broadcast_to([8, P]), sq[0:8, 2, :],
                                   start=True, stop=True).then_inc(B["nc"], 1)
                    beside(p, blocks_by(p, s - 1), blocks_by(p, s))

            def pool_layer():
                p, e = "pool", RSTD_OF["pool"]

                def linear(g, blocks=range(NB)):
                    n = FIRST[p] + g // 2
                    pe_.wait_ge(lo_done, n + 1)
                    for b in blocks:
                        out = ps[:, POOL_BANK[g] + b // 2, (b % 2) * GW:(b % 2) * GW + GW]
                        for k in range(2):
                            m, c = 2 * g + k, (g % 2) * 2 * GW + k * GW
                            if b == 0:
                                operand_ready(p, m)
                            hi, lo = [h[:, m * S + b * P:m * S + b * P + P] for h in (hhi, hlo)]
                            pe_.matmul(out, hi, whi[n % SPL][:, c:c + GW], start=k == 0, stop=False)
                            pe_.matmul(out, lo, whi[n % SPL][:, c:c + GW], start=False, stop=False)
                            last = pe_.matmul(out, hi, wlo[n % SPL][:, c:c + GW], start=False, stop=k == 1)
                    if NB - 1 in blocks:
                        last.then_inc(unit_done if g % 2 else B["z"], 1)

                for g in range(4):
                    for m in (2 * g, 2 * g + 1):
                        squares(e, m)
                    if g < 2:
                        linear(g)
                linear(2, [0, 1])
                pe_.wait_ge(rstd_ready, e + 1)
                for b in range(NB):
                    last = pe_.matmul(ps[:, 7, b:b + 1], rstd[0:1, b * P:b * P + P], ident[0:1, 0:1],
                                      start=True, stop=True)
                last.then_inc(B["rt"], 1)
                linear(2, [2, 3])
                pe_.wait_ge(B["zc_act"], 2)
                pe_.wait_ge(B["zc_dve"], 2)
                linear(3)
                pe_.wait_ge(B["band"], 1)
                for m in range(KD):
                    g = m // 2
                    pe_.wait_ge(B["zc_act"], 2 * g + 2)
                    pe_.wait_ge(B["zc_dve"], 2 * g + 2)
                    for b in range(NB):
                        c = b * P
                        last = pe_.matmul(ps[:, MEAN_BANK[m], c:c + P], zt[:, b, m * P:m * P + P],
                                          band[:, 2 * g + (b == 0), :], start=True, stop=b == 0)
                        if b:
                            last = pe_.matmul(ps[:, MEAN_BANK[m], c:c + MAXW], zt[:, b - 1, m * P:m * P + P],
                                              spill[:, g, :], start=False, stop=True)
                    last.then_inc(B["mean"], 1)

            for kind, what in flow:
                if kind == "post":
                    statistics(what)
                elif what == "pool":
                    pool_layer()
                elif kind == "gemm":
                    gemm(what)
                elif kind == "mix_a":
                    mix_a()
                elif kind == "mix_b":
                    mix_b()


def _tiles(w, n):
    return np.ascontiguousarray(w.reshape(KD, P, n, P).transpose(2, 1, 0, 3).reshape(n, P, KD * P))


def _pairs(w, axis):
    shape = w.shape
    w = np.moveaxis(w, axis, 0)
    w = w.reshape(2, 4, HD, -1).transpose(1, 0, 2, 3).reshape(w.shape)
    return np.moveaxis(w, 0, axis).reshape(shape)


def _down(w):
    return np.ascontiguousarray(w.reshape(2, KH, P, KD, P).transpose(3, 0, 2, 1, 4).reshape(16, P, KH * P))


def _up(a, b):
    return np.ascontiguousarray(np.stack([_tiles(a, KF), _tiles(b, KF)], 1).reshape(2 * KF, P, KD * P))


def _cols(v):
    return v.reshape(-1, P).T


def arrays_of(i):
    f = np.float32
    w = i["w_in"][0]
    c = np.cumsum([0, 256, 256, 512, 512, 16, 512, 128, 128])
    gq, gk, gv, gr, glr, sq, sk, sv = [w[:, c[k]:c[k + 1]] for k in range(8)]
    lr = np.zeros((D, P), f)
    lr[:, 0:16] = glr
    in_a = np.concatenate([_pairs(sq, 1), sk, sv, lr, gk, gq, gv, gr], 1)
    wo = i["w_out"][0]
    out_a = np.concatenate([wo[0:512], _pairs(wo[512:1024], 0)], 0)
    w = i["attn_w_in_2"][0]
    c = np.cumsum([0, 512, 512, 512, 8, 512, 128, 128, 128, 128, 128, 128, 24])
    fq, fk, fv, ff, nq, kc, vc, ks, vs, kw, vw, ng = [w[:, c[k]:c[k + 1]] for k in range(12)]
    gt = np.zeros((D, P), f)
    gt[:, 0:8] = ff
    gt[:, 32:56] = ng
    in_b = np.concatenate([gt, _pairs(nq, 1), kc, vc, ks, vs, kw, vw, fv, fq, fk], 1)
    wo = i["attn_w_out_2"][0]
    out_b = np.concatenate([wo[0:512], _pairs(wo[512:1024], 0)], 0)
    pw = i["pool_w_2"][0].reshape(2, 2, 2, P, 2 * P).transpose(0, 3, 1, 2, 4)
    weights = {
        "in_a": _tiles(in_a, 19), "out_a": _tiles(out_a, 8),
        "up_a": _up(i["w_up"][0][:, 0:FF], i["w_up"][0][:, FF:]), "down_a": _down(i["w_down"][0]),
        "in_b": _tiles(in_b, 23), "out_b": _tiles(out_b, 8),
        "up_b0": _up(i["ffn_w_gate_2"][0], i["ffn_w_up_2"][0]), "down_b0": _down(i["ffn_w_down_2"][0]),
        "pool": np.ascontiguousarray(pw.reshape(2, P, 8 * P)),
        "up_b1": _up(i["ffn_w_gate_2"][1], i["ffn_w_up_2"][1]), "down_b1": _down(i["ffn_w_down_2"][1]),
    }
    v = {"mix_norm": i["mix_norm"], "ffn_norm": i["ffn_norm"], "pool_scale": i["pool_scale_2"],
         "b_alpha": i["b_alpha"], "gla_norm": i["gla_norm"],
         "q_norm": np.concatenate([i["q_norm"][0], i["q_norm"][0]]),
         "k_norm": np.concatenate([i["k_norm"][0], i["k_norm"][0]]),
         "b_f": np.concatenate([i["fox_b_f_2"][0], np.zeros(P - 8, f)])}
    for layer in range(2):
        for k in range(4):
            v[f"g{layer}{k}"] = i["norm_g_2"][layer, k]
    vecs = np.concatenate([_cols(v[name]) for name in VEC], 1)
    conv = np.concatenate([_cols(i["conv_w"][0, k]) for k in range(3)] + [_cols(i["conv_b"][0])], 1)
    x = i["x"][0].T.reshape(KD, P, S).transpose(1, 0, 2).reshape(P, KD * S)
    out = {"xT": x, "vecs": vecs, "conv": conv, "sinks": np.broadcast_to(i["sinks"][0], (P, NHEADS)),
           "w_alpha2": i["w_alpha2"][0],
           "pe": i["nsa_cmp_pe_2"][0].transpose(0, 2, 1),
           "cmp_w1": i["nsa_cmp_w1_2"][0].reshape(2, 32, HD, HD).transpose(0, 2, 1, 3).reshape(2, HD, 32 * HD),
           "cmp_w2": i["nsa_cmp_w2_2"][0]}
    out = {k: np.ascontiguousarray(a) for k, a in out.items()}
    for p in ORDER:
        out["w_" + p] = weights[p]
    return out


def program(nc, arrays, flow=FLOW):
    f32 = mybir.dt.float32
    args = {k: nc.dram_tensor(k, a.shape, f32, kind="ExternalInput").ap() for k, a in arrays.items()}
    y = nc.dram_tensor("yT", (P, KD * S), f32, kind="ExternalOutput").ap()
    weights = {p: args.pop("w_" + p) for p in ORDER}
    build(nc, weights=weights, yT=y, flow=flow, **args)


def kernel(**inputs):
    import concourse.bacc as _bacc
    from concourse.bass_utils import run_bass_kernel_spmd as _run

    arrays = arrays_of({k: np.asarray(a) for k, a in inputs.items()})
    nc = _bacc.Bacc("TRN2", target_bir_lowering=False, num_devices=1)
    program(nc, arrays)
    r = _run(nc, [arrays], core_ids=[0])
    y = np.asarray(r.results[0]["yT"])
    return np.ascontiguousarray(y.reshape(P, KD, S).transpose(2, 1, 0).reshape(1, S, D))
```
